# Optimizing a Trainium2 kernel written in Bass

```python
import math
import jax, jax.numpy as jnp
from jax import lax
import numpy as np

D_MODEL = 1024
BATCH = 1
SEQ = 256
DEPTH = 1
DEC_BATCH = 8
DEC_SEQ = 8
PAST_LEN = 2048
PAGE_SIZE = 128

SSD_INNER = 2 * D_MODEL
SSD_HEAD_DIM = 64
SSD_HEADS = SSD_INNER // SSD_HEAD_DIM
SSD_STATE = 128
SSD_GROUPS = 4
SSD_HPG = SSD_HEADS // SSD_GROUPS
CONV_K = 4
CONV_DIM = SSD_INNER + 2 * SSD_GROUPS * SSD_STATE
SSD_CHUNK = 128
GLA_HEADS = 4
GLA_KEY_DIM = D_MODEL // 2
GLA_VAL_DIM = D_MODEL
GLA_DK = GLA_KEY_DIM // GLA_HEADS
GLA_DV = GLA_VAL_DIM // GLA_HEADS
GLA_GATE_RANK = 16
GLA_TAU = 16.0
GLA_CHUNK = 64
N_EXPERTS = 16
N_EXPERT_GROUPS = 4
EXPERTS_PER_GROUP = N_EXPERTS // N_EXPERT_GROUPS
TOP_K = 2
EXPERT_FF = D_MODEL // 2
EPS = 1e-6
IN_SIZES = (SSD_INNER, CONV_DIM, SSD_HEADS, GLA_KEY_DIM, GLA_KEY_DIM, GLA_VAL_DIM, GLA_VAL_DIM,
            GLA_GATE_RANK, D_MODEL, D_MODEL)
IN_DIM = sum(IN_SIZES)
IN_OFFSETS = tuple(int(o) for o in np.cumsum(IN_SIZES)[:-1])

kernel_name = "hybrid_ssd_gla_moe_adaln_step"

def rms_norm(x, w):
    xf = x.astype(jnp.float32)
    y = xf * lax.rsqrt(jnp.mean(xf * xf, axis=-1, keepdims=True) + EPS)
    return (y * w.astype(jnp.float32)).astype(x.dtype)

def chunk_major(a, chunk):
    bt, s = a.shape[:2]
    nc = -(-s // chunk)
    pad = nc * chunk - s
    a = jnp.pad(a, [(0, 0), (0, pad)] + [(0, 0)] * (a.ndim - 2))
    return a.reshape((bt, nc, chunk) + a.shape[2:]).swapaxes(0, 1)

def unchunk(a, s):
    nc, bt, chunk = a.shape[:3]
    return a.swapaxes(0, 1).reshape((bt, nc * chunk) + a.shape[3:])[:, :s]

def causal_conv(u, buf, w, b):
    s = u.shape[1]
    full = jnp.concatenate([buf.astype(u.dtype), u], axis=1)
    out = b + full[:, 0:s] * w[0]
    for i in range(1, CONV_K):
        out = out + full[:, i:i + s] * w[i]
    return out, full[:, -(CONV_K - 1):]

def ssd_chunked(x, dt, a, bm, cm, state0):
    s = x.shape[1]
    chunk = min(SSD_CHUNK, s)
    f32 = jnp.float32
    mask = jnp.tril(jnp.ones((chunk, chunk), dtype=bool))
    xs = (chunk_major(x.astype(f32), chunk), chunk_major(dt.astype(f32), chunk),
          chunk_major(bm.astype(f32), chunk), chunk_major(cm.astype(f32), chunk))

    def body(state, inp):
        xc, dtc, bc, cc = inp
        cs = jnp.cumsum(dtc * a, axis=1)
        seg = cs[:, :, None, :] - cs[:, None, :, :]
        decay = jnp.exp(jnp.where(mask[None, :, :, None], seg, -jnp.inf))
        cb = jnp.repeat(jnp.einsum('bign,bjgn->bijg', cc, bc), SSD_HPG, axis=-1)
        xdt = xc * dtc[..., None]
        y = jnp.einsum('bijh,bjhp->bihp', cb * decay, xdt)
        ch = jnp.repeat(cc, SSD_HPG, axis=2)
        y = y + jnp.einsum('bihn,bhpn->bihp', ch, state) * jnp.exp(cs)[..., None]
        bh = jnp.repeat(bc, SSD_HPG, axis=2) * jnp.exp(cs[:, -1:, :] - cs)[..., None]
        state = state * jnp.exp(cs[:, -1, :])[:, :, None, None] + jnp.einsum('bjhn,bjhp->bhpn', bh, xdt)
        return state, y

    state, ys = lax.scan(body, state0.astype(f32), xs)
    return unchunk(ys, s), state

def gla_chunked(q, k, v, lg, state0):
    s = q.shape[1]
    chunk = min(GLA_CHUNK, s)
    f32 = jnp.float32
    mask = jnp.tril(jnp.ones((chunk, chunk), dtype=bool))
    xs = (chunk_major(q.astype(f32), chunk), chunk_major(k.astype(f32), chunk),
          chunk_major(v.astype(f32), chunk), chunk_major(lg.astype(f32), chunk))

    def body(state, inp):
        qc, kc, vc, gc = inp
        g = jnp.cumsum(gc, axis=1)
        seg = g[:, :, None] - g[:, None, :]
        decay = jnp.exp(jnp.where(mask[None, :, :, None, None], seg, -jnp.inf))
        att = jnp.einsum('bihk,bjhk,bijhk->bijh', qc, kc, decay)
        o = jnp.einsum('bijh,bjhv->bihv', att, vc)
        o = o + jnp.einsum('bihk,bhkv->bihv', qc * jnp.exp(g), state)
        kd = kc * jnp.exp(g[:, -1:] - g)
        state = state * jnp.exp(g[:, -1])[..., None] + jnp.einsum('bjhk,bjhv->bhkv', kd, vc)
        return state, o

    state, os_ = lax.scan(body, state0.astype(f32), xs)
    return unchunk(os_, s), state

def route(h, w_router, router_bias):
    t = h.shape[0]
    scores = jax.nn.sigmoid(h.astype(jnp.float32) @ w_router.astype(jnp.float32))
    biased = scores + router_bias.astype(jnp.float32)
    grp = biased.reshape(t, N_EXPERT_GROUPS, EXPERTS_PER_GROUP)
    grp_score = lax.top_k(grp, TOP_K)[0].sum(-1)
    best = jnp.argmax(grp_score, axis=-1)
    gmask = jnp.repeat(jnp.arange(N_EXPERT_GROUPS)[None, :] == best[:, None], EXPERTS_PER_GROUP, axis=-1)
    _, idx = lax.top_k(jnp.where(gmask, biased, -jnp.inf), TOP_K)
    w = jnp.take_along_axis(scores, idx, axis=-1)
    w = w / jnp.sum(w, axis=-1, keepdims=True)
    return jnp.sum(jax.nn.one_hot(idx, N_EXPERTS, dtype=jnp.float32) * w[..., None], axis=1)

def moe_ffn(h, comb, wg, wu, wd):
    out = jnp.zeros_like(h)
    for e in range(N_EXPERTS):
        ye = (jax.nn.silu(h @ wg[e]) * (h @ wu[e])) @ wd[e]
        out = out + comb[:, e:e + 1].astype(h.dtype) * ye
    return out

def layer_fwd(x, c, conv_buf, ssm_state, gla_state, p, w_router, router_bias):
    bt, s, _ = x.shape
    f32 = jnp.float32
    mod = (jax.nn.silu(c) @ p['w_ada'] + p['b_ada'])[:, None, :]
    sh1, sc1, g1, sh2, sc2, g2 = jnp.split(mod, 6, axis=-1)
    h = rms_norm(x, p['norm1_w']) * (1 + sc1) + sh1
    z, xbc, dt, q, k, v, r, glr, ga, gb = jnp.split(h @ p['w_in'], IN_OFFSETS, axis=-1)
    xbc, conv_new = causal_conv(xbc, conv_buf, p['conv_w'], p['conv_b'])
    xbc = jax.nn.silu(xbc)
    xs, bm, cm = jnp.split(xbc, [SSD_INNER, SSD_INNER + SSD_GROUPS * SSD_STATE], axis=-1)
    xs = xs.reshape(bt, s, SSD_HEADS, SSD_HEAD_DIM)
    bm = bm.reshape(bt, s, SSD_GROUPS, SSD_STATE)
    cm = cm.reshape(bt, s, SSD_GROUPS, SSD_STATE)
    dtp = jax.nn.softplus(dt.astype(f32) + p['dt_bias'].astype(f32))
    a = -jnp.exp(p['a_log'].astype(f32))
    y_ssd, ssm_new = ssd_chunked(xs, dtp, a, bm, cm, ssm_state)
    y_ssd = y_ssd + p['d_skip'].astype(f32)[:, None] * xs.astype(f32)
    y_ssd = y_ssd.reshape(bt, s, SSD_INNER).astype(x.dtype) * jax.nn.silu(z)
    y_ssd = rms_norm(y_ssd.reshape(bt, s, SSD_GROUPS, SSD_INNER // SSD_GROUPS),
                     p['ssd_norm_w'].reshape(SSD_GROUPS, SSD_INNER // SSD_GROUPS))
    branch_a = y_ssd.reshape(bt, s, SSD_INNER) @ p['w_ssd_br']
    q = q.reshape(bt, s, GLA_HEADS, GLA_DK) * (GLA_DK ** -0.5)
    k = k.reshape(bt, s, GLA_HEADS, GLA_DK)
    v = v.reshape(bt, s, GLA_HEADS, GLA_DV)
    lg = jax.nn.log_sigmoid((glr @ p['gla_gate_up'] + p['gla_gate_b']).astype(f32)) / GLA_TAU
    lg = lg.reshape(bt, s, GLA_HEADS, GLA_DK)
    o, gla_new = gla_chunked(q, k, v, lg, gla_state)
    o = rms_norm(o.astype(x.dtype), p['gla_norm_w'])
    o = o.reshape(bt, s, GLA_VAL_DIM) * jax.nn.silu(r)
    branch_b = o @ p['w_gla_br']
    gate_a = jax.nn.sigmoid(ga + p['merge_b'][:D_MODEL])
    gate_b = jax.nn.sigmoid(gb + p['merge_b'][D_MODEL:])
    mixed = (gate_a * branch_a + gate_b * branch_b) @ p['w_out']
    x = x + g1 * mixed
    h2 = (rms_norm(x, p['norm2_w']) * (1 + sc2) + sh2).reshape(bt * s, D_MODEL)
    comb = route(h2, w_router, router_bias)
    y_moe = moe_ffn(h2, comb, p['w_exp_gate'], p['w_exp_up'], p['w_exp_down']).reshape(bt, s, D_MODEL)
    x = x + g2 * y_moe
    return x, conv_new, ssm_new.astype(x.dtype), gla_new.astype(x.dtype)

def setup_inputs(seed: int = 0) -> dict:
    key = jax.random.key(seed)
    ks = iter(jax.random.split(key, 40))
    nrm = lambda shape, scale: jax.random.normal(next(ks), shape, jnp.float32) * scale
    dt0 = jnp.exp(jax.random.uniform(next(ks), (DEPTH, SSD_HEADS), jnp.float32)
                  * (math.log(0.1) - math.log(0.001)) + math.log(0.001))
    return {
        "x_prompt": nrm((BATCH, SEQ, D_MODEL), 1.0),
        "x_sample": nrm((DEC_BATCH, DEC_SEQ, D_MODEL), 1.0),
        "c_prompt": nrm((BATCH, D_MODEL), 1.0),
        "c_sample": nrm((DEC_BATCH, D_MODEL), 1.0),
        "state_conv": nrm((DEPTH, DEC_BATCH, CONV_K - 1, CONV_DIM), 1.0),
        "state_ssm": nrm((DEPTH, DEC_BATCH, SSD_HEADS, SSD_HEAD_DIM, SSD_STATE), 0.1),
        "state_gla": nrm((DEPTH, DEC_BATCH, GLA_HEADS, GLA_DK, GLA_DV), 0.1),
        "w_ada": nrm((DEPTH, D_MODEL, 6 * D_MODEL), 0.3 * D_MODEL ** -0.5),
        "b_ada": nrm((DEPTH, 6 * D_MODEL), 0.02),
        "norm1_w": 1.0 + nrm((DEPTH, D_MODEL), 0.02),
        "w_in": nrm((DEPTH, D_MODEL, IN_DIM), D_MODEL ** -0.5),
        "conv_w": nrm((DEPTH, CONV_K, CONV_DIM), 0.5),
        "conv_b": nrm((DEPTH, CONV_DIM), 0.02),
        "dt_bias": dt0 + jnp.log(-jnp.expm1(-dt0)),
        "a_log": jnp.log(jax.random.uniform(next(ks), (DEPTH, SSD_HEADS), jnp.float32, 1.0, 16.0)),
        "d_skip": 1.0 + nrm((DEPTH, SSD_HEADS), 0.1),
        "ssd_norm_w": 1.0 + nrm((DEPTH, SSD_INNER), 0.02),
        "w_ssd_br": nrm((DEPTH, SSD_INNER, D_MODEL), SSD_INNER ** -0.5),
        "gla_gate_up": nrm((DEPTH, GLA_GATE_RANK, GLA_KEY_DIM), GLA_GATE_RANK ** -0.5),
        "gla_gate_b": nrm((DEPTH, GLA_KEY_DIM), 0.1),
        "gla_norm_w": 1.0 + nrm((DEPTH, GLA_DV), 0.02),
        "w_gla_br": nrm((DEPTH, GLA_VAL_DIM, D_MODEL), GLA_VAL_DIM ** -0.5),
        "merge_b": nrm((DEPTH, 2 * D_MODEL), 0.02),
        "w_out": nrm((DEPTH, D_MODEL, D_MODEL), D_MODEL ** -0.5),
        "norm2_w": 1.0 + nrm((DEPTH, D_MODEL), 0.02),
        "w_router": nrm((D_MODEL, N_EXPERTS), D_MODEL ** -0.5),
        "router_bias": nrm((N_EXPERTS,), 0.01),
        "w_exp_gate": nrm((DEPTH, N_EXPERTS, D_MODEL, EXPERT_FF), D_MODEL ** -0.5),
        "w_exp_up": nrm((DEPTH, N_EXPERTS, D_MODEL, EXPERT_FF), D_MODEL ** -0.5),
        "w_exp_down": nrm((DEPTH, N_EXPERTS, EXPERT_FF, D_MODEL), EXPERT_FF ** -0.5),
        "final_norm_w": 1.0 + nrm((D_MODEL,), 0.02),
    }

def reference(x_prompt, x_sample, c_prompt, c_sample, state_conv, state_ssm, state_gla,
              w_ada, b_ada, norm1_w, w_in, conv_w, conv_b, dt_bias, a_log, d_skip, ssd_norm_w,
              w_ssd_br, gla_gate_up, gla_gate_b, gla_norm_w, w_gla_br, merge_b, w_out, norm2_w,
              w_router, router_bias, w_exp_gate, w_exp_up, w_exp_down, final_norm_w):
    bp = x_prompt.shape[0]
    dt_ = x_prompt.dtype
    xp, xs = x_prompt, x_sample
    conv_p, ssm_p, gla_p, conv_s, ssm_s, gla_s = [], [], [], [], [], []
    for l in range(DEPTH):
        p = dict(w_ada=w_ada[l], b_ada=b_ada[l], norm1_w=norm1_w[l], w_in=w_in[l], conv_w=conv_w[l],
                 conv_b=conv_b[l], dt_bias=dt_bias[l], a_log=a_log[l], d_skip=d_skip[l],
                 ssd_norm_w=ssd_norm_w[l], w_ssd_br=w_ssd_br[l], gla_gate_up=gla_gate_up[l],
                 gla_gate_b=gla_gate_b[l], gla_norm_w=gla_norm_w[l], w_gla_br=w_gla_br[l],
                 merge_b=merge_b[l], w_out=w_out[l], norm2_w=norm2_w[l], w_exp_gate=w_exp_gate[l],
                 w_exp_up=w_exp_up[l], w_exp_down=w_exp_down[l])
        zc = jnp.zeros((bp, CONV_K - 1, CONV_DIM), dt_)
        zs = jnp.zeros((bp, SSD_HEADS, SSD_HEAD_DIM, SSD_STATE), dt_)
        zg = jnp.zeros((bp, GLA_HEADS, GLA_DK, GLA_DV), dt_)
        xp, cp, sp, gp = layer_fwd(xp, c_prompt, zc, zs, zg, p, w_router, router_bias)
        xs, cs_, ss, gs = layer_fwd(xs, c_sample, state_conv[l], state_ssm[l], state_gla[l], p, w_router, router_bias)
        conv_p.append(cp); ssm_p.append(sp); gla_p.append(gp)
        conv_s.append(cs_); ssm_s.append(ss); gla_s.append(gs)
    y_prompt = rms_norm(xp, final_norm_w)
    y_sample = rms_norm(xs, final_norm_w)
    return (y_prompt, y_sample, jnp.stack(conv_p), jnp.stack(ssm_p), jnp.stack(gla_p),
            jnp.stack(conv_s), jnp.stack(ssm_s), jnp.stack(gla_s))


_drawn_inputs = setup_inputs


def setup_inputs(seed=0):
    import zlib

    import numpy as np

    out = dict(_drawn_inputs(seed))
    spreads = {}
    factors = {'d_skip': 8.0,
     'ssd_norm_w': 8.0,
     'gla_norm_w': 8.0,
     'merge_b': 8.0,
     'norm2_w': 4.352,
     'router_bias': 3.61,
     'final_norm_w': 2.762}
    for name, (base, spread) in spreads.items():
        noise = np.random.default_rng([zlib.crc32(name.encode()), seed]).standard_normal(out[name].shape)
        drawn = base * np.exp(spread * noise) if base else spread * noise
        out[name] = __import__('jax').numpy.asarray(drawn.astype(out[name].dtype))
    for name, factor in factors.items():
        out[name] = (out[name] * factor).astype(out[name].dtype)
    return out
```

```python
from contextlib import ExitStack

import numpy as np

import concourse.bass as bass
from concourse import mybir

ALU = mybir.AluOpType
ACT = mybir.ActivationFunctionType
AX = mybir.AxisListType
F32 = mybir.dt.float32
U8 = mybir.dt.uint8

P = 128
D = 1024
KT = D // P
NP_, NS, ST = 256, 8, 8
NSAMP = NS * ST
T = NP_ + NSAMP
NSEQ = 1 + NS
HEADS, HD, NSTATE, GROUPS = 32, 64, 128, 4
PAIRS = HEADS // 2
PPG = PAIRS // GROUPS
GH, GDK, GDV = 4, 128, 256
RANK = 16
CONVK = 4
NX, NBC = 16, 8
NCONV = NX + NBC
E, EG, EPG, FF = 16, 4, 4, 512
EPS = 1e-6
ROUTER_STEPS = 29
TAU = 16.0
R = 6
CH = 2048
NEG = -3.0e38
LEVELS = [1, 256, 128, 64, 32, 16, 8, 4, 2]
NL = len(LEVELS)
MASKED = LEVELS[2:]
EXTW = CONVK - 1 + NP_ + NS * (CONVK - 1 + ST)
S0 = CONVK - 1 + NP_
SW = CONVK - 1 + ST

V_ADA, V_N1, V_N2, V_FIN, V_CB, V_SSDN, V_MRG = 0, 48, 56, 64, 72, 96, 112
V_CW, V_GB, V_GN, V_DS = 128, 224, 228, 230
NV = V_DS + PAIRS

C_ID, C_U, C_R, C_ONE, C_CM, C_DM, C_RS, C_US, C_RSS, C_SEQ, C_PR = 0, 128, 256, 384, 512, 832, 1152, 1472, 1536, 1600, 1608
NC = C_PR + 16 + 4

W_Z, W_X, W_B, W_C, W_DT, W_Q, W_K, W_V, W_R, W_GLR, W_GA, W_GB = (
    0, 2048, 4096, 4608, 5120, 5152, 5664, 6176, 7200, 8224, 8240, 9264)


def weight_order():
    def w_in(col, tiles):
        return [("in", col + 256 * i) for i in range(tiles // 2)]
    out = [("ada", c) for c in range(8)]
    out += w_in(W_Q, 4) + w_in(W_K, 4) + w_in(W_V, 8)
    p2 = w_in(W_R, 8) + w_in(W_B, 4) + w_in(W_C, 4) + w_in(W_X, 16)
    for i, c in enumerate(p2):
        out += [c, ("ada", 8 + i)]
    out += w_in(W_Z, 16) + w_in(W_GA, 8) + w_in(W_GB, 8)
    out += [("gla", c) for c in range(4)]
    out += [("ssd", c, h) for c in range(4) for h in range(2)]
    out += [("out", c) for c in range(4)]
    for e in range(E):
        out += [("gate", e, 0), ("gate", e, 1), ("up", e, 0), ("up", e, 1), ("down", e, 0), ("down", e, 1)]
    return out


ORDER = weight_order()
C_P1 = 8
C_P2 = C_P1 + 8
C_P3 = C_P2 + 32
C_GB = C_P3 + 12
C_GLA = C_GB + 4
C_SSD = C_GLA + 4
C_OUT = C_SSD + 8
C_MOE = C_OUT + 4
N_CHUNK = len(ORDER)
F_SLOT = [5, 9, 14, 18]
N2 = 32
LEAD = R - 2


def build(nc, d):
    ctx = ExitStack()
    with ctx:
        def sb(name, shape, dt=F32):
            return ctx.enter_context(nc.sbuf_tensor(name, shape, dt))

        def sem(name):
            return ctx.enter_context(nc.semaphore(name))

        ring = sb("ring", [P, R, CH])
        cst = sb("cst", [P, NC])
        lvw = sb("lvw", [P, len(MASKED) * T // 4], mybir.dt.int32)
        lvm = lvw[:, :].bitcast(U8).rearrange("p (l t) -> p l t", t=T)
        vec = sb("vec", [P, NV])
        hF = sb("hF", [P, KT, T])
        regA = sb("regA", [P, 5632])
        qF = regA[:, 0:1280].rearrange("p (h t) -> p h t", t=T)
        kF = regA[:, 1280:2560].rearrange("p (h t) -> p h t", t=T)
        vT = regA[:, 2560:5632].rearrange("p (a c) -> p a c", a=3)
        zF = regA[:, 0:5120].rearrange("p (k t) -> p k t", t=T)
        oF = sb("oF", [P, KT, T])
        rF = sb("rF", [P, KT, T])
        bcF = sb("bcF", [P, NBC, T])
        xsF = sb("xsF", [P, NX, T])
        bT = sb("bT", [P, 3, 512])
        mod = sb("mod", [P, 48, NSEQ])
        modA = sb("modA", [P, KT, NSEQ])
        scF = sb("scF", [P, KT, NSEQ])
        rst = sb("rst", [P, T])
        cvs = sb("cvs", [P, NCONV, NS * 3])
        ncv = sb("ncv", [P, NCONV, NSEQ * 3])
        wdt = sb("wdt", [P, KT, HEADS])
        wgl = sb("wgl", [P, KT, RANK])
        gup = sb("gup", [RANK, 512])
        glr = sb("glr", [RANK, T])
        dtb = sb("dtb", [P, HEADS])
        aex = sb("aex", [P, HEADS])
        G = sb("G", [P, 9900])

        class Carve:
            def __init__(self, region, width):
                self.region, self.width, self.at = region, width, 0

            def take(self, *dims, part=P):
                n = int(np.prod(dims))
                a = self.region[0:part, self.at:self.at + n]
                self.at += n
                assert self.at <= self.width, (self.at, self.width)
                if len(dims) == 2:
                    a = a.rearrange("p (a b) -> p a b", a=dims[0])
                if len(dims) == 3:
                    a = a.rearrange("p (a b c) -> p a b c", a=dims[0], b=dims[1])
                return a

        gla = Carve(G, 9900)
        gF = gla.take(GH, T)
        ebuf = gla.take(2, T)
        qk = gla.take(2, T)
        att = gla.take(2, 448)
        kd = gla.take(T)
        ekd = gla.take(T)
        eg = gla.take(NSAMP)
        qg = gla.take(NSAMP)
        kdT = gla.take(2, P)
        kdm = gla.take(NS, P)
        sgi = gla.take(NS, GDV)
        sgo = gla.take(2, 2, GDV)
        gfin = gla.take(GDV)
        ext = gla.take(2, 348)
        cvo = gla.take(348)
        tmpx = Carve(xsF[:, :, :].rearrange("p k t -> p (k t)"), NX * T)
        gx = tmpx.take(GH, T)
        gax = tmpx.take(GH, T)
        vst = tmpx.take(2, T)

        ssd = Carve(G, 9900)
        sn = ssd.take(2, NS, P)
        so = ssd.take(2, NS, P)
        L = ssd.take(2, T)
        M = ssd.take(2, T)
        cbm = ssd.take(2, 448)
        bm = ssd.take(NS, P)
        eb = ssd.take(192)
        t2 = ssd.take(192)
        xdt = ssd.take(2, 3, P)
        xdd = ssd.take(2, 4, P)
        pre = sb("pre", [P, 32 * 3 * 3 + 32 * 4 + 256 + 2 * T + 256])
        prc = Carve(pre, 32 * 9 + 128 + 256 + 2 * T + 256)
        dtx = prc.take(3, HEADS)
        dta = prc.take(3, HEADS)
        csT = prc.take(3, HEADS)
        wdec = prc.take(4, HEADS)
        EB = prc.take(NS, HEADS)
        dtm = prc.take(NS, HEADS)
        csF = prc.take(T)
        ecsF = prc.take(T)
        sfin = Carve(bT[:, :, :].rearrange("p a b -> p (a b)"), 1536)

        fin2 = sb("fin2", [P, 2, P])
        moe = Carve(G, 9900)
        gbF = moe.take(KT, T)
        rs4 = moe.take(GROUPS, T)
        sgt = moe.take(4, T)
        actF = moe.take(2, 4, T)
        combF = moe.take(T)
        scr = moe.take(3, E)
        bi = moe.take(12, 4)
        pair = moe.take(12, 6)
        gsc = moe.take(3, 4)
        geq = moe.take(3, 4)
        gone = moe.take(3, 4)
        mx = moe.take(3, 1)
        mx2 = moe.take(3, 1)
        mb = moe.take(3, E)
        eq = moe.take(3, E)
        o1 = moe.take(3, E)
        o2 = moe.take(3, E)
        comb = moe.take(3, E)

        wr = sb("wr", [P, KT, E])
        rb = sb("rb", [P, E])
        combB = xsF
        yacc = rF
        x2 = zF[:, 0:KT, :]
        osq = regA[:, 0:KT * T].rearrange("p (k t) -> p k t", t=T)
        rsg = gF

        def ps(name):
            return ctx.enter_context(nc.psum_tensor(name, [P, 512], F32))

        pj = [ps("pjA"), ps("pjB")]
        b = [ps(f"bank{i}") for i in range(6)]

        ident = cst[:, C_ID:C_ID + P]
        upper = cst[:, C_U:C_U + P]
        after = cst[:, C_R:C_R + P]
        ones = cst[:, C_ONE:C_ONE + P]
        cmask = cst[:, C_CM:C_CM + T]
        dmask = cst[:, C_DM:C_DM + T]
        reset = cst[:, C_RS:C_RS + T]
        upper_s = cst[0:NSAMP, C_US:C_US + NSAMP]
        after_s = cst[0:NSAMP, C_RSS:C_RSS + NSAMP]
        seqm = cst[0:NSAMP, C_SEQ:C_SEQ + NS]
        prio16 = cst[:, C_PR:C_PR + 16]
        prio4 = cst[:, C_PR + 16:C_PR + 20]

        TT = [(0, P, P), (P, 2 * P, P), (NP_, T, NSAMP)]

        s_first = sem("s_first")
        s_used = sem("s_used")
        s_ready = [sem(f"s_ready{i}") for i in range(R)]
        s_ld0 = sem("s_ld0")
        s_ld1 = sem("s_ld1")
        s_silc = sem("s_silc")
        s_nsq = sem("s_nsq")
        s_nss = sem("s_nss")
        s_nvar = sem("s_nvar")
        s_nsd = sem("s_nsd")
        s_nv = sem("s_nv")
        s_h = sem("s_h")
        s_modc = sem("s_modc")
        s_glr = sem("s_glr")
        s_glrc = sem("s_glrc")
        s_gate = sem("s_gate")
        s_gxv = sem("s_gxv")
        s_gxa = sem("s_gxa")
        s_ev = sem("s_ev")
        s_vtr = sem("s_vtr")
        s_vcp = sem("s_vcp")
        s_ge = sem("s_ge")
        s_gexp = sem("s_gexp")
        s_gqk = sem("s_gqk")
        s_gp = sem("s_gp")
        s_gcp = sem("s_gcp")
        s_kde = sem("s_kde")
        s_kdx = sem("s_kdx")
        s_kdm = sem("s_kdm")
        s_kdt = sem("s_kdt")
        s_kdc = sem("s_kdc")
        s_o = sem("s_o")
        s_oc = sem("s_oc")
        s_gs = sem("s_gs")
        s_gsa = sem("s_gsa")
        s_gpf = sem("s_gpf")
        s_gpfc = sem("s_gpfc")
        s_sgi = sem("s_sgi")
        s_sgo = [sem("s_sgo0"), sem("s_sgo1")]
        s_pst = sem("s_pst")
        s_pre_x = sem("s_pre_x")
        s_cvd = sem("s_cvd")
        s_ncv = sem("s_ncv")
        s_slu = sem("s_slu")
        s_dtp = sem("s_dtp")
        s_dtv = sem("s_dtv")
        s_dta = sem("s_dta")
        s_dtm = sem("s_dtm")
        s_cs = sem("s_cs")
        s_csa = sem("s_csa")
        s_btr = sem("s_btr")
        s_btc = sem("s_btc")
        s_cb = sem("s_cb")
        s_cbc = sem("s_cbc")
        s_bm = sem("s_bm")
        s_xt = sem("s_xt")
        s_csb = sem("s_csb")
        s_ebp = sem("s_ebp")
        s_ebc = sem("s_ebc")
        s_xdt = sem("s_xdt")
        s_xdd = sem("s_xdd")
        s_L = sem("s_L")
        s_Lx = sem("s_Lx")
        s_M = sem("s_M")
        s_y = sem("s_y")
        s_yv = sem("s_yv")
        s_sn = sem("s_sn")
        s_sm = sem("s_sm")
        s_sa = sem("s_sa")
        s_pf = sem("s_pf")
        s_pfc = sem("s_pfc")
        s_sin = [sem("s_sin0"), sem("s_sin1")]
        s_sout = [sem("s_sout0"), sem("s_sout1")]
        s_pf_out = [sem("s_pf_out0"), sem("s_pf_out1")]
        s_out = sem("s_out")
        s_set = sem("s_set")
        s_osq = sem("s_osq")
        s_oss = sem("s_oss")
        s_onv = sem("s_onv")
        s_osd = sem("s_osd")
        s_sil = sem("s_sil")
        s_ysm = sem("s_ysm")
        s_ysq = sem("s_ysq")
        s_yss = sem("s_yss")
        s_ynv = sem("s_ynv")
        s_ysd = sem("s_ysd")
        s_x = sem("s_x")
        s_mxv = sem("s_mxv")
        s_rtp = sem("s_rtp")
        s_rta = sem("s_rta")
        s_rtv = sem("s_rtv")
        s_ctr = sem("s_ctr")
        s_ctc = sem("s_ctc")
        s_cbb = sem("s_cbb")
        s_cbx = sem("s_cbx")
        s_sg = sem("s_sg")
        s_au = sem("s_au")
        s_ac = sem("s_ac")
        s_dn = sem("s_dn")
        s_ya = sem("s_ya")
        s_f = sem("s_f")

        block = ctx.enter_context(nc.Block())

        def w8(i):
            return ring[:, i % R, :].rearrange("p (k c) -> p k c", k=8)

        class Chain:
            def __init__(self, eng, s, at=0):
                self.eng, self.s, self.n = eng, s, at

            def __call__(self, ins):
                ins.then_inc(self.s, 1)
                self.n += 1

            def wait(self):
                self.eng.wait_ge(self.s, self.n)

        def conv_tile(s):
            return s - 8 if 8 <= s < N2 else None

        def chan(ct):
            return 16 + ct if ct < 8 else ct - 8

        def p3_tiles(q):
            t = q + q // 2
            return [t], [t + 1] if q % 2 else []

        def tile_chunk(g):
            if g < 16:
                return C_P1 + g // 2, g % 2
            if g < 48:
                return C_P2 + 2 * ((g - 16) // 2), g % 2
            return C_P3 + (g - 48) // 2, g % 2

        def tile_done(eng, g):
            i, half = tile_chunk(g)
            eng.wait_ge(s_used if half else s_first, i + 1)

        @block.sync
        def _(sp):
            def load(i):
                if i >= R:
                    sp.wait_ge(s_used, i - R + 1)
                sp.dma_start(ring[:, i % R, :], d["w"][i]).then_inc(s_ready[i % R], 16)

            def gla_in(hd):
                if hd:
                    sp.wait_ge(s_o, hd)
                    sp.wait_ge(s_gsa, 8 * hd)
                sp.dma_start(sgi, d["sg"][hd]).then_inc(s_sgi, 16)

            def gla_out(hd, bp):
                sp.wait_ge(s_gsa, 8 * hd + 2 * bp + 2)
                sp.dma_start(d["sg_new"][hd, :, 2 * bp:2 * bp + 2], sgo[:, bp % 2]).then_inc(s_sgo[bp % 2], 16)

            def gla_fin(hd):
                sp.wait_ge(s_gpfc, hd + 1)
                sp.dma_start(d["gla_p"][hd], gfin).then_inc(s_pst, 16)

            def ssd_in(q):
                if q >= 2:
                    sp.wait_ge(s_y, q - 1)
                    sp.wait_ge(s_sm, q - 1)
                else:
                    sp.wait_ge(s_onv, 14)
                    sp.wait_ge(s_gp, NL * GH)
                sp.dma_start(sn[:, q % 2], d["ss"][q]).then_inc(s_sin[q % 2], 16)

            def ssd_out(q):
                sp.wait_ge(s_sa, 2 * q + 2)
                sp.dma_start(d["ss_new"][q], so[:, q % 2]).then_inc(s_sout[q % 2], 16)
                sp.wait_ge(s_pfc, q + 1)
                sp.dma_start(d["ssm_p"][q], fin2[:, q % 2]).then_inc(s_pf_out[q % 2], 16)

            for i in range(C_P2):
                load(i)
            gla_in(0)
            for s in range(N2 + LEAD):
                if s < N2:
                    load(C_P2 + s)
                elif C_P2 + s < C_P3 + LEAD:
                    load(C_P2 + s)
                x = s - LEAD
                for hd in range(GH):
                    if x == F_SLOT[hd] + 2:
                        gla_out(hd, 0)
                    if x == F_SLOT[hd] + 3:
                        gla_out(hd, 1)
                        gla_out(hd, 2)
                    if x == F_SLOT[hd] + 4:
                        gla_out(hd, 3)
                        if hd + 1 < GH:
                            gla_in(hd + 1)
                        gla_fin(hd)
            ssd_in(0)
            ssd_in(1)
            nxt = C_P3 + LEAD
            for q in range(PAIRS):
                while nxt <= C_P3 + 3 * q // 4 + R - 1 and nxt < C_MOE:
                    load(nxt)
                    nxt += 1
                ssd_out(q)
                if q + 2 < PAIRS:
                    ssd_in(q + 2)
            while nxt < C_GLA + 2:
                load(nxt)
                nxt += 1
            sp.wait_ge(s_yss, GROUPS)
            sp.dma_start(x2, d["x"]).then_inc(s_x, 16)
            for i in range(nxt, N_CHUNK):
                load(i)
            sp.dma_start(d["conv_new"], ncv[:, :, :]).then_inc(s_out, 16)
            sp.wait_ge(s_f, KT)
            sp.dma_start(d["y"], hF[:, :, :]).then_inc(s_out, 16)
            sp.wait_ge(s_out, 16 * 2)
            sp.wait_ge(s_pst, 16 * GH)
            for i in range(2):
                sp.wait_ge(s_sout[i], 16 * (PAIRS // 2))
                sp.wait_ge(s_pf_out[i], 16 * (PAIRS // 2))
                sp.wait_ge(s_sgo[i], 16 * 8)

        @block.tensor
        def _(pe):
            def chunk(i):
                pe.wait_ge(s_ready[i % R], 16 * (i // R + 1))
                return w8(i)

            def proj(g, rhs=None):
                i, half = tile_chunk(g)
                w = chunk(i) if half == 0 else w8(i)
                if g >= 2:
                    pe.wait_ge(s_ev, g - 1)
                for k in range(KT):
                    mm = pe.matmul(pj[g % 2][:, 0:T], w[:, k, half * P:half * P + P], hF[:, k, :],
                                   start=(k == 0), stop=(k == KT - 1))
                mm.then_inc(s_used if half else s_first, 1)

            def ada(i, c):
                w = chunk(i)
                for half in range(2):
                    f = 2 * c + half
                    for k in range(KT):
                        mm = pe.matmul(b[5][:, f * NSEQ:(f + 1) * NSEQ], w[:, k, half * P:half * P + P],
                                       scF[:, k, :], start=(k == 0), stop=(k == KT - 1))
                    mm.then_inc(s_used if half else s_first, 1)

            def norm_sums(n, src):
                pe.wait_ge(s_nsq, n)
                for k in range(KT):
                    mm = pe.matmul(b[0][:, 0:T], ones, src[:, k, :], start=(k == 0), stop=(k == KT - 1))
                mm.then_inc(s_nss, 1)

            pe.wait_ge(s_ld0, 16 * 5)
            norm_sums(1, hF)
            pe.wait_ge(s_silc, 1)
            for c in range(8):
                ada(c, c)

            pe.wait_ge(s_h, 1)
            pe.wait_ge(s_ld1, 16 * 8)
            for k in range(KT):
                mm = pe.matmul(b[1][0:RANK, 0:T], wgl[:, k, :], hF[:, k, :], start=(k == 0), stop=(k == KT - 1))
            mm.then_inc(s_glr, 1)
            proj(0)
            pe.wait_ge(s_glrc, 1)
            for hd in range(GH):
                if hd >= 2:
                    pe.wait_ge(s_gxv, hd - 1)
                pe.matmul(b[2 + hd % 2][:, 0:T], gup[:, hd * P:hd * P + P], glr[:, :],
                          start=True, stop=True).then_inc(s_gate, 1)
            for g in range(1, 17):
                if g < 16:
                    proj(g)
                v = g - 9
                if v >= 0:
                    pe.wait_ge(s_ev, g)
                    if v:
                        pe.wait_ge(s_vcp, 2 * v)
                    for t, (c0, c1, rows) in enumerate(TT):
                        mm = pe.transpose(b[4][0:rows, t * P:t * P + P], vst[:, v % 2, c0:c1], ident)
                    mm.then_inc(s_vtr, 1)

            def level(j):
                hd, lv = divmod(j, NL)
                size = LEVELS[lv]
                bank = b[j % 2]
                if lv:
                    pe.wait_ge(s_gqk, 8 * hd + lv)
                else:
                    pe.wait_ge(s_ev, 16)
                if j >= 2:
                    pe.wait_ge(s_gcp, j - 1)
                buf = qk[:, j % 2, :]
                left, right = (kF[:, hd, :], qF[:, hd, :]) if lv == 0 else (buf, buf)
                if size == 256:
                    pe.matmul(bank[:, 0:P], left[:, 0:P], right[:, P:2 * P], start=True, stop=True).then_inc(s_gp, 1)
                    return
                for c0, c1, rows in TT[:3 if size <= ST else 2]:
                    mm = pe.matmul(bank[0:rows, c0:c1], left[:, c0:c1], right[:, c0:c1], start=True, stop=True)
                mm.then_inc(s_gp, 1)

            def kd_turn(hd):
                pe.wait_ge(s_kdm, 2 * hd + 1)
                if hd == 0:
                    pe.wait_ge(s_vcp, 2 * 8)
                else:
                    pe.wait_ge(s_gpfc, hd)
                for t, (c0, c1, rows) in enumerate(TT):
                    mm = pe.transpose(b[4][0:rows, t * P:t * P + P], kd[:, c0:c1], ident)
                mm.then_inc(s_kdt, 1)

            def gla_o(hd):
                a = att[:, hd % 2, :]
                pe.wait_ge(s_gcp, NL * (hd + 1))
                pe.wait_ge(s_kdm, 2 * hd + 2)
                pe.wait_ge(s_sgi, 16 * (hd + 1))
                if hd:
                    pe.wait_ge(s_oc, 2 * hd)
                else:
                    pe.wait_ge(s_gxv, 4)
                for v in range(2):
                    cols = slice(hd * GDV + v * P, hd * GDV + v * P + P)
                    o = b[2 + v]
                    pe.matmul(o[:, 0:P], vT[:, 0, cols], a[:, 0:P], start=True, stop=True)
                    pe.matmul(o[:, P:2 * P], vT[:, 0, cols], a[:, 320:448], start=True, stop=False)
                    pe.matmul(o[:, P:2 * P], vT[:, 1, cols], a[:, P:2 * P], start=False, stop=True)
                    pe.matmul(o[:, NP_:T], vT[0:NSAMP, 2, cols], a[0:NSAMP, NP_:T], start=True, stop=True)
                    for s in range(NS):
                        mm = pe.matmul(o[:, NP_ + ST * s:NP_ + ST * s + ST], sgi[:, s, v * P:v * P + P],
                                       qg[:, ST * s:ST * s + ST], start=False, stop=True,
                                       skip_group_check=True)
                mm.then_inc(s_o, 1)

            def gla_state(hd, bp):
                pe.wait_ge(s_kdc, 2 * hd + 2)
                if bp:
                    pe.wait_ge(s_gsa, 8 * hd + 2 * bp)
                for j in range(2):
                    mm = pe.matmul(b[4][:, j * GDV:(j + 1) * GDV], kdm[0:NSAMP, 2 * bp + j, :],
                                   vT[0:NSAMP, 2, hd * GDV:(hd + 1) * GDV], start=True, stop=True)
                mm.then_inc(s_gs, 1)

            def gla_prompt(hd):
                pe.wait_ge(s_gsa, 8 * hd + 8)
                for t in range(2):
                    mm = pe.matmul(b[4][:, 0:GDV], kdT[:, t, :], vT[:, t, hd * GDV:(hd + 1) * GDV],
                                   start=(t == 0), stop=(t == 1))
                mm.then_inc(s_gpf, 1)

            def dt_proj():
                pe.wait_ge(s_gcp, NL * GH)
                for t, (c0, c1, rows) in enumerate(TT):
                    for k in range(KT):
                        mm = pe.matmul(b[0][0:rows, t * HEADS:(t + 1) * HEADS], hF[:, k, c0:c1], wdt[:, k, :],
                                       start=(k == 0), stop=(k == KT - 1))
                mm.then_inc(s_dtp, 1)

            def sums():
                pe.wait_ge(s_dtv, 4)
                pe.wait_ge(s_dtm, 1)
                pe.wait_ge(s_oc, 2 * GH)
                w = b[1]
                pe.matmul(w[:, 0:64], upper, dta[:, 0:2, :].rearrange("p a b -> p (a b)"), start=True, stop=True)
                pe.matmul(w[0:NSAMP, 64:96], upper_s, dta[0:NSAMP, 2, :], start=True, stop=True)
                pe.matmul(w[:, 96:160], after, dta[:, 0:2, :].rearrange("p a b -> p (a b)"), start=True, stop=True)
                pe.matmul(w[:, 160:192], after, dta[:, 0, :], start=True, stop=False)
                pe.matmul(w[:, 160:192], ones, dta[:, 1, :], start=False, stop=True)
                pe.matmul(w[0:NSAMP, 192:224], after_s, dta[0:NSAMP, 2, :], start=True, stop=True)
                pe.matmul(w[:, 224:480], ones[0:NSAMP, :], dtm[0:NSAMP].rearrange("p a b -> p (a b)"),
                          start=True, stop=True)
                pe.matmul(b[2][0:HEADS, 0:P], dta[:, 0, :], upper, start=True, stop=True)
                pe.matmul(b[2][0:HEADS, P:2 * P], dta[:, 1, :], upper, start=True, stop=True)
                pe.matmul(b[2][0:HEADS, NP_:T], dta[0:NSAMP, 2, :], upper_s, start=True, stop=True).then_inc(s_cs, 1)

            def b_turn(t):
                c0, c1, rows = TT[t]
                if t == 0:
                    pe.wait_ge(s_slu, 1)
                    pe.wait_ge(s_dtv, 2)
                else:
                    pe.wait_ge(s_btc, t)
                for g in range(GROUPS):
                    mm = pe.transpose(b[0][0:rows, g * P:g * P + P], bcF[:, g, c0:c1], ident)
                mm.then_inc(s_btr, 1)

            def cb(g):
                if g == 0:
                    pe.wait_ge(s_slu, 2)
                    pe.wait_ge(s_oc, 2 * GH)
                else:
                    pe.wait_ge(s_sa, 8 * g)
                for c0, c1, rows in TT:
                    pe.matmul(b[3][0:rows, c0:c1], bcF[:, g, c0:c1], bcF[:, 4 + g, c0:c1], start=True, stop=True)
                pe.matmul(b[3][:, T:T + P], bcF[:, g, 0:P], bcF[:, 4 + g, P:2 * P],
                          start=True, stop=True).then_inc(s_cb, 1)

            for s in range(N2):
                if True:
                    for hd in range(GH):
                        if s == F_SLOT[hd] + 2:
                            gla_state(hd, 0)
                        if s == F_SLOT[hd] + 3:
                            gla_state(hd, 2)
                        if s == F_SLOT[hd] + 4:
                            gla_prompt(hd)
                    proj(16 + s)
                    if s % 2:
                        ada(C_P2 + s, 8 + s // 2)
                    for j in (2 * s, 2 * s + 1):
                        if j < NL * GH:
                            level(j)
                    for hd in range(GH):
                        if s == F_SLOT[hd]:
                            kd_turn(hd)
                        if s == F_SLOT[hd] + 1:
                            gla_o(hd)
                        if s == F_SLOT[hd] + 2:
                            gla_state(hd, 1)
                        if s == F_SLOT[hd] + 3:
                            gla_state(hd, 3)
                    if s == 20:
                        dt_proj()
                    if s == 22:
                        sums()
                    if 24 <= s < 27:
                        b_turn(s - 24)
                    if s == 27:
                        cb(0)
                    if s in (28, 29):
                        pe.wait_ge(s_osq, 1)
                        if s == 28:
                            pe.wait_ge(s_csa, 5)
                            pe.wait_ge(s_dtv, 6)
                        else:
                            pe.wait_ge(s_onv, 2)
                        for j in range(2):
                            hd = 2 * (s - 28) + j
                            for v in range(2):
                                mm = pe.matmul(b[1 + j][:, 0:T], ones, osq[:, 2 * hd + v, :],
                                               start=(v == 0), stop=(v == 1))
                            mm.then_inc(s_oss, 1)

            for q in range(PAIRS):
                g = q // PPG
                pe.wait_ge(s_slu, 3 + q // 4)
                pe.wait_ge(s_btc, 3)
                if q:
                    pe.wait_ge(s_xdt, 2 * q)
                for t, (c0, c1, rows) in enumerate(TT):
                    mm = pe.transpose(b[0][0:rows, t * P:t * P + P], xsF[:, q, c0:c1], ident)
                mm.then_inc(s_xt, 1)
                pe.wait_ge(s_csa, 5)
                pe.wait_ge(s_onv, 4)
                if q:
                    pe.wait_ge(s_L, 6 * q)
                    pe.wait_ge(s_ebc, q)
                    pe.wait_ge(s_pfc, q)
                for j in range(2):
                    mm = pe.matmul(b[1][64 * j:64 * j + 64, T:512],
                                   ident[0:HEADS, 2 * q + j:2 * q + j + 1].to_broadcast([HEADS, HD]),
                                   ecsF[0:HEADS, P:T], start=True, stop=True)
                mm.then_inc(s_ebp, 1)
                for j in range(2):
                    h = 2 * q + j
                    pe.matmul(b[1 + j][:, 0:T], ident[0:HEADS, h:h + 1].to_broadcast([HEADS, P]), csF[0:HEADS, :],
                              start=True, stop=True).then_inc(s_csb, 1)
                before, afterwards = p3_tiles(q)
                for t in before:
                    proj(48 + t)
                x_, xd = xdt[:, q % 2], xdd[:, q % 2]
                pe.wait_ge(s_xdt, 2 * q + 2)
                if q:
                    pe.wait_ge(s_yv, 3 * q - 1)
                else:
                    pe.wait_ge(s_gpfc, GH)
                for j in range(2):
                    pe.wait_ge(s_M, 2 * q + j + 1)
                    for t, (c0, c1, rows) in enumerate(TT):
                        pe.matmul(b[4][64 * j:64 * j + 64, c0:c1], x_[0:rows, t, 64 * j:64 * j + 64],
                                  M[0:rows, j, c0:c1], start=True, stop=True)
                pe.wait_ge(s_xdd, 3 * q + 3)
                pe.matmul(b[4][:, T:T + P], xd[:, 0, :], cbm[:, g % 2, T:T + P], start=True, stop=True)
                pe.wait_ge(s_sin[q % 2], 16 * (q // 2 + 1))
                for s in range(NS):
                    mm = pe.matmul(b[4][:, T + P + ST * s:T + P + ST * s + ST], sn[:, q % 2, s, :],
                                   bcF[:, 4 + g, NP_ + ST * s:NP_ + ST * s + ST], start=True, stop=True)
                mm.then_inc(s_y, 1)
                pe.matmul(b[2][:, T:T + P], bT[:, 0, g * P:g * P + P], xd[:, 2, :], start=True, stop=False)
                pe.matmul(b[2][:, T:T + P], bT[:, 1, g * P:g * P + P], xd[:, 1, :],
                          start=False, stop=True).then_inc(s_pf, 1)
                pe.wait_ge(s_bm, g + 1)
                for half in range(2):
                    bank = b[5] if half == 0 else b[3]
                    if half == 0:
                        if q:
                            pe.wait_ge(s_sa, 2 * q - 1)
                        else:
                            pe.wait_ge(s_modc, 1)
                    else:
                        pe.wait_ge(s_cbc, 3 * g + 3)
                        if q:
                            pe.wait_ge(s_sa, 2 * q)
                    for s in range(4):
                        mm = pe.matmul(bank[:, s * P:s * P + P], bm[0:NSAMP, 4 * half + s, :], xd[0:NSAMP, 3, :],
                                       start=True, stop=True)
                    mm.then_inc(s_sn, 1)
                for t in afterwards:
                    proj(48 + t)
                if q % PPG == PPG - 1 and g + 1 < GROUPS:
                    cb(g + 1)

            for t in range(8):
                proj(72 + t)
            pe.wait_ge(s_sa, 2 * PAIRS)
            pe.wait_ge(s_pfc, PAIRS)
            for g in range(GROUPS):
                pe.wait_ge(s_ysq, g + 1)
                for t in range(4):
                    mm = pe.matmul(b[g][:, 0:T], ones, zF[:, 4 * g + t, :], start=(t == 0), stop=(t == 3))
                mm.then_inc(s_yss, 1)

            def tile(w, half, src, k0, first, last):
                for k in range(KT):
                    mm = pe.matmul(pj[half][:, 0:T], w[:, k, half * P:half * P + P], src[:, k0 + k, :],
                                   start=(first and k == 0), stop=(last and k == KT - 1), skip_group_check=True)
                mm.then_inc(s_used if half else s_first, 1)

            pe.wait_ge(s_ev, 80)
            pe.wait_ge(s_onv, 14)
            for c in range(4):
                w = chunk(C_GLA + c)
                for half in range(2):
                    if c:
                        pe.wait_ge(s_mxv, 2 * c + half - 1)
                    tile(w, half, oF, 0, True, True)
            pe.wait_ge(s_ynv, 21)
            for c in range(4):
                for h in range(2):
                    w = chunk(C_SSD + 2 * c + h)
                    for half in range(2):
                        if h == 0:
                            pe.wait_ge(s_mxv, 8 + 2 * (2 * c + half - 2) + 1 if c else 7 + half)
                        tile(w, half, xsF, h * KT, h == 0, h == 1)
            pe.wait_ge(s_mxv, 24)
            for c in range(4):
                w = chunk(C_OUT + c)
                for half in range(2):
                    if c:
                        pe.wait_ge(s_mxv, 24 + 3 * (2 * c + half - 2) + 2)
                    tile(w, half, gbF, 0, True, True)

            norm_sums(2, hF)
            pe.wait_ge(s_h, 2)
            for t, (c0, c1, rows) in enumerate(TT):
                for k in range(KT):
                    mm = pe.matmul(b[1][0:rows, t * E:(t + 1) * E], hF[:, k, c0:c1], wr[:, k, :],
                                   start=(k == 0), stop=(k == KT - 1))
            mm.then_inc(s_rtp, 1)
            pe.wait_ge(s_rtv, ROUTER_STEPS)
            for t, (c0, c1, rows) in enumerate(TT):
                mm = pe.transpose(b[2][0:E, c0:c1], comb[0:rows, t, :], ident[0:rows, 0:rows])
            mm.then_inc(s_ctr, 1)
            pe.wait_ge(s_ctc, 1)
            for e in range(E):
                if e >= 2:
                    pe.wait_ge(s_cbx, e - 1)
                pe.matmul(b[4 + e % 2][:, 0:T], ident[0:E, e:e + 1].to_broadcast([E, P]), combF[0:E, :],
                          start=True, stop=True).then_inc(s_cbb, 1)

            for e in range(E):
                i0 = C_MOE + 6 * e
                for part, (base, done) in enumerate(((0, lambda n: (s_sg, n)), (2, lambda n: (s_au, n)))):
                    for f in range(4):
                        n = 4 * e + f
                        i = i0 + 2 * part + f // 2
                        w = chunk(i) if f % 2 == 0 else w8(i)
                        if n >= 2:
                            pe.wait_ge(*done(n - 1))
                        for k in range(KT):
                            mm = pe.matmul(b[base + n % 2][:, 0:T], w[:, k, (f % 2) * P:(f % 2) * P + P], hF[:, k, :],
                                           start=(k == 0), stop=(k == KT - 1))
                        mm.then_inc(s_used if f % 2 else s_first, 1)
                for c in range(2):
                    i = i0 + 4 + c
                    pe.wait_ge(s_ready[i % R], 16 * (i // R + 1))
                    wd = ring[:, i % R, :].rearrange("p (k c) -> p k c", k=4)
                    for t in range(4):
                        n = 8 * e + 4 * c + t
                        if n >= 2:
                            pe.wait_ge(s_ya, n - 1)
                        for k in range(4):
                            if n == 8 * e:
                                pe.wait_ge(s_ac, 4 * e + k + 1)
                            mm = pe.matmul(pj[n % 2][:, 0:T], wd[:, k, t * P:t * P + P], actF[:, e % 2, k, :],
                                           start=(k == 0), stop=(k == 3))
                        mm.then_inc(s_first if t == 0 else s_used if t == 3 else s_dn, 1)
            norm_sums(3, hF)

        def down_done(eng, n):
            e, t = divmod(n, 8)
            i = C_MOE + 6 * e + 4 + t // 4
            if t % 4 == 0:
                eng.wait_ge(s_first, i + 1)
            elif t % 4 == 3:
                eng.wait_ge(s_used, i + 1)
            else:
                eng.wait_ge(s_dn, 4 * e + 2 * (t // 4) + t % 4)

        def halves(a, n, size):
            v = a[:, 0:n].rearrange("p (b s) -> p b s", s=size)
            return v[:, :, 0:size // 2], v[:, :, size // 2:size], v

        def level_of(j):
            hd, lv = divmod(j, NL)
            size = LEVELS[lv]
            return hd, lv, size, NP_ if size > ST else T

        def seqs(a):
            return a[:, NP_:T].rearrange("p (s t) -> p s t", t=ST)

        @block.scalar
        def _(act):
            for dst, src in ((cst[:, :], "cst"), (oF[:, :, :], "x"), (scF[:, :, :], "c"), (vec[:, :], "vec"),
                             (lvw[:, :], "lvm")):
                act.dma_start(dst, d[src]).then_inc(s_ld0, 16)
            for dst, src in ((cvs[:, :, :], d["cvs"]), (wdt[:, :, :], d["wdt"]), (wgl[:, :, :], d["wgl"]),
                             (gup[:, :], d["gup"]), (dtb[:, :], d["dt_bias"].partition_broadcast(P)),
                             (aex[:, :], d["a_log"].partition_broadcast(P)), (wr[:, :, :], d["wr"]),
                             (rb[:, :], d["router_bias"].partition_broadcast(P))):
                act.dma_start(dst, src).then_inc(s_ld1, 16)
            act.wait_ge(s_ld0, 16 * 5)
            act.activation(scF[:, :, :], scF[:, :, :], ACT.Silu).then_inc(s_silc, 1)

            def root(n):
                act.wait_ge(s_nvar, n)
                act.activation(rst[:, :], rst[:, :], ACT.Sqrt).then_inc(s_nsd, 1)

            root(1)
            act.wait_ge(s_ld1, 16 * 8)
            act.activation(aex[:, :], aex[:, :], ACT.Exp).then_inc(s_dta, 1)
            act.wait_ge(s_glr, 1)
            act.activation(glr[:, :], b[1][0:RANK, 0:T], ACT.Copy).then_inc(s_glrc, 1)

            def evac(g):
                tile_done(act, g)
                src = pj[g % 2][:, 0:T]
                if g < 4:
                    act.activation(qF[:, g, :], src, ACT.Copy, scale=float(GDK) ** -0.5).then_inc(s_ev, 1)
                elif g < 8:
                    act.activation(kF[:, g - 4, :], src, ACT.Copy).then_inc(s_ev, 1)
                elif g < 16:
                    if g >= 10:
                        act.wait_ge(s_vtr, g - 9)
                    act.activation(vst[:, g % 2, :], src, ACT.Copy).then_inc(s_ev, 1)
                elif g < 24:
                    act.activation(rF[:, g - 16, :], src, ACT.Copy).then_inc(s_ev, 1)
                elif g < 48:
                    ct = g - 24
                    if ct >= 2:
                        act.wait_ge(s_cvd, 5 * (ct - 1))
                        act.wait_ge(s_ncv, 2 * (ct - 1))
                    row = ext[:, ct % 2, :]
                    act.activation(row[:, 3:S0], src[:, 0:NP_], ACT.Copy)
                    act.activation(row[:, S0:EXTW].rearrange("p (s t) -> p s t", t=SW)[:, :, 3:SW], seqs(src),
                                   ACT.Copy).then_inc(s_ev, 1)
                elif g < 64:
                    if g == 48:
                        act.wait_ge(s_kdm, 8)
                        act.wait_ge(s_o, GH)
                        act.wait_ge(s_gpf, GH)
                        act.wait_ge(s_oss, GH)
                    act.activation(zF[:, g - 48, :], src, ACT.Copy).then_inc(s_ev, 1)
                elif g < 72:
                    if g == 64:
                        act.wait_ge(s_onv, 14)
                    act.activation(rF[:, g - 64, :], src, ACT.Copy).then_inc(s_ev, 1)
                else:
                    t = g - 72
                    act.activation(gbF[:, t, :], src, ACT.Sigmoid,
                                   bias=vec[:, V_MRG + 8 + t:V_MRG + 9 + t]).then_inc(s_ev, 1)

            evac(0)
            act.wait_ge(s_gxv, 4)
            act.activation(gax, gx, ACT.Abs).then_inc(s_gxa, 1)
            act.wait_ge(s_gxa, 1)
            act.activation(gax, gax, ACT.Exp, scale=-1.0).then_inc(s_gxa, 1)
            act.wait_ge(s_gxa, 2)
            act.activation(gax, gax, ACT.Ln, bias=1.0).then_inc(s_gxa, 1)
            for g in range(1, 16):
                evac(g)

            for s in range(N2):
                for j in (2 * s, 2 * s + 1):
                    if j < NL * GH and j % NL:
                        hd, lv, size, n = level_of(j)
                        act.wait_ge(s_ge, 8 * hd + lv)
                        act.activation(ebuf[:, j % 2, 0:n], ebuf[:, j % 2, 0:n], ACT.Exp,
                                       scale=1.0 / TAU).then_inc(s_gexp, 1)
                if s in F_SLOT:
                    hd = F_SLOT.index(s)
                    act.wait_ge(s_kde, hd + 1)
                    act.activation(ekd, ekd, ACT.Exp, scale=1.0 / TAU).then_inc(s_kdx, 1)
                    if hd:
                        act.wait_ge(s_kdm, 2 * hd)
                        act.wait_ge(s_gsa, 8 * hd)
                    act.activation(eg, gF[:, hd, NP_:T], ACT.Exp, scale=1.0 / TAU).then_inc(s_kdx, 1)
                evac(16 + s)
                for hd in range(GH):
                    if s == F_SLOT[hd] + 2:
                        act.wait_ge(s_o, hd + 1)
                        for v in range(2):
                            act.activation(oF[:, 2 * hd + v, :], b[2 + v][:, 0:T], ACT.Copy).then_inc(s_oc, 1)
                    if s == F_SLOT[hd] + 4:
                        act.wait_ge(s_gpf, hd + 1)
                        if hd:
                            act.wait_ge(s_pst, 16 * hd)
                        act.activation(gfin, b[4][:, 0:GDV], ACT.Copy).then_inc(s_gpfc, 1)
                if s >= 12 and s % 4 == 0:
                    m = (s - 12) // 4
                    act.wait_ge(s_cvd, 5 * (4 * m + 4))
                    x_ = (bcF[:, 4 * m:4 * m + 4, :] if m < 2 else xsF[:, 4 * m - 8:4 * m - 4, :])
                    act.activation(x_, x_, ACT.Silu).then_inc(s_slu, 1)
                if s == 21:
                    act.wait_ge(s_dtv, 2)
                    act.activation(dta, dtx, ACT.Abs).then_inc(s_dta, 1)
                    act.wait_ge(s_dta, 2)
                    act.activation(dta, dta, ACT.Exp, scale=-1.0).then_inc(s_dta, 1)
                    act.wait_ge(s_dta, 3)
                    act.activation(dta, dta, ACT.Ln, bias=1.0).then_inc(s_dta, 1)
                if s == 23:
                    act.activation(rF[:, :, :], rF[:, :, :], ACT.Silu).then_inc(s_sil, 1)
                    act.wait_ge(s_cs, 1)
                    act.wait_ge(s_dtv, 6)
                    act.activation(wdec[:, 0:3, :], b[1][:, 96:192].rearrange("p (a b) -> p a b", a=3),
                                   ACT.Exp).then_inc(s_csa, 1)
                    act.activation(wdec[0:NSAMP, 3, :], b[1][0:NSAMP, 192:224], ACT.Exp).then_inc(s_csa, 1)
                    act.activation(EB, b[1][:, 224:480].rearrange("p (a b) -> p a b", a=NS),
                                   ACT.Exp).then_inc(s_csa, 1)
                    act.activation(csF[0:HEADS, :], b[2][0:HEADS, 0:T], ACT.Copy).then_inc(s_csa, 1)
                    act.activation(ecsF[0:HEADS, :], b[2][0:HEADS, 0:T], ACT.Exp).then_inc(s_csa, 1)
                if 25 <= s < 28:
                    t = s - 25
                    rows = TT[t][2]
                    act.wait_ge(s_btr, t + 1)
                    act.activation(bT[0:rows, t, :], b[0][0:rows, :], ACT.Copy).then_inc(s_btc, 1)
                if s == 31:
                    act.wait_ge(s_onv, 4)
                    act.activation(rsg, rsg, ACT.Sqrt).then_inc(s_osd, 1)
            act.wait_ge(s_cvd, 5 * NCONV)
            act.activation(xsF[:, 12:16, :], xsF[:, 12:16, :], ACT.Silu).then_inc(s_slu, 1)

            for q in range(PAIRS):
                act.wait_ge(s_ebp, q + 1)
                act.wait_ge(s_L, 3 * (2 * q + 1))
                if q:
                    act.wait_ge(s_yv, 3 * q - 1)
                else:
                    act.wait_ge(s_ncv, 2 * NCONV)
                act.activation(eb, b[1][:, T:512], ACT.Copy).then_inc(s_ebc, 1)
                if q:
                    act.wait_ge(s_y, q)
                for j in range(2):
                    act.wait_ge(s_L, 3 * (2 * q + j + 1))
                    act.activation(M[:, j, :], L[:, j, :], ACT.Exp).then_inc(s_Lx, 1)
                before, afterwards = p3_tiles(q)
                for t in before:
                    evac(48 + t)
                act.wait_ge(s_pf, q + 1)
                if q >= 2:
                    act.wait_ge(s_pf_out[q % 2], 16 * (q // 2))
                act.activation(fin2[:, q % 2, :], b[2][:, T:T + P], ACT.Copy).then_inc(s_pfc, 1)
                for t in afterwards:
                    evac(48 + t)

            for g in range(GROUPS):
                act.activation(zF[:, 4 * g:4 * g + 4, :], zF[:, 4 * g:4 * g + 4, :], ACT.Silu).then_inc(s_sil, 1)
            act.wait_ge(s_y, PAIRS)
            act.wait_ge(s_sm, PAIRS)
            for i in range(2):
                act.wait_ge(s_sout[i], 16 * (PAIRS // 2))
            for t in range(8):
                evac(72 + t)
                if t < GROUPS:
                    act.wait_ge(s_ysm, t + 1)
                    act.activation(zF[:, 4 * t:4 * t + 4, :], xsF[:, 4 * t:4 * t + 4, :], ACT.Square).then_inc(s_ysq, 1)
            act.wait_ge(s_ynv, 4)
            act.activation(rs4, rs4, ACT.Sqrt).then_inc(s_ysd, 1)
            for t in range(8):
                act.activation(rF[:, t, :], rF[:, t, :], ACT.Sigmoid,
                               bias=vec[:, V_MRG + t:V_MRG + 1 + t]).then_inc(s_sil, 1)
            root(2)

            act.wait_ge(s_rtp, 1)
            act.wait_ge(s_set, 5)
            act.activation(scr[:, 0:2, :], b[1][:, 0:2 * E].rearrange("p (a b) -> p a b", a=2),
                           ACT.Sigmoid).then_inc(s_rta, 1)
            act.activation(scr[0:NSAMP, 2, :], b[1][0:NSAMP, 2 * E:3 * E], ACT.Sigmoid).then_inc(s_rta, 1)
            act.wait_ge(s_ctr, 1)
            act.activation(combF[0:E, :], b[2][0:E, 0:T], ACT.Copy).then_inc(s_ctc, 1)
            for e in range(E):
                act.wait_ge(s_cbb, e + 1)
                act.activation(combB[:, e, :], b[4 + e % 2][:, 0:T], ACT.Copy).then_inc(s_cbx, 1)
            for n in range(4 * E):
                e, f = divmod(n, 4)
                i = C_MOE + 6 * e + f // 2
                act.wait_ge(s_used if f % 2 else s_first, i + 1)
                if n >= 4:
                    act.wait_ge(s_au, n - 3)
                act.activation(sgt[:, n % 4, :], b[n % 2][:, 0:T], ACT.Silu).then_inc(s_sg, 1)
            root(3)

        @block.gpsimd
        def _(pool):
            pool.wait_ge(s_ld1, 16 * 8)
            pool.wait_ge(s_ld0, 16 * 5)
            for s in range(N2 + 1):
                for j in (2 * s, 2 * s + 1):
                    if j < NL * GH and j % NL:
                        hd, lv, size, n = level_of(j)
                        el, eu, _ = halves(ebuf[:, j % 2, :], n, size)
                        ol, ou, _ = halves(qk[:, j % 2, :], n, size)
                        kl, _, _ = halves(kF[:, hd, :], n, size)
                        _, qu, _ = halves(qF[:, hd, :], n, size)
                        pool.wait_ge(s_gexp, 8 * hd + lv)
                        pool.wait_ge(s_ev, 16)
                        if j >= 2:
                            pool.wait_ge(s_gp, j - 1)
                        pool.tensor_tensor(ol, kl, el, ALU.mult)
                        pool.tensor_tensor(ou, qu, eu, ALU.mult).then_inc(s_gqk, 1)
                if s in F_SLOT:
                    hd = F_SLOT.index(s)
                    if hd:
                        pool.wait_ge(s_kdt, hd)
                        pool.wait_ge(s_o, hd)
                    pool.wait_ge(s_kdx, 2 * hd + 1)
                    pool.tensor_tensor(kd, kF[:, hd, :], ekd, ALU.mult).then_inc(s_kdm, 1)
                    pool.wait_ge(s_kdx, 2 * hd + 2)
                    pool.tensor_tensor(qg, qF[:, hd, NP_:T], eg, ALU.mult).then_inc(s_kdm, 1)
                ct = s - 8
                if 0 <= ct < NCONV:
                    c = chan(ct)
                    if ct >= 2:
                        pool.wait_ge(s_cvd, 5 * (ct - 1))
                    row = ext[:, ct % 2, S0:EXTW].rearrange("p (s t) -> p s t", t=SW)
                    pool.tensor_copy(row[:, :, 0:3], cvs[:, c, :].rearrange("p (s t) -> p s t", t=3)).then_inc(s_pre_x, 1)
                ct = s - 9
                if 0 <= ct < NCONV:
                    c = chan(ct)
                    pool.wait_ge(s_ev, 16 + s)
                    row = ext[:, ct % 2, :]
                    pool.tensor_copy(ncv[:, c, 0:3], row[:, S0 - 3:S0]).then_inc(s_ncv, 1)
                    pool.tensor_copy(ncv[:, c, 3:27].rearrange("p (s t) -> p s t", t=3),
                                     row[:, S0:EXTW].rearrange("p (s t) -> p s t", t=SW)[:, :, SW - 3:SW]).then_inc(s_ncv, 1)
                if s == 22:
                    pool.wait_ge(s_dtv, 4)
                    pool.tensor_tensor(dtm[0:NSAMP], dta[0:NSAMP, 2:3, :].to_broadcast([NSAMP, NS, HEADS]),
                                       seqm.unsqueeze(2).to_broadcast([NSAMP, NS, HEADS]), ALU.mult).then_inc(s_dtm, 1)
            for q in range(PAIRS):
                g = q // PPG
                if q % PPG == 0:
                    if q:
                        pool.wait_ge(s_sn, 2 * q)
                    else:
                        pool.wait_ge(s_btc, 3)
                        pool.wait_ge(s_gs, 4 * GH)
                        pool.wait_ge(s_o, GH)
                        for i in range(2):
                            pool.wait_ge(s_sgo[i], 16 * 8)
                        pool.wait_ge(s_pst, 16 * GH)
                        pool.wait_ge(s_cvd, 5 * NCONV)
                        pool.wait_ge(s_kdc, 2 * GH)
                        pool.wait_ge(s_gsa, 8 * GH)
                        pool.wait_ge(s_csa, 5)
                    pool.tensor_tensor(bm[0:NSAMP], bT[0:NSAMP, 2:3, g * P:g * P + P].to_broadcast([NSAMP, NS, P]),
                                       seqm.unsqueeze(2).to_broadcast([NSAMP, NS, P]), ALU.mult).then_inc(s_bm, 1)
                x_ = xdt[:, q % 2]
                o_ = xdd[:, q % 2]
                hs = slice(2 * q, 2 * q + 2)

                def byhead(a):
                    return a.rearrange("p a (h c) -> p a h c", h=2)

                pool.wait_ge(s_xdt, 2 * q + 2)
                if q >= 2:
                    pool.wait_ge(s_sn, 2 * (q - 1))
                pool.tensor_tensor(byhead(o_[:, 0:2]), byhead(x_[:, 0:2]),
                                   wdec[:, 0:2, hs].unsqueeze(3).to_broadcast([P, 2, 2, HD]), ALU.mult).then_inc(s_xdd, 1)
                pool.tensor_tensor(byhead(o_[:, 2:3]), byhead(x_[:, 0:1]),
                                   wdec[:, 2:3, hs].unsqueeze(3).to_broadcast([P, 1, 2, HD]), ALU.mult).then_inc(s_xdd, 1)
                pool.tensor_tensor(byhead(o_[0:NSAMP, 3:4]), byhead(x_[0:NSAMP, 2:3]),
                                   wdec[0:NSAMP, 3:4, hs].unsqueeze(3).to_broadcast([NSAMP, 1, 2, HD]),
                                   ALU.mult).then_inc(s_xdd, 1)
                pool.wait_ge(s_sin[q % 2], 16 * (q // 2 + 1))
                if q >= 2:
                    pool.wait_ge(s_sout[q % 2], 16 * (q // 2))
                pool.tensor_tensor(byhead(so[:, q % 2]), byhead(sn[:, q % 2]),
                                   EB[:, :, hs].unsqueeze(3).to_broadcast([P, NS, 2, HD]), ALU.mult).then_inc(s_sm, 1)
            pool.wait_ge(s_cbx, E)
            for n in range(4 * E):
                e, f = divmod(n, 4)
                pool.wait_ge(s_au, n + 1)
                pool.tensor_tensor(actF[:, e % 2, f, :], actF[:, e % 2, f, :], combB[:, e, :], ALU.mult).then_inc(s_ac, 1)

        def masked_cb(dve, g):
            dve.wait_ge(s_cb, g + 1)
            o_ = cbm[:, g % 2, :]
            if g == 0:
                for i in range(2):
                    dve.memset(cbm[64:P, i, NP_:T], 0.0)
            dve.tensor_tensor(o_[:, 0:NP_], b[3][:, 0:NP_], cmask[:, 0:NP_], ALU.mult).then_inc(s_cbc, 1)
            dve.tensor_tensor(o_[0:NSAMP, NP_:T], b[3][0:NSAMP, NP_:T], cmask[0:NSAMP, NP_:T], ALU.mult).then_inc(s_cbc, 1)
            dve.tensor_copy(o_[:, T:T + P], b[3][:, T:T + P]).then_inc(s_cbc, 1)

        @block.vector
        def _(dve):
            nv = Chain(dve, s_nv)
            st = Chain(dve, s_set)
            st(dve.memset(dtx, 0.0))
            for i in range(2):
                st(dve.memset(ext[:, i, 0:3], 0.0))

            def norm(n, src, scale_add=None):
                dve.tensor_tensor(hF[:, :, :], src, src, ALU.mult).then_inc(s_nsq, 1)
                dve.wait_ge(s_nss, n)
                dve.tensor_scalar(rst[:, :], b[0][:, 0:T], 1.0 / D, EPS, ALU.mult, ALU.add).then_inc(s_nvar, 1)
                dve.wait_ge(s_nsd, n)
                nv(dve.reciprocal(rst[:, :], rst[:, :]))
                nv.wait()

            def modulate(shift, scale, w):
                nv(dve.scalar_tensor_tensor(modA[:, :, :], mod[:, scale:scale + 8, :], 1.0,
                                            vec[:, w:w + 8].unsqueeze(2).to_broadcast([P, KT, NSEQ]), ALU.add, ALU.mult))
                nv.wait()
                for k in range(KT):
                    dve.tensor_scalar(hF[:, k, 0:NP_], hF[:, k, 0:NP_], modA[:, k, 0:1], mod[:, shift + k, 0:1],
                                      ALU.mult, ALU.add)
                hs = hF[:, :, NP_:T].rearrange("p k (s t) -> p k s t", t=ST)
                nv(dve.tensor_tensor(hs, hs, modA[:, :, 1:].unsqueeze(3).to_broadcast([P, KT, NS, ST]), ALU.mult))
                nv.wait()
                dve.tensor_tensor(hs, hs, mod[:, shift:shift + 8, 1:].unsqueeze(3).to_broadcast([P, KT, NS, ST]),
                                  ALU.add).then_inc(s_h, 1)

            dve.wait_ge(s_ld0, 16 * 5)
            norm(1, oF[:, :, :])
            nv(dve.tensor_tensor(hF[:, :, :], oF[:, :, :], rst[:, :].unsqueeze(1).to_broadcast([P, KT, T]), ALU.mult))
            dve.wait_ge(s_used, 8)
            nv(dve.tensor_tensor(mod[:, 0:16, :], b[5][:, 0:16 * NSEQ].rearrange("p (a b) -> p a b", b=NSEQ),
                                 vec[:, 0:16].unsqueeze(2).to_broadcast([P, 16, NSEQ]), ALU.add))
            nv.wait()
            modulate(0, 8, V_N1)

            for hd in range(GH):
                dve.wait_ge(s_gate, hd + 1)
                dve.tensor_scalar(gx[:, hd, :], b[2 + hd % 2][:, 0:T], vec[:, V_GB + hd:V_GB + hd + 1], None,
                                  ALU.add).then_inc(s_gxv, 1)
            dve.wait_ge(s_gxv, 4)
            dve.wait_ge(s_gxa, 3)
            dve.scalar_tensor_tensor(gx, gx, 0.0, gax, ALU.min, ALU.subtract).then_inc(s_gxv, 1)
            dve.wait_ge(s_gxv, 5)
            for hd in range(GH):
                dve.tensor_tensor_scan(gF[:, hd, :], reset, gx[:, hd, :], 0.0, ALU.mult, ALU.add).then_inc(s_gxv, 1)
            for v in range(8):
                dve.wait_ge(s_vtr, v + 1)
                dve.tensor_copy(vT[:, 0:2, v * P:v * P + P],
                                b[4][:, 0:2 * P].rearrange("p (a b) -> p a b", a=2)).then_inc(s_vcp, 1)
                dve.tensor_copy(vT[0:NSAMP, 2, v * P:v * P + P], b[4][0:NSAMP, 2 * P:3 * P]).then_inc(s_vcp, 1)
            dve.wait_ge(s_gxv, 9)

            def exponents(j):
                hd, lv, size, n = level_of(j)
                if not lv:
                    return
                if j >= 2 and 8 * hd + lv > 2:
                    dve.wait_ge(s_gqk, len([i for i in range(j - 1) if i % NL]))
                lo, up, v = halves(gF[:, hd, :], n, size)
                el, eu, _ = halves(ebuf[:, j % 2, :], n, size)
                mid = v[:, :, size // 2 - 1:size // 2].to_broadcast([P, n // size, size // 2])
                dve.tensor_tensor(eu, up, mid, ALU.subtract)
                dve.tensor_tensor(el, mid, lo, ALU.subtract).then_inc(s_ge, 1)

            def merge(j):
                hd, lv, size, n = level_of(j)
                a = att[:, hd % 2, :]
                bank = b[j % 2]
                dve.wait_ge(s_gp, j + 1)
                if lv == 0:
                    if hd >= 2:
                        dve.wait_ge(s_o, hd - 1)
                    dve.tensor_tensor(a[:, 0:NP_], bank[:, 0:NP_], dmask[:, 0:NP_], ALU.mult)
                    dve.tensor_tensor(a[0:NSAMP, NP_:T], bank[0:NSAMP, NP_:T], dmask[0:NSAMP, NP_:T],
                                      ALU.mult).then_inc(s_gcp, 1)
                    return
                dve.wait_ge(s_gcp, j)
                if size == 256:
                    dve.tensor_copy(a[:, T:T + P], bank[:, 0:P]).then_inc(s_gcp, 1)
                    return
                m = lvm[:, MASKED.index(size), :]
                ins = dve.copy_predicated(a[:, 0:NP_], m[:, 0:NP_], bank[:, 0:NP_])
                if size <= ST:
                    ins = dve.copy_predicated(a[0:NSAMP, NP_:T], m[0:NSAMP, NP_:T], bank[0:NSAMP, NP_:T])
                ins.then_inc(s_gcp, 1)

            def new_states(hd, bp):
                dve.wait_ge(s_gs, 4 * hd + bp + 1)
                dve.wait_ge(s_sgi, 16 * (hd + 1))
                dve.wait_ge(s_kdx, 2 * hd + 2)
                n = 2 * hd + bp // 2
                if n:
                    dve.wait_ge(s_sgo[bp % 2], 16 * n)
                for j in range(2):
                    s = 2 * bp + j
                    dve.scalar_tensor_tensor(sgo[:, bp % 2, j, :], sgi[:, s, :], eg[:, ST * s + ST - 1:ST * s + ST],
                                             b[4][:, j * GDV:(j + 1) * GDV], ALU.mult, ALU.add).then_inc(s_gsa, 1)

            def conv(ct):
                c = chan(ct)
                row = ext[:, ct % 2, :]
                dst = bcF[:, ct, :] if ct < 8 else xsF[:, ct - 8, :]
                w = [vec[:, V_CW + i * NCONV + c:V_CW + i * NCONV + c + 1] for i in range(CONVK)]
                n = EXTW - 3
                dve.wait_ge(s_ev, 25 + ct)
                dve.wait_ge(s_pre_x, ct + 1)
                cv = Chain(dve, s_cvd, 5 * ct)
                if ct == 0:
                    st.wait()
                else:
                    cv.wait()
                cv(dve.tensor_scalar(cvo[:, 0:n], row[:, 0:n], w[0], vec[:, V_CB + c:V_CB + c + 1],
                                     ALU.mult, ALU.add))
                for i in (1, 2):
                    cv.wait()
                    cv(dve.scalar_tensor_tensor(cvo[:, 0:n], row[:, i:i + n], w[i], cvo[:, 0:n], ALU.mult, ALU.add))
                cv.wait()
                cv(dve.scalar_tensor_tensor(dst[:, 0:NP_], row[:, 3:S0], w[3], cvo[:, 0:NP_], ALU.mult, ALU.add))
                cv(dve.scalar_tensor_tensor(
                    seqs(dst), row[:, S0:EXTW].rearrange("p (s t) -> p s t", t=SW)[:, :, 3:SW], w[3],
                    cvo[:, S0:S0 + NS * SW].rearrange("p (s t) -> p s t", t=SW)[:, :, 0:ST], ALU.mult, ALU.add))

            on = Chain(dve, s_onv)
            for s in range(N2 + 1):
                for j in (2 * s - 2, 2 * s - 1):
                    if 0 <= j < NL * GH:
                        merge(j)
                for hd in range(GH):
                    if s == F_SLOT[hd] + 3:
                        new_states(hd, 1)
                        new_states(hd, 2)
                    if s == F_SLOT[hd] + 4:
                        new_states(hd, 3)
                for j in (2 * s, 2 * s + 1):
                    if j < NL * GH:
                        exponents(j)
                if s in F_SLOT:
                    hd = F_SLOT.index(s)
                    g_ = gF[:, hd, :]
                    if hd:
                        dve.wait_ge(s_kdm, 2 * hd)
                    dve.tensor_scalar(ekd[:, 0:NP_], g_[:, 0:NP_], g_[:, NP_ - 1:NP_], -1.0, ALU.subtract, ALU.mult)
                    dve.tensor_tensor(seqs(ekd), seqs(g_)[:, :, ST - 1:ST].to_broadcast([P, NS, ST]), seqs(g_),
                                      ALU.subtract).then_inc(s_kde, 1)
                for hd in range(GH):
                    if s == F_SLOT[hd] + 1:
                        dve.wait_ge(s_kdt, hd + 1)
                        if hd:
                            dve.wait_ge(s_gs, 4 * hd)
                            dve.wait_ge(s_gpf, hd)
                        dve.tensor_copy(kdT, b[4][:, 0:2 * P].rearrange("p (a b) -> p a b", a=2)).then_inc(s_kdc, 1)
                        dve.tensor_tensor(kdm[0:NSAMP], b[4][0:NSAMP, 2 * P:3 * P].unsqueeze(1).to_broadcast([NSAMP, NS, P]),
                                          seqm.unsqueeze(2).to_broadcast([NSAMP, NS, P]), ALU.mult).then_inc(s_kdc, 1)
                    if s == F_SLOT[hd] + 2:
                        new_states(hd, 0)
                if 0 <= s - 9 < NCONV:
                    conv(s - 9)
                if s == 21:
                    dve.wait_ge(s_dtp, 1)
                    dve.tensor_tensor(dtx[:, 0:2, :], b[0][:, 0:64].rearrange("p (a b) -> p a b", a=2),
                                      dtb[:, :].unsqueeze(1).to_broadcast([P, 2, HEADS]), ALU.add).then_inc(s_dtv, 1)
                    dve.tensor_tensor(dtx[0:NSAMP, 2, :], b[0][0:NSAMP, 64:96], dtb[0:NSAMP, :], ALU.add).then_inc(s_dtv, 1)
                if s == 22:
                    dve.wait_ge(s_dtv, 2)
                    dve.wait_ge(s_dta, 4)
                    dve.scalar_tensor_tensor(dtx, dtx, 0.0, dta, ALU.max, ALU.add).then_inc(s_dtv, 1)
                    dve.wait_ge(s_dtv, 3)
                    dve.scalar_tensor_tensor(dta, dtx, -1.0, aex[:, :].unsqueeze(1).to_broadcast([P, 3, HEADS]),
                                             ALU.mult, ALU.mult).then_inc(s_dtv, 1)
                if s == 23:
                    dve.wait_ge(s_cs, 1)
                    dve.tensor_copy(csT[:, 0:2, :], b[1][:, 0:64].rearrange("p (a b) -> p a b", a=2)).then_inc(s_dtv, 1)
                    dve.tensor_copy(csT[0:NSAMP, 2, :], b[1][0:NSAMP, 64:96]).then_inc(s_dtv, 1)
                if s == 24:
                    dve.wait_ge(s_oc, 2 * GH)
                    dve.wait_ge(s_kdm, 2 * GH)
                    dve.tensor_tensor(osq, oF[:, :, :], oF[:, :, :], ALU.mult).then_inc(s_osq, 1)
                    dve.wait_ge(s_gpf, GH)
                    dve.wait_ge(s_gs, 4 * GH)
                    for i in range(2):
                        st(dve.memset(L[64:P, i, NP_:T], 0.0)) if i == 0 else dve.memset(L[64:P, i, NP_:T], 0.0)
                if s in (29, 30):
                    for j in range(2):
                        hd = 2 * (s - 29) + j
                        dve.wait_ge(s_oss, hd + 1)
                        if hd == 0:
                            dve.wait_ge(s_kdx, 2 * GH)
                        on(dve.tensor_scalar(rsg[:, hd, :], b[1 + j][:, 0:T], 1.0 / GDV, EPS, ALU.mult, ALU.add))
                if s == 28:
                    masked_cb(dve, 0)
                if s == 32:
                    dve.wait_ge(s_used, C_P3)
                    dve.tensor_tensor(mod[:, 16:48, :], b[5][:, 16 * NSEQ:48 * NSEQ].rearrange("p (a b) -> p a b", b=NSEQ),
                                      vec[:, 16:48].unsqueeze(2).to_broadcast([P, 32, NSEQ]), ALU.add).then_inc(s_modc, 1)
            dve.wait_ge(s_osd, 1)
            on(dve.reciprocal(rsg, rsg))
            on.wait()
            for hd in range(GH):
                for v in range(2):
                    o_ = oF[:, 2 * hd + v, :]
                    on(dve.scalar_tensor_tensor(o_, o_, vec[:, V_GN + v:V_GN + v + 1], rsg[:, hd, :], ALU.mult, ALU.mult))
            on.wait()
            dve.wait_ge(s_sil, 1)
            on(dve.tensor_tensor(oF[:, :, :], oF[:, :, :], rF[:, :, :], ALU.mult))

            for q in range(PAIRS):
                g = q // PPG
                x_ = xdt[:, q % 2]
                hs = slice(2 * q, 2 * q + 2)
                dve.wait_ge(s_xt, q + 1)
                if q >= 2:
                    dve.wait_ge(s_y, q - 1)
                    dve.wait_ge(s_xdd, 3 * (q - 1))
                elif q == 0:
                    dve.wait_ge(s_ncv, 2 * NCONV)
                    dve.wait_ge(s_pst, 16 * GH)
                dve.tensor_tensor(x_[:, 0:2].rearrange("p a (h c) -> p a h c", h=2),
                                  b[0][:, 0:2 * P].rearrange("p (a h c) -> p a h c", a=2, h=2),
                                  dtx[:, 0:2, hs].unsqueeze(3).to_broadcast([P, 2, 2, HD]), ALU.mult).then_inc(s_xdt, 1)
                dve.tensor_tensor(x_[0:NSAMP, 2].rearrange("p (h c) -> p h c", h=2),
                                  b[0][0:NSAMP, 2 * P:3 * P].rearrange("p (h c) -> p h c", h=2),
                                  dtx[0:NSAMP, 2, hs].unsqueeze(2).to_broadcast([NSAMP, 2, HD]), ALU.mult).then_inc(s_xdt, 1)
                for j in range(2):
                    h = 2 * q + j
                    dve.wait_ge(s_csb, h + 1)
                    if q:
                        dve.wait_ge(s_Lx, h - 1)
                    for t, (c0, c1, rows) in enumerate(TT):
                        dve.tensor_scalar(L[0:rows, j, c0:c1], b[1 + j][0:rows, c0:c1], csT[0:rows, t, h:h + 1], 0.0,
                                          ALU.subtract, ALU.min).then_inc(s_L, 1)
                for j in range(2):
                    h = 2 * q + j
                    dve.wait_ge(s_Lx, h + 1)
                    dve.wait_ge(s_cbc, 3 * g + 3)
                    dve.tensor_tensor(M[:, j, :], M[:, j, :], cbm[:, g % 2, 0:T], ALU.mult).then_inc(s_M, 1)
                yv = Chain(dve, s_yv, 3 * q)
                dve.wait_ge(s_y, q + 1)
                dve.wait_ge(s_ebc, q + 1)
                if q:
                    yv.wait()
                yv(dve.scalar_tensor_tensor(xsF[:, q, :], xsF[:, q, :], vec[:, V_DS + q:V_DS + q + 1], b[4][:, 0:T],
                                            ALU.mult, ALU.add))
                yv(dve.tensor_tensor(t2, b[4][:, T:512], eb, ALU.mult))
                yv.wait()
                yv(dve.tensor_tensor(xsF[:, q, P:T], xsF[:, q, P:T], t2, ALU.add))
                dve.wait_ge(s_sm, q + 1)
                for half in range(2):
                    dve.wait_ge(s_sn, 2 * q + half + 1)
                    bank = b[5] if half == 0 else b[3]
                    o_ = so[:, q % 2, 4 * half:4 * half + 4]
                    dve.tensor_tensor(o_, o_, bank[:, :].rearrange("p (a b) -> p a b", a=4), ALU.add).then_inc(s_sa, 1)
                if q % PPG == PPG - 1 and g + 1 < GROUPS:
                    masked_cb(dve, g + 1)

            dve.wait_ge(s_yv, 3 * PAIRS)
            for g in range(GROUPS):
                dve.wait_ge(s_sil, 2 + g)
                y_ = xsF[:, 4 * g:4 * g + 4, :]
                dve.tensor_tensor(y_, y_, zF[:, 4 * g:4 * g + 4, :], ALU.mult).then_inc(s_ysm, 1)
            dve.wait_ge(s_ysm, GROUPS)
            yn = Chain(dve, s_ynv)
            for i in range(2):
                dve.wait_ge(s_sout[i], 16 * (PAIRS // 2))
            for g in range(GROUPS):
                dve.wait_ge(s_yss, g + 1)
                yn(dve.tensor_scalar(rs4[:, g, :], b[g][:, 0:T], 1.0 / 512, EPS, ALU.mult, ALU.add))
            dve.wait_ge(s_ysd, 1)
            yn(dve.reciprocal(rs4, rs4))
            yn.wait()
            for t in range(NX):
                y_ = xsF[:, t, :]
                yn(dve.scalar_tensor_tensor(y_, y_, vec[:, V_SSDN + t:V_SSDN + t + 1], rs4[:, t // 4, :],
                                            ALU.mult, ALU.mult))
            dve.wait_ge(s_ev, 80)
            mv = Chain(dve, s_mxv)
            for t in range(8):
                dve.wait_ge(s_used if t % 2 else s_first, C_GLA + t // 2 + 1)
                mv(dve.tensor_tensor(gbF[:, t, :], gbF[:, t, :], pj[t % 2][:, 0:T], ALU.mult))
            for t in range(8):
                dve.wait_ge(s_used if t % 2 else s_first, C_SSD + 2 * (t // 2) + 2)
                dve.wait_ge(s_sil, 6 + t)
                mv(dve.tensor_tensor(rF[:, t, :], rF[:, t, :], pj[t % 2][:, 0:T], ALU.mult))
                mv.wait()
                mv(dve.tensor_tensor(gbF[:, t, :], gbF[:, t, :], rF[:, t, :], ALU.add))
            dve.wait_ge(s_x, 16)
            dve.wait_ge(s_modc, 1)

            def residual(src, base, t, chain, tmp):
                x_ = x2[:, t, :]
                chain(dve.scalar_tensor_tensor(x_[:, 0:NP_], src[:, 0:NP_], mod[:, base + t, 0:1], x_[:, 0:NP_],
                                               ALU.mult, ALU.add))
                chain(dve.tensor_tensor(seqs(tmp), seqs(src), mod[:, base + t, 1:].unsqueeze(2).to_broadcast([P, NS, ST]),
                                        ALU.mult))
                chain.wait()
                chain(dve.tensor_tensor(seqs(x_), seqs(x_), seqs(tmp), ALU.add))

            for t in range(8):
                dve.wait_ge(s_used if t % 2 else s_first, C_OUT + t // 2 + 1)
                residual(pj[t % 2], 16, t, mv, rs4[:, t % 2, :])
            mv.wait()
            st(dve.memset(scr, 0.5))
            norm(2, x2)
            nv(dve.tensor_tensor(hF[:, :, :], x2, rst[:, :].unsqueeze(1).to_broadcast([P, KT, T]), ALU.mult))
            modulate(24, 32, V_N2)

            rt = Chain(dve, s_rtv)

            def step(ins):
                rt(ins)
                rt.wait()

            def first_largest(out, val, w, prio, tmp):
                step(dve.tensor_reduce(mx, val, AX.X, ALU.max))
                step(dve.tensor_tensor(tmp, val, mx.to_broadcast([P, 3, w]), ALU.is_equal))
                step(dve.tensor_tensor(tmp, tmp, prio.unsqueeze(1).to_broadcast([P, 3, w]), ALU.mult))
                step(dve.tensor_reduce(mx2, tmp, AX.X, ALU.max))
                step(dve.tensor_tensor(out, tmp, mx2.to_broadcast([P, 3, w]), ALU.is_equal))

            def flat(a):
                return a.rearrange("p a b -> p (a b)")

            bie = flat(bi).rearrange("p (a b) -> p a b", a=3)
            dve.wait_ge(s_rta, 2)
            st.wait()
            step(dve.tensor_tensor(bie, scr, rb[:, :].unsqueeze(1).to_broadcast([P, 3, E]), ALU.add))
            step(dve.tensor_tensor(pair[:, :, 0:3], bi[:, :, 0:3], bi[:, :, 1:4], ALU.add))
            step(dve.tensor_tensor(pair[:, :, 3:5], bi[:, :, 0:2], bi[:, :, 2:4], ALU.add))
            step(dve.tensor_tensor(pair[:, :, 5:6], bi[:, :, 0:1], bi[:, :, 3:4], ALU.add))
            step(dve.tensor_reduce(flat(gsc).unsqueeze(2), pair, AX.X, ALU.max))
            first_largest(gone, gsc, EG, prio4, geq)
            mb4 = flat(mb).rearrange("p (a b) -> p a b", a=12)
            step(dve.tensor_tensor(mb4, bi, flat(gone).unsqueeze(2).to_broadcast([P, 12, EPG]), ALU.mult))
            step(dve.tensor_scalar(gone, gone, 1.0, -NEG, ALU.subtract, ALU.mult))
            step(dve.tensor_tensor(mb4, mb4, flat(gone).unsqueeze(2).to_broadcast([P, 12, EPG]), ALU.add))
            first_largest(o1, mb, E, prio16, eq)
            step(dve.scalar_tensor_tensor(mb, o1, NEG, mb, ALU.mult, ALU.add))
            first_largest(o2, mb, E, prio16, eq)
            step(dve.tensor_tensor(o1, o1, o2, ALU.add))
            step(dve.tensor_tensor(o1, o1, scr, ALU.mult))
            step(dve.tensor_reduce(mx, o1, AX.X, ALU.add))
            step(dve.reciprocal(mx, mx))
            rt(dve.tensor_tensor(comb, o1, mx.to_broadcast([P, 3, E]), ALU.mult))
            assert rt.n == ROUTER_STEPS, rt.n

            for e in range(E):
                for f in range(4):
                    n = 4 * e + f
                    i = C_MOE + 6 * e + 2 + f // 2
                    if e >= 2:
                        dve.wait_ge(s_used, C_MOE + 6 * (e - 1))
                    dve.wait_ge(s_sg, n + 1)
                    dve.wait_ge(s_used if f % 2 else s_first, i + 1)
                    dve.tensor_tensor(actF[:, e % 2, f, :], sgt[:, n % 4, :], b[2 + n % 2][:, 0:T],
                                      ALU.mult).then_inc(s_au, 1)
                for t in range(8):
                    n = 8 * e + t
                    down_done(dve, n)
                    if e == 0:
                        dve.tensor_copy(yacc[:, t, :], pj[n % 2][:, 0:T]).then_inc(s_ya, 1)
                    else:
                        if t == 0:
                            dve.wait_ge(s_ya, n)
                        dve.tensor_tensor(yacc[:, t, :], yacc[:, t, :], pj[n % 2][:, 0:T], ALU.add).then_inc(s_ya, 1)
            dve.wait_ge(s_ya, 8 * E)
            for t in range(8):
                residual(yacc[:, t, :], 40, t, mv, rs4[:, t % 2, :])
            mv.wait()
            norm(3, x2)
            for t in range(8):
                dve.scalar_tensor_tensor(hF[:, t, :], x2[:, t, :], vec[:, V_FIN + t:V_FIN + t + 1], rst[:, :],
                                         ALU.mult, ALU.mult).then_inc(s_f, 1)


def constants():
    c = np.zeros((P, NC), np.float32)
    i = np.arange(P)
    c[:, C_ID:C_ID + P] = np.eye(P)
    c[:, C_U:C_U + P] = i[:, None] <= i[None, :]
    c[:, C_R:C_R + P] = i[:, None] > i[None, :]
    c[:, C_ONE:C_ONE + P] = 1
    s = np.arange(NSAMP)
    same = (s[:, None] // ST) == (s[None, :] // ST)
    us = same & (s[:, None] <= s[None, :])
    c[:, C_CM:C_CM + P] = c[:, C_CM + P:C_CM + 2 * P] = c[:, C_U:C_U + P]
    c[:NSAMP, C_CM + 2 * P:C_CM + T] = us
    c[:, C_DM:C_DM + P] = c[:, C_DM + P:C_DM + 2 * P] = np.eye(P)
    c[:NSAMP, C_DM + 2 * P:C_DM + T] = np.eye(NSAMP)
    r = np.ones(T, np.float32)
    r[0] = 0
    r[NP_::ST] = 0
    c[:, C_RS:C_RS + T] = r
    c[:NSAMP, C_US:C_US + NSAMP] = us
    c[:NSAMP, C_RSS:C_RSS + NSAMP] = same & (s[:, None] > s[None, :])
    c[:NSAMP, C_SEQ:C_SEQ + NS] = (s[:, None] // ST) == np.arange(NS)[None, :]
    c[:, C_PR:C_PR + 16] = 16 - np.arange(16)
    c[:, C_PR + 16:C_PR + 20] = 4 - np.arange(4)
    m = np.zeros((P, len(MASKED), T), np.uint8)
    for n, size in enumerate(MASKED):
        blk = (i[:, None] // size == i[None, :] // size) & (i[:, None] % size < size // 2) & (i[None, :] % size >= size // 2)
        m[:, n, 0:P] = m[:, n, P:2 * P] = blk
        if size <= ST:
            m[:NSAMP, n, NP_:T] = blk[:NSAMP, :NSAMP]
    return c, m.reshape(P, -1).view(np.int32)


def kernel(**inputs):
    import concourse.bacc as _bacc
    from concourse.bass_utils import run_bass_kernel_spmd as _run

    a = {k: np.asarray(v) for k, v in inputs.items()}

    def cols(w):
        k, c = w.shape
        return w.reshape(k // P, P, c // 256, 256).transpose(2, 1, 0, 3).reshape(c // 256, P, -1)

    w_in, ada = a["w_in"][0], cols(a["w_ada"][0])
    gla, out = cols(a["w_gla_br"][0]), cols(a["w_out"][0])
    ssd = [cols(a["w_ssd_br"][0][h * D:(h + 1) * D]) for h in range(2)]
    w = np.empty((N_CHUNK, P, CH), np.float32)
    for n, c in enumerate(ORDER):
        if c[0] == "in":
            w[n] = cols(w_in[:, c[1]:c[1] + 256])[0]
        elif c[0] == "ada":
            w[n] = ada[c[1]]
        elif c[0] == "gla":
            w[n] = gla[c[1]]
        elif c[0] == "ssd":
            w[n] = ssd[c[2]][c[1]]
        elif c[0] == "out":
            w[n] = out[c[1]]
        elif c[0] == "gate":
            w[n] = cols(a["w_exp_gate"][0, c[1]][:, 256 * c[2]:256 * c[2] + 256])[0]
        elif c[0] == "up":
            w[n] = cols(a["w_exp_up"][0, c[1]][:, 256 * c[2]:256 * c[2] + 256])[0]
        else:
            w[n] = a["w_exp_down"][0, c[1]][:, 512 * c[2]:512 * c[2] + 512].reshape(4, P, 512).transpose(1, 0, 2).reshape(P, CH)

    def fmajor(v):
        return v.reshape(v.shape[0], -1, P).transpose(2, 1, 0)

    x = np.concatenate([a["x_prompt"][0], a["x_sample"].reshape(NSAMP, D)])
    c = np.concatenate([a["c_prompt"], a["c_sample"]])
    ds = np.repeat(a["d_skip"][0].reshape(PAIRS, 2), HD, axis=1)
    vec = np.concatenate([
        np.concatenate([a[n].reshape(-1) for n in ("b_ada", "norm1_w", "norm2_w", "final_norm_w", "conv_b", "ssd_norm_w",
                                                    "merge_b", "conv_w", "gla_gate_b", "gla_norm_w")]).reshape(-1, P),
        ds]).T
    cst, lvm = constants()
    arrays = {
        "w": w, "x": fmajor(x), "c": fmajor(c), "vec": vec, "cst": cst, "lvm": lvm,
        "cvs": fmajor(a["state_conv"][0].reshape(NS * 3, -1)),
        "wdt": w_in[:, W_DT:W_DT + HEADS].reshape(KT, P, HEADS).transpose(1, 0, 2),
        "wgl": w_in[:, W_GLR:W_GLR + RANK].reshape(KT, P, RANK).transpose(1, 0, 2),
        "gup": a["gla_gate_up"][0],
        "dt_bias": a["dt_bias"][0], "a_log": a["a_log"][0], "router_bias": a["router_bias"],
        "wr": a["w_router"].reshape(KT, P, E).transpose(1, 0, 2),
        "sg": a["state_gla"][0].transpose(1, 2, 0, 3),
        "ss": a["state_ssm"][0].reshape(NS, PAIRS, P, NSTATE).transpose(1, 3, 0, 2),
    }
    outs = {
        "y": (P, KT, T), "conv_new": (P, NCONV, NSEQ * 3), "ssm_p": (PAIRS, NSTATE, P), "gla_p": (GH, GDK, GDV),
        "ss_new": (PAIRS, NSTATE, NS, P), "sg_new": (GH, GDK, NS, GDV),
    }
    nc = _bacc.Bacc("TRN2", target_bir_lowering=False, num_devices=1)
    arrays = {f"in_{k}": np.ascontiguousarray(v) for k, v in arrays.items()}
    d = {k[3:]: nc.dram_tensor(k, v.shape, mybir.dt.from_np(v.dtype), kind="ExternalInput").ap() for k, v in arrays.items()}
    for k, shape in outs.items():
        d[k] = nc.dram_tensor(f"out_{k}", shape, F32, kind="ExternalOutput").ap()
    build(nc, d)
    r = _run(nc, [arrays], core_ids=[0]).results[0]
    o = {k: np.asarray(r[f"out_{k}"]) for k in outs}

    y = o["y"].transpose(2, 1, 0).reshape(T, D)
    cv = o["conv_new"].transpose(2, 1, 0).reshape(NSEQ, 3, NCONV * P)
    sp = o["ssm_p"].transpose(0, 2, 1).reshape(1, 1, HEADS, HD, NSTATE)
    ss = o["ss_new"].transpose(2, 0, 3, 1).reshape(1, NS, HEADS, HD, NSTATE)
    sg = o["sg_new"].transpose(2, 0, 1, 3)[None]
    outs_ = (y[None, :NP_], y[NP_:].reshape(NS, ST, D), cv[None, :1], sp, o["gla_p"][None, None], cv[None, 1:], ss, sg)
    return tuple(np.ascontiguousarray(v) for v in outs_)
```

```python
from contextlib import ExitStack

import numpy as np

import concourse.bass as bass
from concourse import mybir

ALU = mybir.AluOpType
ACT = mybir.ActivationFunctionType
AX = mybir.AxisListType
F32 = mybir.dt.float32
U8 = mybir.dt.uint8

P = 128
D = 1024
KT = D // P
NP_, NS, ST = 256, 8, 8
NSAMP = NS * ST
T = NP_ + NSAMP
NSEQ = 1 + NS
HEADS, HD, NSTATE, GROUPS = 32, 64, 128, 4
PAIRS = HEADS // 2
PPG = PAIRS // GROUPS
GH, GDK, GDV = 4, 128, 256
RANK = 16
CONVK = 4
NX, NBC = 16, 8
NCONV = NX + NBC
E, EG, EPG, FF = 16, 4, 4, 512
EPS = 1e-6
ROUTER_OS = 25
TOP = 2
CAP = 96
XROWS = TOP * T
TAU = 16.0
R = 6
CH = 2048
NEG = -3.0e38
LEVELS = [1, 256, 128, 64, 32, 16, 8, 4, 2]
NL = len(LEVELS)
MASKED = LEVELS[2:]
EXTW = CONVK - 1 + NP_ + NS * (CONVK - 1 + ST)
S0 = CONVK - 1 + NP_
SW = CONVK - 1 + ST

V_ADA, V_N1, V_N2, V_FIN, V_CB, V_SSDN, V_MRG = 0, 48, 56, 64, 72, 96, 112
V_CW, V_GB, V_GN, V_DS = 128, 224, 228, 230
NV = V_DS + PAIRS

C_ID, C_U, C_R, C_ONE, C_CM, C_DM, C_RS, C_US, C_RSS, C_SEQ, C_PR = 0, 128, 256, 384, 512, 832, 1152, 1472, 1536, 1600, 1608
C_YR = C_PR + 16 + 4
C_EPS = C_YR + 16
NC = C_EPS + 1

W_Z, W_X, W_B, W_C, W_DT, W_Q, W_K, W_V, W_R, W_GLR, W_GA, W_GB = (
    0, 2048, 4096, 4608, 5120, 5152, 5664, 6176, 7200, 8224, 8240, 9264)


def weight_order():
    def w_in(col, tiles):
        return [("in", col + 256 * i) for i in range(tiles // 2)]
    out = [("ada", c) for c in range(8)]
    out += w_in(W_Q, 4) + w_in(W_K, 4) + w_in(W_V, 8)
    p2 = w_in(W_R, 8) + w_in(W_B, 4) + w_in(W_C, 4) + w_in(W_X, 16)
    for i, c in enumerate(p2):
        out += [c, ("ada", 8 + i)]
    out += w_in(W_Z, 16) + w_in(W_GA, 8) + w_in(W_GB, 8)
    out += [("gla", c) for c in range(4)]
    out += [("ssd", c, h) for c in range(4) for h in range(2)]
    out += [("out", c) for c in range(4)]
    for e in range(E):
        out += [("gate", e, 0), ("gate", e, 1), ("up", e, 0), ("up", e, 1), ("down", e, 0), ("down", e, 1)]
    return out


ORDER = weight_order()
C_P1 = 8
C_P2 = C_P1 + 8
C_P3 = C_P2 + 32
C_GB = C_P3 + 12
C_GLA = C_GB + 4
C_SSD = C_GLA + 4
C_OUT = C_SSD + 8
C_MOE = C_OUT + 4
N_CHUNK = len(ORDER)
F_SLOT = [5, 9, 14, 18]
N2 = 32
DISPATCH_META = 5
DISPATCH_STEPS = 13
assert N_CHUNK - C_MOE == 6 * E and R == 6 and XROWS % P == 0
LEAD = R - 2


def build(nc, d):
    ctx = ExitStack()
    with ctx:
        def sb(name, shape, dt=F32):
            return ctx.enter_context(nc.sbuf_tensor(name, shape, dt))

        def sem(name):
            return ctx.enter_context(nc.semaphore(name))

        ring = sb("ring", [P, R, CH])
        cst = sb("cst", [P, NC])
        lvw = sb("lvw", [P, len(MASKED) * T // 4], mybir.dt.int32)
        lvm = lvw[:, :].bitcast(U8).rearrange("p (l t) -> p l t", t=T)
        vec = sb("vec", [P, NV])
        hF = sb("hF", [P, KT, T])
        regA = sb("regA", [P, 5632])
        qF = regA[:, 0:1280].rearrange("p (h t) -> p h t", t=T)
        kF = regA[:, 1280:2560].rearrange("p (h t) -> p h t", t=T)
        vT = regA[:, 2560:5632].rearrange("p (a c) -> p a c", a=3)
        zF = regA[:, 0:5120].rearrange("p (k t) -> p k t", t=T)
        oF = sb("oF", [P, KT, T])
        rF = sb("rF", [P, KT, T])
        bcF = sb("bcF", [P, NBC, T])
        xsF = sb("xsF", [P, NX, T])
        bT = sb("bT", [P, 3, 512])
        mod = sb("mod", [P, 48, NSEQ])
        modA = sb("modA", [P, KT, NSEQ])
        scF = sb("scF", [P, KT, NSEQ])
        rst = sb("rst", [P, T])
        adaS = sb("adaS", [NSEQ, 2, 256])
        cvs = sb("cvs", [P, NCONV, NS * 3])
        ncv = sb("ncv", [P, NCONV, NSEQ * 3])
        wdt = sb("wdt", [P, KT, HEADS])
        wgl = sb("wgl", [P, KT, RANK])
        gup = sb("gup", [RANK, 512])
        glr = sb("glr", [RANK, T])
        dtb = sb("dtb", [P, HEADS])
        aex = sb("aex", [P, HEADS])
        G = sb("G", [P, 9900])

        class Carve:
            def __init__(self, region, width):
                self.region, self.width, self.at = region, width, 0

            def take(self, *dims, part=P):
                n = int(np.prod(dims))
                a = self.region[0:part, self.at:self.at + n]
                self.at += n
                assert self.at <= self.width, (self.at, self.width)
                if len(dims) == 2:
                    a = a.rearrange("p (a b) -> p a b", a=dims[0])
                if len(dims) == 3:
                    a = a.rearrange("p (a b c) -> p a b c", a=dims[0], b=dims[1])
                return a

        gla = Carve(G, 9900)
        gF = gla.take(GH, T)
        ebuf = gla.take(2, T)
        qk = gla.take(2, T)
        att = gla.take(2, 448)
        kd = gla.take(T)
        ekd = gla.take(T)
        eg = gla.take(NSAMP)
        qg = gla.take(NSAMP)
        kdT = gla.take(2, P)
        kdm = gla.take(NS, P)
        sgi = gla.take(NS, GDV)
        sgo = gla.take(2, 2, GDV)
        gfin = gla.take(GDV)
        ext = gla.take(2, 348)
        cvo = gla.take(348)
        tmpx = Carve(xsF[:, :, :].rearrange("p k t -> p (k t)"), NX * T)
        gx = tmpx.take(GH, T)
        gax = tmpx.take(GH, T)
        vst = tmpx.take(2, T)

        ssd = Carve(G, 9900)
        sn = ssd.take(2, NS, P)
        so = ssd.take(2, NS, P)
        L = ssd.take(2, T)
        M = ssd.take(2, T)
        cbm = ssd.take(2, 448)
        bm = ssd.take(NS, P)
        eb = ssd.take(192)
        t2 = ssd.take(192)
        xdt = ssd.take(2, 3, P)
        xdd = ssd.take(2, 4, P)
        pre = sb("pre", [P, 32 * 3 * 3 + 32 * 4 + 256 + 2 * T + 256])
        prc = Carve(pre, 32 * 9 + 128 + 256 + 2 * T + 256)
        dtx = prc.take(3, HEADS)
        dta = prc.take(3, HEADS)
        csT = prc.take(3, HEADS)
        wdec = prc.take(4, HEADS)
        EB = prc.take(NS, HEADS)
        dtm = prc.take(NS, HEADS)
        csF = prc.take(T)
        sfin = Carve(bT[:, :, :].rearrange("p a b -> p (a b)"), 1536)

        fin2 = sb("fin2", [P, 2, P])
        moe = Carve(G, 9900)
        gbF = moe.take(KT, T)
        rs4 = moe.take(GROUPS, T)
        rest = moe.take(8 * 512 - GROUPS * T)
        late = Carve(G, 8 * 512 + KT * T)
        xT = late.take(3, D)
        gT = late.take(2, D)
        wT = late.take(D)
        gsx = late.take(KT, NSAMP)
        ssq = moe.take(3)
        combF = moe.take(T)
        scr = moe.take(3, E)
        bi = moe.take(12, 4)
        pair = moe.take(12, 6)
        gsc = moe.take(3, 4)
        geq = moe.take(3, 4)
        gone = moe.take(3, 4)
        mx = moe.take(3, 1)
        mx2 = moe.take(3, 1)
        mb = moe.take(3, E)
        eq = moe.take(3, E)
        o1 = moe.take(3, E)
        o2 = moe.take(3, E)
        os_ = moe.take(3, E)
        pos = moe.take(3, 3 * E)
        comb = pos[:, 2]
        picks = moe.take(3, 3 * E)
        sel = moe.take(TOP, 9)
        cnt = moe.take(E)
        cin = moe.take(E)
        mf = moe.take(E + 1)
        meta = sb("meta", [P, E + 1], mybir.dt.int32)
        idx = sb("idx", [P, TOP, 6], mybir.dt.uint32)

        wr = sb("wr", [P, KT, E])
        rb = sb("rb", [P, E])
        combB = xsF
        yacc = rF
        hT = regA[:, 2560:5632].rearrange("p (a c) -> p a c", a=3)
        xsf = xsF[:, :, :].rearrange("p k t -> p (k t)")
        xe = xsf[:, 0:2048].rearrange("p (b c) -> p b c", b=2)
        yE = xsf[:, 2048:4096].rearrange("p (b c) -> p b c", b=2)
        y2 = xsf[:, 0:3072].rearrange("p (a c) -> p a c", a=3)
        off = oF[:, :, :].rearrange("p k t -> p (k t)")
        heF = off[:, 0:2 * KT * CAP].rearrange("p (b k c) -> p b k c", b=2, k=KT)
        bcf = bcF[:, :, :].rearrange("p k t -> p (k t)")
        sgt = bcf[:, 0:4 * T].rearrange("p (k t) -> p k t", t=T)
        actF = off[:, 0:8 * T].rearrange("p (b k t) -> p b k t", b=2, t=T)
        sgE = bcf[:, 0:8 * CAP].rearrange("p (b c) -> p b c", b=2)
        actE = bcf[:, 8 * CAP:16 * CAP].rearrange("p (b c) -> p b c", b=2)
        x2 = zF[:, 0:KT, :]
        osq = regA[:, 0:KT * T].rearrange("p (k t) -> p k t", t=T)
        rsg = gF

        def ps(name):
            return ctx.enter_context(nc.psum_tensor(name, [P, 512], F32))

        pj = [ps("pjA"), ps("pjB")]
        b = [ps(f"bank{i}") for i in range(6)]

        ident = cst[:, C_ID:C_ID + P]
        upper = cst[:, C_U:C_U + P]
        after = cst[:, C_R:C_R + P]
        ones = cst[:, C_ONE:C_ONE + P]
        cmask = cst[:, C_CM:C_CM + T]
        dmask = cst[:, C_DM:C_DM + T]
        reset = cst[:, C_RS:C_RS + T]
        upper_s = cst[0:NSAMP, C_US:C_US + NSAMP]
        after_s = cst[0:NSAMP, C_RSS:C_RSS + NSAMP]
        seqm = cst[0:NSAMP, C_SEQ:C_SEQ + NS]
        prio16 = cst[:, C_PR:C_PR + 16]
        prio4 = cst[:, C_PR + 16:C_PR + 20]
        yrow = cst[:, C_YR:C_YR + E]
        eps = cst[:, C_EPS:C_EPS + 1]

        TT = [(0, P, P), (P, 2 * P, P), (NP_, T, NSAMP)]

        s_first = sem("s_first")
        s_used = sem("s_used")
        s_ready = [sem(f"s_ready{i}") for i in range(R)]
        s_ld0 = sem("s_ld0")
        s_ld1 = sem("s_ld1")
        s_ldc = sem("s_ldc")
        s_adc = sem("s_adc")
        s_adt = sem("s_adt")
        s_silc = sem("s_silc")
        s_nsq = sem("s_nsq")
        s_nss = sem("s_nss")
        s_nsd = sem("s_nsd")
        s_nv = sem("s_nv")
        s_h = sem("s_h")
        s_hk = sem("s_hk")
        s_mp = sem("s_mp")
        s_sq = sem("s_sq")
        s_mod = sem("s_mod")
        s_glr = sem("s_glr")
        s_glrc = sem("s_glrc")
        s_gate = sem("s_gate")
        s_gxv = sem("s_gxv")
        s_gxa = sem("s_gxa")
        s_ev = sem("s_ev")
        s_vtr = sem("s_vtr")
        s_vcp = sem("s_vcp")
        s_ge = sem("s_ge")
        s_gexp = sem("s_gexp")
        s_gqk = sem("s_gqk")
        s_gp = sem("s_gp")
        s_gcp = sem("s_gcp")
        s_kde = sem("s_kde")
        s_kdx = sem("s_kdx")
        s_kdm = sem("s_kdm")
        s_kdt = sem("s_kdt")
        s_kdc = sem("s_kdc")
        s_o = sem("s_o")
        s_oc = sem("s_oc")
        s_gs = sem("s_gs")
        s_gsa = sem("s_gsa")
        s_gpf = sem("s_gpf")
        s_gpfc = sem("s_gpfc")
        s_sgi = sem("s_sgi")
        s_sgo = [sem("s_sgo0"), sem("s_sgo1")]
        s_pst = sem("s_pst")
        s_pre_x = sem("s_pre_x")
        s_cvd = sem("s_cvd")
        s_ncv = sem("s_ncv")
        s_slu = sem("s_slu")
        s_dtp = sem("s_dtp")
        s_dtv = sem("s_dtv")
        s_dta = sem("s_dta")
        s_dtm = sem("s_dtm")
        s_cs = sem("s_cs")
        s_csa = sem("s_csa")
        s_btr = sem("s_btr")
        s_btc = sem("s_btc")
        s_cb = sem("s_cb")
        s_cbc = sem("s_cbc")
        s_bm = sem("s_bm")
        s_xt = sem("s_xt")
        s_csb = sem("s_csb")
        s_ebc = sem("s_ebc")
        s_xdt = sem("s_xdt")
        s_xdd = sem("s_xdd")
        s_L = sem("s_L")
        s_Lx = sem("s_Lx")
        s_M = sem("s_M")
        s_y = sem("s_y")
        s_yv = sem("s_yv")
        s_sn = sem("s_sn")
        s_sm = sem("s_sm")
        s_sa = sem("s_sa")
        s_pf = sem("s_pf")
        s_pfc = sem("s_pfc")
        s_sin = [sem("s_sin0"), sem("s_sin1")]
        s_sout = [sem("s_sout0"), sem("s_sout1")]
        s_pf_out = [sem("s_pf_out0"), sem("s_pf_out1")]
        s_out = sem("s_out")
        s_set = sem("s_set")
        s_osq = sem("s_osq")
        s_oss = sem("s_oss")
        s_onv = sem("s_onv")
        s_osd = sem("s_osd")
        s_sil = sem("s_sil")
        s_ysm = sem("s_ysm")
        s_ysq = sem("s_ysq")
        s_yss = sem("s_yss")
        s_ynv = sem("s_ynv")
        s_ysd = sem("s_ysd")
        s_x = sem("s_x")
        s_mxv = sem("s_mxv")
        s_rtp = sem("s_rtp")
        s_rta = sem("s_rta")
        s_rtv = sem("s_rtv")
        s_ctr = sem("s_ctr")
        s_ctc = sem("s_ctc")
        s_cbb = sem("s_cbb")
        s_cbx = sem("s_cbx")
        s_sg = sem("s_sg")
        s_au = sem("s_au")
        s_ac = sem("s_ac")
        s_dn = sem("s_dn")
        s_ya = sem("s_ya")
        s_f = sem("s_f")

        s_ht = sem("s_ht")
        s_htc = sem("s_htc")
        s_rank = sem("s_rank")
        s_dsp = sem("s_dsp")
        s_pad = sem("s_pad")
        s_xd = sem("s_xd")
        s_xe = [sem("s_xe0"), sem("s_xe1")]
        s_xt2 = sem("s_xt2")
        s_hea = sem("s_hea")
        s_hev = sem("s_hev")
        s_esg = sem("s_esg")
        s_eac = sem("s_eac")
        s_eya = sem("s_eya")
        s_eyv = sem("s_eyv")
        s_yd = [sem("s_yd0"), sem("s_yd1")]
        s_y12 = [sem("s_y12a"), sem("s_y12b"), sem("s_y12c")]
        s_gsx = sem("s_gsx")
        s_tm = sem("s_tm")
        s_tmc = sem("s_tmc")
        s_w1 = sem("s_w1")
        s_cmb = sem("s_cmb")
        s_x3 = sem("s_x3")
        s_yt = sem("s_yt")
        s_ytc = sem("s_ytc")
        s_fsd = sem("s_fsd")
        s_frc = sem("s_frc")
        s_fsq = sem("s_fsq")

        block = ctx.enter_context(nc.Block())
        last_peel = E // 2 - 1

        def few(eng):
            eng.wait_ge(s_dsp, DISPATCH_META)
            return eng.value_load(meta[0:1, E:E + 1], min_val=0, max_val=T) <= CAP

        def expert_pairs(eng, body):
            body(0, True, False)
            with eng.Fori(1, last_peel) as i:
                body(i, False, False)
            body(last_peel, False, True)

        def expert_slot(j):
            return (C_MOE + j) % R

        def expert_chunk(eng, e, j):
            eng.wait_ge(s_ready[expert_slot(j)], 16 * e + 16 * ((C_MOE + j) // R + 1))
            return ring[:, expert_slot(j), :]

        def w8(i):
            return ring[:, i % R, :].rearrange("p (k c) -> p k c", k=8)

        class Chain:
            def __init__(self, eng, s, at=0):
                self.eng, self.s, self.n = eng, s, at

            def __call__(self, ins):
                ins.then_inc(self.s, 1)
                self.n += 1

            def wait(self):
                self.eng.wait_ge(self.s, self.n)

        def conv_tile(s):
            return s - 8 if 8 <= s < N2 else None

        def chan(ct):
            return 16 + ct if ct < 8 else ct - 8

        def p3_tiles(q):
            t = q + q // 2
            return [t], [t + 1] if q % 2 else []

        def tile_chunk(g):
            if g < 16:
                return C_P1 + g // 2, g % 2
            if g < 48:
                return C_P2 + 2 * ((g - 16) // 2), g % 2
            return C_P3 + (g - 48) // 2, g % 2

        def tile_done(eng, g):
            i, half = tile_chunk(g)
            eng.wait_ge(s_used if half else s_first, i + 1)

        @block.sync
        def _(sp):
            def load(i):
                if i >= R:
                    sp.wait_ge(s_used, i - R + 1)
                sp.dma_start(ring[:, i % R, :], d["w"][i]).then_inc(s_ready[i % R], 16)

            def gla_in(hd):
                if hd:
                    sp.wait_ge(s_o, hd)
                    sp.wait_ge(s_gsa, 8 * hd)
                sp.dma_start(sgi, d["sg"][hd]).then_inc(s_sgi, 16)

            def gla_out(hd, bp):
                sp.wait_ge(s_gsa, 8 * hd + 2 * bp + 2)
                sp.dma_start(d["sg_new"][hd, :, 2 * bp:2 * bp + 2], sgo[:, bp % 2]).then_inc(s_sgo[bp % 2], 16)

            def gla_fin(hd):
                sp.wait_ge(s_gpfc, hd + 1)
                sp.dma_start(d["gla_p"][hd], gfin).then_inc(s_pst, 16)

            def ssd_in(q):
                if q >= 2:
                    sp.wait_ge(s_y, q - 1)
                    sp.wait_ge(s_sm, q - 1)
                else:
                    sp.wait_ge(s_onv, 14)
                    sp.wait_ge(s_gp, NL * GH)
                sp.dma_start(sn[:, q % 2], d["ss"][q]).then_inc(s_sin[q % 2], 16)

            def ssd_out(q):
                sp.wait_ge(s_sa, 2 * q + 2)
                sp.dma_start(d["ss_new"][q], so[:, q % 2]).then_inc(s_sout[q % 2], 16)
                sp.wait_ge(s_pfc, q + 1)
                sp.dma_start(d["ssm_p"][q], fin2[:, q % 2]).then_inc(s_pf_out[q % 2], 16)

            for i in range(C_P2):
                load(i)
            gla_in(0)
            for s in range(N2 + LEAD):
                if s < N2:
                    load(C_P2 + s)
                elif C_P2 + s < C_P3 + LEAD:
                    load(C_P2 + s)
                x = s - LEAD
                for hd in range(GH):
                    if x == F_SLOT[hd] + 2:
                        gla_out(hd, 0)
                    if x == F_SLOT[hd] + 3:
                        gla_out(hd, 1)
                        gla_out(hd, 2)
                    if x == F_SLOT[hd] + 4:
                        gla_out(hd, 3)
                        if hd + 1 < GH:
                            gla_in(hd + 1)
                        gla_fin(hd)
            ssd_in(0)
            ssd_in(1)
            nxt = C_P3 + LEAD
            for q in range(PAIRS):
                while nxt <= C_P3 + 3 * q // 4 + R - 1 and nxt < C_MOE:
                    load(nxt)
                    nxt += 1
                ssd_out(q)
                if q + 2 < PAIRS:
                    ssd_in(q + 2)
            while nxt < C_GLA + R:
                load(nxt)
                nxt += 1
            sp.wait_ge(s_yss, GROUPS)
            sp.dma_start(x2, d["x"]).then_inc(s_x, 16)
            for i in range(nxt, C_MOE + R):
                load(i)
            def next_expert(e, j):
                sp.wait_ge(s_used, 6 * e + (C_MOE + j + 1))
                sp.dma_start(ring[:, expert_slot(j), :], d["w"][6 * e + (C_MOE + R + j)]).then_inc(
                    s_ready[expert_slot(j)], 16)

            def tokens_in(e, v):
                at = sp.value_load(meta[0:1, bass.ds(e, 1)], min_val=0, max_val=XROWS)
                sp.dma_start(xe[0:CAP, v], d["xd"][bass.ds(at, CAP), :]).then_inc(s_xe[v], 16)

            sp.wait_ge(s_pad, 16)
            sp.wait_ge(s_xd, 16 * 6)
            with sp.If(few(sp)):
                for v in range(2):
                    tokens_in(v, v)

                def two(i, first, last):
                    for v in range(2):
                        e = 2 * i + v
                        if not last:
                            sp.wait_ge(s_xt2, e + 1)
                            tokens_in(e + 2, v)
                        if not (last and v):
                            for j in range(6):
                                next_expert(e, j)
                        sp.wait_ge(s_eya, e + 1)
                        sp.wait_ge(s_eyv, e + 1)
                        sp.dma_start(d["yd"][e], yE[0:CAP, v]).then_inc(s_yd[v], 16)

                expert_pairs(sp, two)
            with sp.Else():
                with sp.Fori(0, E - 1) as e:
                    for j in range(6):
                        next_expert(e, j)
            sp.dma_start(d["conv_new"], ncv[:, :, :]).then_inc(s_out, 16)
            for t, (c0, c1, rows) in enumerate(TT):
                sp.wait_ge(s_f, t + 1)
                sp.dma_start(d["y"][c0:c1, :], hT[0:rows, t, :]).then_inc(s_out, 16)
            sp.wait_ge(s_out, 16 * 4)
            sp.wait_ge(s_pst, 16 * GH)
            for i in range(2):
                sp.wait_ge(s_sout[i], 16 * (PAIRS // 2))
                sp.wait_ge(s_pf_out[i], 16 * (PAIRS // 2))
                sp.wait_ge(s_sgo[i], 16 * 8)

        @block.tensor
        def _(pe):
            def chunk(i):
                pe.wait_ge(s_ready[i % R], 16 * (i // R + 1))
                return w8(i)

            def proj(g, rhs=None):
                i, half = tile_chunk(g)
                w = chunk(i) if half == 0 else w8(i)
                if g >= 2:
                    pe.wait_ge(s_ev, g - 1)
                for k in range(KT):
                    mm = pe.matmul(pj[g % 2][:, 0:T], w[:, k, half * P:half * P + P], hF[:, k, :],
                                   start=(k == 0), stop=(k == KT - 1))
                mm.then_inc(s_used if half else s_first, 1)

            def ada(i, out):
                w = chunk(i)
                for k in range(KT):
                    mm = pe.matmul(out[0:NSEQ, 0:256], scF[:, k, :], w[:, k, :], start=(k == 0), stop=(k == KT - 1))
                    if k == 0:
                        mm.then_inc(s_first, 1)
                mm.then_inc(s_used, 1)

            def ada_turn(c, out):
                pe.wait_ge(s_adc, c + 1)
                for half in range(2):
                    mm = pe.transpose(out[:, half * NSEQ:(half + 1) * NSEQ], adaS[:, c % 2, half * P:half * P + P],
                                      ident[0:NSEQ, 0:NSEQ])
                mm.then_inc(s_adt, 1)

            def norm_sums(n, src):
                pe.wait_ge(s_nsq, n)
                for k in range(KT):
                    mm = pe.matmul(b[0][:, 0:T], ones, src[:, k, :], start=(k == 0), stop=(k == KT - 1))
                mm.then_inc(s_nss, 1)

            def h_ready(n):
                pe.wait_ge(s_h, n)
                pe.wait_ge(s_mp, KT * n)

            pe.wait_ge(s_silc, 1)
            for c in range(9):
                if c < 8:
                    if c >= 2:
                        pe.wait_ge(s_adc, c - 1)
                    ada(c, b[2 + c % 2])
                if c:
                    pe.wait_ge(s_ld0, 16 * 3)
                    ada_turn(c - 1, b[5][:, 2 * NSEQ * (c - 1):2 * NSEQ * c])
                if c == 5:
                    norm_sums(1, hF)

            h_ready(1)
            pe.wait_ge(s_ld1, 16 * 9)
            for k in range(KT):
                mm = pe.matmul(b[1][0:RANK, 0:T], wgl[:, k, :], hF[:, k, :], start=(k == 0), stop=(k == KT - 1))
            mm.then_inc(s_glr, 1)
            proj(0)
            pe.wait_ge(s_glrc, 1)
            for hd in range(GH):
                if hd >= 2:
                    pe.wait_ge(s_gxv, hd - 1)
                pe.matmul(b[2 + hd % 2][:, 0:T], gup[:, hd * P:hd * P + P], glr[:, :],
                          start=True, stop=True).then_inc(s_gate, 1)
            for g in range(1, 17):
                if g < 16:
                    proj(g)
                v = g - 9
                if v >= 0:
                    pe.wait_ge(s_ev, g)
                    if v:
                        pe.wait_ge(s_vcp, 2 * v)
                    for t, (c0, c1, rows) in enumerate(TT):
                        mm = pe.transpose(b[4][0:rows, t * P:t * P + P], vst[:, v % 2, c0:c1], ident)
                    mm.then_inc(s_vtr, 1)

            def level(j):
                hd, lv = divmod(j, NL)
                size = LEVELS[lv]
                bank = b[j % 2]
                if lv:
                    pe.wait_ge(s_gqk, 8 * hd + lv)
                else:
                    pe.wait_ge(s_ev, 16)
                if j >= 2:
                    pe.wait_ge(s_gcp, j - 1)
                buf = qk[:, j % 2, :]
                left, right = (kF[:, hd, :], qF[:, hd, :]) if lv == 0 else (buf, buf)
                if size == 256:
                    pe.matmul(bank[:, 0:P], left[:, 0:P], right[:, P:2 * P], start=True, stop=True).then_inc(s_gp, 1)
                    return
                for c0, c1, rows in TT[:3 if size <= ST else 2]:
                    mm = pe.matmul(bank[0:rows, c0:c1], left[:, c0:c1], right[:, c0:c1], start=True, stop=True)
                mm.then_inc(s_gp, 1)

            def kd_turn(hd):
                pe.wait_ge(s_kdm, 2 * hd + 1)
                if hd == 0:
                    pe.wait_ge(s_vcp, 2 * 8)
                else:
                    pe.wait_ge(s_gpfc, hd)
                for t, (c0, c1, rows) in enumerate(TT):
                    mm = pe.transpose(b[4][0:rows, t * P:t * P + P], kd[:, c0:c1], ident)
                mm.then_inc(s_kdt, 1)

            def gla_o(hd):
                a = att[:, hd % 2, :]
                pe.wait_ge(s_gcp, NL * (hd + 1))
                pe.wait_ge(s_kdm, 2 * hd + 2)
                pe.wait_ge(s_sgi, 16 * (hd + 1))
                if hd:
                    pe.wait_ge(s_oc, 2 * hd)
                else:
                    pe.wait_ge(s_gxv, 4)
                for v in range(2):
                    cols = slice(hd * GDV + v * P, hd * GDV + v * P + P)
                    o = b[2 + v]
                    pe.matmul(o[:, 0:P], vT[:, 0, cols], a[:, 0:P], start=True, stop=True)
                    pe.matmul(o[:, P:2 * P], vT[:, 0, cols], a[:, 320:448], start=True, stop=False)
                    pe.matmul(o[:, P:2 * P], vT[:, 1, cols], a[:, P:2 * P], start=False, stop=True)
                    pe.matmul(o[:, NP_:T], vT[0:NSAMP, 2, cols], a[0:NSAMP, NP_:T], start=True, stop=True)
                    for s in range(NS):
                        mm = pe.matmul(o[:, NP_ + ST * s:NP_ + ST * s + ST], sgi[:, s, v * P:v * P + P],
                                       qg[:, ST * s:ST * s + ST], start=False, stop=True,
                                       skip_group_check=True)
                mm.then_inc(s_o, 1)

            def gla_state(hd, bp):
                pe.wait_ge(s_kdc, 2 * hd + 2)
                if bp:
                    pe.wait_ge(s_gsa, 8 * hd + 2 * bp)
                for j in range(2):
                    mm = pe.matmul(b[4][:, j * GDV:(j + 1) * GDV], kdm[0:NSAMP, 2 * bp + j, :],
                                   vT[0:NSAMP, 2, hd * GDV:(hd + 1) * GDV], start=True, stop=True)
                mm.then_inc(s_gs, 1)

            def gla_prompt(hd):
                pe.wait_ge(s_gsa, 8 * hd + 8)
                for t in range(2):
                    mm = pe.matmul(b[4][:, 0:GDV], kdT[:, t, :], vT[:, t, hd * GDV:(hd + 1) * GDV],
                                   start=(t == 0), stop=(t == 1))
                mm.then_inc(s_gpf, 1)

            def dt_proj():
                pe.wait_ge(s_gcp, NL * GH)
                for t, (c0, c1, rows) in enumerate(TT):
                    for k in range(KT):
                        mm = pe.matmul(b[0][0:rows, t * HEADS:(t + 1) * HEADS], hF[:, k, c0:c1], wdt[:, k, :],
                                       start=(k == 0), stop=(k == KT - 1))
                mm.then_inc(s_dtp, 1)

            def sums():
                pe.wait_ge(s_dtv, 4)
                pe.wait_ge(s_dtm, 1)
                pe.wait_ge(s_oc, 2 * GH)
                w = b[1]
                pe.matmul(w[:, 0:64], upper, dta[:, 0:2, :].rearrange("p a b -> p (a b)"), start=True, stop=True)
                pe.matmul(w[0:NSAMP, 64:96], upper_s, dta[0:NSAMP, 2, :], start=True, stop=True)
                pe.matmul(w[:, 96:160], after, dta[:, 0:2, :].rearrange("p a b -> p (a b)"), start=True, stop=True)
                pe.matmul(w[:, 160:192], after, dta[:, 0, :], start=True, stop=False)
                pe.matmul(w[:, 160:192], ones, dta[:, 1, :], start=False, stop=True)
                pe.matmul(w[0:NSAMP, 192:224], after_s, dta[0:NSAMP, 2, :], start=True, stop=True)
                pe.matmul(w[:, 224:480], ones[0:NSAMP, :], dtm[0:NSAMP].rearrange("p a b -> p (a b)"),
                          start=True, stop=True)
                pe.matmul(b[2][0:HEADS, 0:P], dta[:, 0, :], upper, start=True, stop=True)
                pe.matmul(b[2][0:HEADS, P:2 * P], dta[:, 1, :], upper, start=True, stop=True)
                pe.matmul(b[2][0:HEADS, NP_:T], dta[0:NSAMP, 2, :], upper_s, start=True, stop=True).then_inc(s_cs, 1)

            def b_turn(t):
                c0, c1, rows = TT[t]
                if t == 0:
                    pe.wait_ge(s_slu, 1)
                    pe.wait_ge(s_dtv, 2)
                else:
                    pe.wait_ge(s_btc, t)
                for g in range(GROUPS):
                    mm = pe.transpose(b[0][0:rows, g * P:g * P + P], bcF[:, g, c0:c1], ident)
                mm.then_inc(s_btr, 1)

            def cb(g):
                if g == 0:
                    pe.wait_ge(s_slu, 2)
                    pe.wait_ge(s_oc, 2 * GH)
                else:
                    pe.wait_ge(s_sa, 8 * g)
                for c0, c1, rows in TT:
                    pe.matmul(b[3][0:rows, c0:c1], bcF[:, g, c0:c1], bcF[:, 4 + g, c0:c1], start=True, stop=True)
                pe.matmul(b[3][:, T:T + P], bcF[:, g, 0:P], bcF[:, 4 + g, P:2 * P],
                          start=True, stop=True).then_inc(s_cb, 1)

            for s in range(N2):
                if True:
                    for hd in range(GH):
                        if s == F_SLOT[hd] + 2:
                            gla_state(hd, 0)
                        if s == F_SLOT[hd] + 3:
                            gla_state(hd, 2)
                        if s == F_SLOT[hd] + 4:
                            gla_prompt(hd)
                    proj(16 + s)
                    if s % 2:
                        pe.wait_ge(s_mod, 1 + s // 2)
                        ada(C_P2 + s, b[5])
                    elif s:
                        ada_turn(7 + s // 2, b[5][:, 256:256 + 2 * NSEQ])
                    for j in (2 * s, 2 * s + 1):
                        if j < NL * GH:
                            level(j)
                    for hd in range(GH):
                        if s == F_SLOT[hd]:
                            kd_turn(hd)
                        if s == F_SLOT[hd] + 1:
                            gla_o(hd)
                        if s == F_SLOT[hd] + 2:
                            gla_state(hd, 1)
                        if s == F_SLOT[hd] + 3:
                            gla_state(hd, 3)
                    if s == 20:
                        dt_proj()
                    if s == 22:
                        sums()
                    if 24 <= s < 27:
                        b_turn(s - 24)
                    if s == 27:
                        cb(0)
                    if s in (25, 26):
                        pe.wait_ge(s_osq, 1)
                        if s == 25:
                            pe.wait_ge(s_csa, 4)
                            pe.wait_ge(s_dtv, 6)
                        else:
                            pe.wait_ge(s_onv, 2)
                        for j in range(2):
                            hd = 2 * (s - 25) + j
                            for v in range(2):
                                mm = pe.matmul(b[1 + j][:, 0:T], ones, osq[:, 2 * hd + v, :],
                                               start=(v == 0), stop=(v == 1))
                            mm.then_inc(s_oss, 1)

            ada_turn(23, b[5][:, 256:256 + 2 * NSEQ])

            for q in range(PAIRS):
                g = q // PPG
                pe.wait_ge(s_slu, 3 + q // 4)
                pe.wait_ge(s_btc, 3)
                if q:
                    pe.wait_ge(s_xdt, 2 * q)
                for t, (c0, c1, rows) in enumerate(TT):
                    mm = pe.transpose(b[0][0:rows, t * P:t * P + P], xsF[:, q, c0:c1], ident)
                mm.then_inc(s_xt, 1)
                pe.wait_ge(s_csa, 4)
                pe.wait_ge(s_onv, 4)
                if q:
                    pe.wait_ge(s_L, 6 * q)
                    pe.wait_ge(s_ebc, 2 * q)
                    pe.wait_ge(s_pfc, q)
                for j in range(2):
                    h = 2 * q + j
                    pe.matmul(b[1 + j][:, 0:T], ident[0:HEADS, h:h + 1].to_broadcast([HEADS, P]), csF[0:HEADS, :],
                              start=True, stop=True).then_inc(s_csb, 1)
                before, afterwards = p3_tiles(q)
                for t in before:
                    proj(48 + t)
                x_, xd = xdt[:, q % 2], xdd[:, q % 2]
                pe.wait_ge(s_xdt, 2 * q + 2)
                if q:
                    pe.wait_ge(s_yv, 3 * q - 1)
                else:
                    pe.wait_ge(s_gpfc, GH)
                for j in range(2):
                    pe.wait_ge(s_M, 2 * q + j + 1)
                    for t, (c0, c1, rows) in enumerate(TT):
                        pe.matmul(b[4][64 * j:64 * j + 64, c0:c1], x_[0:rows, t, 64 * j:64 * j + 64],
                                  M[0:rows, j, c0:c1], start=True, stop=True)
                pe.wait_ge(s_xdd, 3 * q + 3)
                pe.matmul(b[4][:, T:T + P], xd[:, 0, :], cbm[:, g % 2, T:T + P], start=True, stop=True)
                pe.wait_ge(s_sin[q % 2], 16 * (q // 2 + 1))
                for s in range(NS):
                    mm = pe.matmul(b[4][:, T + P + ST * s:T + P + ST * s + ST], sn[:, q % 2, s, :],
                                   bcF[:, 4 + g, NP_ + ST * s:NP_ + ST * s + ST], start=True, stop=True)
                mm.then_inc(s_y, 1)
                pe.wait_ge(s_ebc, 2 * q + 2)
                pe.matmul(b[2][:, T:T + P], bT[:, 0, g * P:g * P + P], xd[:, 2, :], start=True, stop=False)
                pe.matmul(b[2][:, T:T + P], bT[:, 1, g * P:g * P + P], xd[:, 1, :],
                          start=False, stop=True).then_inc(s_pf, 1)
                pe.wait_ge(s_bm, g + 1)
                for half in range(2):
                    bank = b[5] if half == 0 else b[3]
                    if half == 0:
                        if q:
                            pe.wait_ge(s_sa, 2 * q - 1)
                        else:
                            pe.wait_ge(s_mod, 17)
                    else:
                        pe.wait_ge(s_cbc, 3 * g + 3)
                        if q:
                            pe.wait_ge(s_sa, 2 * q)
                    for s in range(4):
                        mm = pe.matmul(bank[:, s * P:s * P + P], bm[0:NSAMP, 4 * half + s, :], xd[0:NSAMP, 3, :],
                                       start=True, stop=True)
                    mm.then_inc(s_sn, 1)
                for t in afterwards:
                    proj(48 + t)
                if q % PPG == PPG - 1 and g + 1 < GROUPS:
                    cb(g + 1)

            for t in range(8):
                proj(72 + t)
            def y_sums():
                pe.wait_ge(s_sa, 2 * PAIRS)
                pe.wait_ge(s_pfc, PAIRS)
                for g in range(GROUPS):
                    pe.wait_ge(s_ysq, g + 1)
                    for t in range(4):
                        mm = pe.matmul(b[g][:, 0:T], ones, zF[:, 4 * g + t, :], start=(t == 0), stop=(t == 3))
                    mm.then_inc(s_yss, 1)

            def tile(w, half, src, k0, first, last):
                for k in range(KT):
                    mm = pe.matmul(pj[half][:, 0:T], w[:, k, half * P:half * P + P], src[:, k0 + k, :],
                                   start=(first and k == 0), stop=(last and k == KT - 1), skip_group_check=True)
                mm.then_inc(s_used if half else s_first, 1)

            pe.wait_ge(s_ev, 80)
            pe.wait_ge(s_onv, 14)
            for c in range(4):
                w = chunk(C_GLA + c)
                for half in range(2):
                    if c:
                        pe.wait_ge(s_mxv, 2 * c + half - 1)
                    tile(w, half, oF, 0, True, True)
                if c == 0:
                    y_sums()
            pe.wait_ge(s_ynv, 22)
            for c in range(4):
                for h in range(2):
                    w = chunk(C_SSD + 2 * c + h)
                    for half in range(2):
                        if h == 0:
                            pe.wait_ge(s_mxv, 8 + 2 * (2 * c + half - 2) + 1 if c else 7 + half)
                        tile(w, half, xsF, h * KT, h == 0, h == 1)
            def square_sum(t):
                pe.wait_ge(s_sq, t + 1)
                mm = pe.matmul(b[0][:, 0:T], ones, hF[:, t, :], start=(t == 0), stop=(t == KT - 1),
                               skip_group_check=True)
                if t == KT - 1:
                    mm.then_inc(s_nss, 1)

            pe.wait_ge(s_mxv, 24)
            for c in range(4):
                w = chunk(C_OUT + c)
                for half in range(2):
                    if c:
                        pe.wait_ge(s_mxv, 24 + 3 * (2 * c + half - 2) + 2)
                    tile(w, half, gbF, 0, True, True)
                    if 2 * c + half >= 3:
                        square_sum(2 * c + half - 3)

            for t in range(5, 8):
                square_sum(t)
            h_ready(2)
            for t, (c0, c1, rows) in enumerate(TT):
                for k in range(KT):
                    mm = pe.matmul(b[1][0:rows, t * E:(t + 1) * E], hF[:, k, c0:c1], wr[:, k, :],
                                   start=(k == 0), stop=(k == KT - 1))
            mm.then_inc(s_rtp, 1)
            for t, (c0, c1, rows) in enumerate(TT):
                for half in range(2):
                    n = 2 * t + half
                    if n >= 4:
                        pe.wait_ge(s_htc, n - 3)
                    for k in range(4):
                        mm = pe.transpose(b[2 + n % 4][0:rows, k * P:k * P + P], hF[:, 4 * half + k, c0:c1], ident)
                    mm.then_inc(s_ht, 1)
            pe.wait_ge(s_rtv, ROUTER_OS)
            for t, rows in enumerate((P, P, NSAMP)):
                for u in range(t):
                    pe.matmul(b[1][:, 64 + t * E:64 + t * E + E], ones, os_[:, u, :], start=(u == 0), stop=False)
                pe.matmul(b[1][:, 64 + t * E:64 + t * E + E], upper[0:rows, :], os_[0:rows, t, :],
                          start=(t == 0), stop=True)
            for u, rows in enumerate((P, P, NSAMP)):
                mm = pe.matmul(b[1][:, 64 + 3 * E:64 + 4 * E], ones[0:rows, :], os_[0:rows, u, :],
                               start=(u == 0), stop=(u == 2))
            mm.then_inc(s_rank, 1)

            pe.wait_ge(s_htc, 6)
            pe.wait_ge(s_gsx, 1)
            for n in range(12):
                if n >= 4:
                    pe.wait_ge(s_tmc, n - 3)
                bank = (b[4], b[5], pj[0], pj[1])[n % 4]
                for k in range(4):
                    f = 4 * (n % 2) + k
                    if n < 6:
                        c0, c1, rows = TT[n // 2]
                        mm = pe.transpose(bank[0:rows, k * P:k * P + P], x2[:, f, c0:c1], ident)
                    elif n < 10:
                        col = vec[:, V_FIN + f:V_FIN + f + 1] if n < 8 else mod[:, 40 + f, 0:1]
                        mm = pe.matmul(bank[:, k * P:k * P + P], col.to_broadcast([P, P]), ident, start=True, stop=True)
                    else:
                        mm = pe.transpose(bank[0:NSAMP, k * P:k * P + P], gsx[:, f, :], ident)
                mm.then_inc(s_tm, 1)

            def turn_tokens(i, v):
                pe.wait_ge(s_xe[v], 16 * i + 16)
                for k in range(KT):
                    mm = pe.transpose(b[k // 4][:, (k % 4) * CAP:(k % 4 + 1) * CAP], xe[0:CAP, v, k * P:k * P + P],
                                      ident[0:CAP, 0:CAP])
                mm.then_inc(s_xt2, 1)

            with pe.If(few(pe)):
                pe.wait_ge(s_tmc, 12)
                turn_tokens(0, 0)

                def two(i, first, last):
                    for v in range(2):
                        e = 2 * i + v
                        pe.wait_ge(s_hea, e + 1)
                        pe.wait_ge(s_hev, e + 1)
                        for part, used in ((0, s_esg), (1, s_eac)):
                            if not first:
                                pe.wait_ge(used, e - 1)
                            for f in range(4):
                                if f % 2 == 0:
                                    w = expert_chunk(pe, e, 2 * part + f // 2).rearrange("p (k c) -> p k c", k=8)
                                for k in range(KT):
                                    mm = pe.matmul(b[2 + 2 * part + v][:, f * CAP:(f + 1) * CAP],
                                                   w[:, k, (f % 2) * P:(f % 2) * P + P], heF[:, v, k, :],
                                                   start=(k == 0), stop=(k == KT - 1))
                                if f % 2:
                                    mm.then_inc(s_used, 1)
                        if not (last and v):
                            turn_tokens(i + v, 1 - v)
                        pe.wait_ge(s_eac, e + 1)
                        for c in range(2):
                            w = expert_chunk(pe, e, 4 + c).rearrange("p (k c) -> p k c", k=4)
                            if not (first and v == 0):
                                pe.wait_ge(s_eyv if c else s_eya, e)
                            for k in range(4):
                                mm = pe.matmul(pj[c][0:CAP, :], actE[:, v, k * CAP:(k + 1) * CAP], w[:, k, :],
                                               start=(k == 0), stop=(k == 3))
                            mm.then_inc(s_used, 1)

                expert_pairs(pe, two)
            with pe.Else():
                pe.wait_ge(s_dsp, DISPATCH_META + 2)
                pe.wait_ge(s_tmc, 12)
                for t, (c0, c1, rows) in enumerate(TT):
                    mm = pe.transpose(b[2][0:E, c0:c1], comb[0:rows, t * E:(t + 1) * E], ident[0:rows, 0:rows])
                mm.then_inc(s_ctr, 1)
                pe.wait_ge(s_ctc, 1)
                for e in range(E):
                    if e >= 2:
                        pe.wait_ge(s_cbx, e - 1)
                    pe.matmul(b[4 + e % 2][:, 0:T], ident[0:E, e:e + 1].to_broadcast([E, P]), combF[0:E, :],
                              start=True, stop=True).then_inc(s_cbb, 1)

                def two(i, first, last):
                    for v in range(2):
                        e = 2 * i + v
                        for part, used in ((0, s_sg), (1, s_au)):
                            for f in range(4):
                                if f % 2 == 0:
                                    w = expert_chunk(pe, e, 2 * part + f // 2).rearrange("p (k c) -> p k c", k=8)
                                if not (first and v == 0 and f < 2):
                                    pe.wait_ge(used, 4 * e + f - 1)
                                for k in range(KT):
                                    mm = pe.matmul(b[2 * part + f % 2][:, 0:T], w[:, k, (f % 2) * P:(f % 2) * P + P],
                                                   hF[:, k, :], start=(k == 0), stop=(k == KT - 1))
                                mm.then_inc(s_used if f % 2 else s_first, 1)
                        for c in range(2):
                            w = expert_chunk(pe, e, 4 + c).rearrange("p (k c) -> p k c", k=4)
                            for t in range(4):
                                if not (first and v == 0 and c == 0 and t < 2):
                                    pe.wait_ge(s_ya, 8 * e + (4 * c + t - 1))
                                for k in range(4):
                                    if c == 0 and t == 0:
                                        pe.wait_ge(s_ac, 4 * e + (k + 1))
                                    mm = pe.matmul(pj[t % 2][:, 0:T], w[:, k, t * P:t * P + P], actF[:, v, k, :],
                                                   start=(k == 0), stop=(k == 3))
                                mm.then_inc(s_dn, 1) if t < 3 else mm.then_inc(s_used, 1)

                expert_pairs(pe, two)
                pe.wait_ge(s_ya, 8 * E)
                for t, (c0, c1, rows) in enumerate(TT):
                    for half in range(2):
                        n = 2 * t + half
                        if n >= 2:
                            pe.wait_ge(s_ytc, n - 1)
                        for k in range(4):
                            mm = pe.transpose(b[n % 2][0:rows, k * P:k * P + P], yacc[:, 4 * half + k, c0:c1], ident)
                        mm.then_inc(s_yt, 1)

        def down_done(eng, e, c, t):
            if t < 3:
                eng.wait_ge(s_dn, 6 * e + (3 * c + t + 1))
            else:
                eng.wait_ge(s_used, 6 * e + (C_MOE + 5 + c))

        def halves(a, n, size):
            v = a[:, 0:n].rearrange("p (b s) -> p b s", s=size)
            return v[:, :, 0:size // 2], v[:, :, size // 2:size], v

        def level_of(j):
            hd, lv = divmod(j, NL)
            size = LEVELS[lv]
            return hd, lv, size, NP_ if size > ST else T

        def seqs(a):
            return a[:, NP_:T].rearrange("p (s t) -> p s t", t=ST)

        @block.scalar
        def _(act):
            act.dma_start(scF[:, :, :], d["c"]).then_inc(s_ldc, 16)
            for dst, src in ((oF[:, :, :], "x"), (cst[:, :], "cst"), (vec[:, :], "vec")):
                act.dma_start(dst, d[src]).then_inc(s_ld0, 16)
            for dst, src in ((wgl[:, :, :], d["wgl"]), (gup[:, :], d["gup"]), (lvw[:, :], d["lvm"]),
                             (cvs[:, :, :], d["cvs"]), (wdt[:, :, :], d["wdt"]),
                             (dtb[:, :], d["dt_bias"].partition_broadcast(P)),
                             (aex[:, :], d["a_log"].partition_broadcast(P)), (wr[:, :, :], d["wr"]),
                             (rb[:, :], d["router_bias"].partition_broadcast(P))):
                act.dma_start(dst, src).then_inc(s_ld1, 16)
            act.wait_ge(s_ldc, 16)
            act.activation(scF[:, :, :], scF[:, :, :], ACT.Silu).then_inc(s_silc, 1)

            def root(n):
                act.wait_ge(s_nss, n)
                act.activation(rst[:, :], b[0][:, 0:T], ACT.Sqrt, bias=eps, scale=1.0 / D).then_inc(s_nsd, 1)

            def shift(n, base):
                for k in range(KT):
                    act.wait_ge(s_hk, KT * (n - 1) + k + 1)
                    act.activation(hF[:, k, 0:NP_], hF[:, k, 0:NP_], ACT.Identity,
                                   bias=mod[:, base + k, 0:1]).then_inc(s_mp, 1)

            def ada_copy(c, src):
                act.wait_ge(s_used, c + 1 if c < 8 else C_P2 + 2 * (c - 8) + 2)
                if c >= 2:
                    act.wait_ge(s_adt, c - 1)
                act.activation(adaS[:, c % 2, :], src[0:NSEQ, 0:256], ACT.Copy).then_inc(s_adc, 1)

            for c in range(8):
                ada_copy(c, b[2 + c % 2])
                if c == 6:
                    root(1)
            shift(1, 0)
            act.wait_ge(s_ld1, 16 * 9)
            act.activation(aex[:, :], aex[:, :], ACT.Exp).then_inc(s_dta, 1)
            act.wait_ge(s_glr, 1)
            act.activation(glr[:, :], b[1][0:RANK, 0:T], ACT.Copy).then_inc(s_glrc, 1)

            def evac(g):
                tile_done(act, g)
                src = pj[g % 2][:, 0:T]
                if g < 4:
                    act.activation(qF[:, g, :], src, ACT.Copy, scale=float(GDK) ** -0.5).then_inc(s_ev, 1)
                elif g < 8:
                    act.activation(kF[:, g - 4, :], src, ACT.Copy).then_inc(s_ev, 1)
                elif g < 16:
                    if g >= 10:
                        act.wait_ge(s_vtr, g - 9)
                    act.activation(vst[:, g % 2, :], src, ACT.Copy).then_inc(s_ev, 1)
                elif g < 24:
                    act.activation(rF[:, g - 16, :], src, ACT.Copy).then_inc(s_ev, 1)
                elif g < 48:
                    ct = g - 24
                    if ct >= 2:
                        act.wait_ge(s_cvd, 5 * (ct - 1))
                        act.wait_ge(s_ncv, 2 * (ct - 1))
                    row = ext[:, ct % 2, :]
                    act.activation(row[:, 3:S0], src[:, 0:NP_], ACT.Copy)
                    act.activation(row[:, S0:EXTW].rearrange("p (s t) -> p s t", t=SW)[:, :, 3:SW], seqs(src),
                                   ACT.Copy).then_inc(s_ev, 1)
                elif g < 64:
                    if g == 48:
                        act.wait_ge(s_kdm, 8)
                        act.wait_ge(s_o, GH)
                        act.wait_ge(s_gpf, GH)
                        act.wait_ge(s_oss, GH)
                    act.activation(zF[:, g - 48, :], src, ACT.Copy).then_inc(s_ev, 1)
                elif g < 72:
                    if g == 64:
                        act.wait_ge(s_onv, 14)
                    act.activation(rF[:, g - 64, :], src, ACT.Copy).then_inc(s_ev, 1)
                else:
                    t = g - 72
                    act.activation(gbF[:, t, :], src, ACT.Sigmoid,
                                   bias=vec[:, V_MRG + 8 + t:V_MRG + 9 + t]).then_inc(s_ev, 1)

            evac(0)
            act.wait_ge(s_gxv, 4)
            act.activation(gax, gx, ACT.Abs).then_inc(s_gxa, 1)
            act.wait_ge(s_gxa, 1)
            act.activation(gax, gax, ACT.Exp, scale=-1.0).then_inc(s_gxa, 1)
            act.wait_ge(s_gxa, 2)
            act.activation(gax, gax, ACT.Ln, bias=1.0).then_inc(s_gxa, 1)
            for g in range(1, 16):
                evac(g)

            for s in range(N2):
                for j in (2 * s, 2 * s + 1):
                    if j < NL * GH and j % NL:
                        hd, lv, size, n = level_of(j)
                        act.wait_ge(s_ge, 8 * hd + lv)
                        act.activation(ebuf[:, j % 2, 0:n], ebuf[:, j % 2, 0:n], ACT.Exp,
                                       scale=1.0 / TAU).then_inc(s_gexp, 1)
                if s in F_SLOT:
                    hd = F_SLOT.index(s)
                    act.wait_ge(s_kde, hd + 1)
                    act.activation(ekd, ekd, ACT.Exp, scale=1.0 / TAU).then_inc(s_kdx, 1)
                    if hd:
                        act.wait_ge(s_kdm, 2 * hd)
                        act.wait_ge(s_gsa, 8 * hd)
                    act.activation(eg, gF[:, hd, NP_:T], ACT.Exp, scale=1.0 / TAU).then_inc(s_kdx, 1)
                evac(16 + s)
                if s % 2:
                    ada_copy(8 + s // 2, b[5])
                for hd in range(GH):
                    if s == F_SLOT[hd] + 2:
                        act.wait_ge(s_o, hd + 1)
                        for v in range(2):
                            act.activation(oF[:, 2 * hd + v, :], b[2 + v][:, 0:T], ACT.Copy).then_inc(s_oc, 1)
                    if s == F_SLOT[hd] + 4:
                        act.wait_ge(s_gpf, hd + 1)
                        if hd:
                            act.wait_ge(s_pst, 16 * hd)
                        act.activation(gfin, b[4][:, 0:GDV], ACT.Copy).then_inc(s_gpfc, 1)
                if s >= 12 and s % 4 == 0:
                    m = (s - 12) // 4
                    act.wait_ge(s_cvd, 5 * (4 * m + 4))
                    x_ = (bcF[:, 4 * m:4 * m + 4, :] if m < 2 else xsF[:, 4 * m - 8:4 * m - 4, :])
                    act.activation(x_, x_, ACT.Silu).then_inc(s_slu, 1)
                if s == 21:
                    act.wait_ge(s_dtv, 2)
                    act.activation(dta, dtx, ACT.Abs).then_inc(s_dta, 1)
                    act.wait_ge(s_dta, 2)
                    act.activation(dta, dta, ACT.Exp, scale=-1.0).then_inc(s_dta, 1)
                    act.wait_ge(s_dta, 3)
                    act.activation(dta, dta, ACT.Ln, bias=1.0).then_inc(s_dta, 1)
                if s == 23:
                    act.activation(rF[:, :, :], rF[:, :, :], ACT.Silu).then_inc(s_sil, 1)
                    act.wait_ge(s_cs, 1)
                    act.wait_ge(s_dtv, 6)
                    act.activation(wdec[:, 0:3, :], b[1][:, 96:192].rearrange("p (a b) -> p a b", a=3),
                                   ACT.Exp).then_inc(s_csa, 1)
                    act.activation(wdec[0:NSAMP, 3, :], b[1][0:NSAMP, 192:224], ACT.Exp).then_inc(s_csa, 1)
                    act.activation(EB, b[1][:, 224:480].rearrange("p (a b) -> p a b", a=NS),
                                   ACT.Exp).then_inc(s_csa, 1)
                    act.activation(csF[0:HEADS, :], b[2][0:HEADS, 0:T], ACT.Copy).then_inc(s_csa, 1)
                if 25 <= s < 28:
                    t = s - 25
                    rows = TT[t][2]
                    act.wait_ge(s_btr, t + 1)
                    act.activation(bT[0:rows, t, :], b[0][0:rows, :], ACT.Copy).then_inc(s_btc, 1)
                if s == 28:
                    act.wait_ge(s_onv, 4)
                    act.activation(rsg, rsg, ACT.Sqrt).then_inc(s_osd, 1)
            act.wait_ge(s_cvd, 5 * NCONV)
            act.activation(xsF[:, 12:16, :], xsF[:, 12:16, :], ACT.Silu).then_inc(s_slu, 1)

            for q in range(PAIRS):
                if q:
                    act.wait_ge(s_yv, 3 * q - 1)
                else:
                    act.wait_ge(s_ncv, 2 * NCONV)
                if q:
                    act.wait_ge(s_y, q)
                for j in range(2):
                    act.wait_ge(s_L, 3 * (2 * q + j + 1))
                    act.activation(M[:, j, :], L[:, j, :], ACT.Exp).then_inc(s_Lx, 1)
                    act.activation(eb[64 * j:64 * j + 64, :], b[1 + j][64 * j:64 * j + 64, P:T], ACT.Exp).then_inc(s_ebc, 1)
                before, afterwards = p3_tiles(q)
                for t in before:
                    evac(48 + t)
                act.wait_ge(s_pf, q + 1)
                if q >= 2:
                    act.wait_ge(s_pf_out[q % 2], 16 * (q // 2))
                act.activation(fin2[:, q % 2, :], b[2][:, T:T + P], ACT.Copy).then_inc(s_pfc, 1)
                for t in afterwards:
                    evac(48 + t)

            for g in range(GROUPS):
                act.activation(zF[:, 4 * g:4 * g + 4, :], zF[:, 4 * g:4 * g + 4, :], ACT.Silu).then_inc(s_sil, 1)
            act.wait_ge(s_y, PAIRS)
            act.wait_ge(s_sm, PAIRS)
            for i in range(2):
                act.wait_ge(s_sout[i], 16 * (PAIRS // 2))
            for t in range(8):
                evac(72 + t)
                if t < GROUPS:
                    act.wait_ge(s_ysm, t + 1)
                    act.activation(zF[:, 4 * t:4 * t + 4, :], xsF[:, 4 * t:4 * t + 4, :], ACT.Square).then_inc(s_ysq, 1)
            act.wait_ge(s_ynv, 4)
            act.activation(rs4, rs4, ACT.Sqrt).then_inc(s_ysd, 1)
            for t in range(8):
                act.activation(rF[:, t, :], rF[:, t, :], ACT.Sigmoid,
                               bias=vec[:, V_MRG + t:V_MRG + 1 + t]).then_inc(s_sil, 1)
            for t in range(KT):
                act.wait_ge(s_mxv, 24 + 3 * t + 3)
                act.activation(hF[:, t, :], x2[:, t, :], ACT.Square).then_inc(s_sq, 1)
            root(2)
            shift(2, 24)

            act.wait_ge(s_rtp, 1)
            act.wait_ge(s_set, 5)
            act.activation(scr[:, 0:2, :], b[1][:, 0:2 * E].rearrange("p (a b) -> p a b", a=2),
                           ACT.Sigmoid).then_inc(s_rta, 1)
            act.activation(scr[0:NSAMP, 2, :], b[1][0:NSAMP, 2 * E:3 * E], ACT.Sigmoid).then_inc(s_rta, 1)
            for n in range(6):
                t, half = divmod(n, 2)
                rows = TT[t][2]
                act.wait_ge(s_ht, n + 1)
                act.activation(hT[0:rows, t, half * 512:half * 512 + 512], b[2 + n % 4][0:rows, :],
                               ACT.Copy).then_inc(s_htc, 1)

            for n in range(12):
                t, half = divmod(n, 2)
                act.wait_ge(s_tm, n + 1)
                rows = TT[t][2] if n < 6 else NSAMP if n >= 10 else P
                dst = xT[:, t] if n < 6 else wT if n < 8 else gT[:, t - 4]
                act.activation(dst[0:rows, half * 512:half * 512 + 512], (b[4], b[5], pj[0], pj[1])[n % 4][0:rows, :],
                               ACT.Copy).then_inc(s_tmc, 1)

            with act.If(few(act)):
                def first_half(e, v):
                    act.wait_ge(s_xt2, e + 1)
                    act.activation(heF[:, v, 0:4, :], b[0][:, 0:4 * CAP].rearrange("p (k c) -> p k c", k=4),
                                   ACT.Copy).then_inc(s_hea, 1)

                first_half(0, 0)

                def two(i, first, last):
                    for v in range(2):
                        e = 2 * i + v
                        act.wait_ge(s_used, 6 * e + (C_MOE + 2))
                        if not first:
                            act.wait_ge(s_eac, e - 1)
                        act.activation(sgE[:, v, :], b[2 + v][:, 0:4 * CAP], ACT.Silu).then_inc(s_esg, 1)
                        if not (last and v):
                            first_half(e + 1, 1 - v)
                        act.wait_ge(s_used, 6 * e + (C_MOE + 5))
                        if not first:
                            act.wait_ge(s_yd[v], 16 * i)
                        act.activation(yE[0:CAP, v, 0:512], pj[0][0:CAP, :], ACT.Copy).then_inc(s_eya, 1)

                expert_pairs(act, two)
                for t, (c0, c1, rows) in enumerate(TT):
                    act.wait_ge(s_y12[t], 32)
                    act.activation(hT[0:rows, t, :], hT[0:rows, t, :], ACT.Copy,
                                   scale=sel[0:rows, 0, 6 + t:7 + t]).then_inc(s_w1, 1)
            with act.Else():
                act.wait_ge(s_ctr, 1)
                act.activation(combF[0:E, :], b[2][0:E, 0:T], ACT.Copy).then_inc(s_ctc, 1)
                for e in range(E):
                    act.wait_ge(s_cbb, e + 1)
                    act.activation(combB[:, e, :], b[4 + e % 2][:, 0:T], ACT.Copy).then_inc(s_cbx, 1)

                def two(i, first, last):
                    for v in range(2):
                        e = 2 * i + v
                        for f in range(4):
                            if f % 2:
                                act.wait_ge(s_used, 6 * e + (C_MOE + f // 2 + 1))
                            else:
                                act.wait_ge(s_first, 4 * e + (C_MOE + f // 2 + 1))
                            if not (first and v == 0):
                                act.wait_ge(s_au, 4 * e + (f - 3))
                            act.activation(sgt[:, f, :], b[f % 2][:, 0:T], ACT.Silu).then_inc(s_sg, 1)

                expert_pairs(act, two)
                for n in range(6):
                    t, half = divmod(n, 2)
                    rows = TT[t][2]
                    act.wait_ge(s_yt, n + 1)
                    act.activation(hT[0:rows, t, half * 512:half * 512 + 512], b[n % 2][0:rows, :],
                                   ACT.Copy).then_inc(s_ytc, 1)
            for t, (c0, c1, rows) in enumerate(TT):
                act.wait_ge(s_x3, t + 1)
                act.activation(y2[0:rows, t, :], hT[0:rows, t, :], ACT.Square,
                               accum_out=ssq[0:rows, t:t + 1]).then_inc(s_fsq, 1)
                act.wait_ge(s_fsq, t + 1)
                act.activation(ssq[0:rows, t:t + 1], ssq[0:rows, t:t + 1], ACT.Sqrt, bias=eps[0:rows, :],
                               scale=1.0 / D).then_inc(s_fsd, 1)

        @block.gpsimd
        def _(pool):
            pool.dma_start(d["xd"][XROWS:XROWS + CAP, :], d["w"][0][0:CAP // 2].rearrange("p (a c) -> (p a) c", a=2)
                           ).then_inc(s_pad, 16)
            pool.wait_ge(s_ld1, 16 * 9)
            pool.wait_ge(s_ld0, 16 * 3)
            for s in range(N2 + 1):
                for j in (2 * s, 2 * s + 1):
                    if j < NL * GH and j % NL:
                        hd, lv, size, n = level_of(j)
                        el, eu, _ = halves(ebuf[:, j % 2, :], n, size)
                        ol, ou, _ = halves(qk[:, j % 2, :], n, size)
                        kl, _, _ = halves(kF[:, hd, :], n, size)
                        _, qu, _ = halves(qF[:, hd, :], n, size)
                        pool.wait_ge(s_gexp, 8 * hd + lv)
                        pool.wait_ge(s_ev, 16)
                        if j >= 2:
                            pool.wait_ge(s_gp, j - 1)
                        pool.tensor_tensor(ol, kl, el, ALU.mult)
                        pool.tensor_tensor(ou, qu, eu, ALU.mult).then_inc(s_gqk, 1)
                if s in F_SLOT:
                    hd = F_SLOT.index(s)
                    if hd:
                        pool.wait_ge(s_kdt, hd)
                        pool.wait_ge(s_o, hd)
                    pool.wait_ge(s_kdx, 2 * hd + 1)
                    pool.tensor_tensor(kd, kF[:, hd, :], ekd, ALU.mult).then_inc(s_kdm, 1)
                    pool.wait_ge(s_kdx, 2 * hd + 2)
                    pool.tensor_tensor(qg, qF[:, hd, NP_:T], eg, ALU.mult).then_inc(s_kdm, 1)
                ct = s - 8
                if 0 <= ct < NCONV:
                    c = chan(ct)
                    if ct >= 2:
                        pool.wait_ge(s_cvd, 5 * (ct - 1))
                    row = ext[:, ct % 2, S0:EXTW].rearrange("p (s t) -> p s t", t=SW)
                    pool.tensor_copy(row[:, :, 0:3], cvs[:, c, :].rearrange("p (s t) -> p s t", t=3)).then_inc(s_pre_x, 1)
                ct = s - 9
                if 0 <= ct < NCONV:
                    c = chan(ct)
                    pool.wait_ge(s_ev, 16 + s)
                    row = ext[:, ct % 2, :]
                    pool.tensor_copy(ncv[:, c, 0:3], row[:, S0 - 3:S0]).then_inc(s_ncv, 1)
                    pool.tensor_copy(ncv[:, c, 3:27].rearrange("p (s t) -> p s t", t=3),
                                     row[:, S0:EXTW].rearrange("p (s t) -> p s t", t=SW)[:, :, SW - 3:SW]).then_inc(s_ncv, 1)
                if s == 22:
                    pool.wait_ge(s_dtv, 4)
                    pool.tensor_tensor(dtm[0:NSAMP], dta[0:NSAMP, 2:3, :].to_broadcast([NSAMP, NS, HEADS]),
                                       seqm.unsqueeze(2).to_broadcast([NSAMP, NS, HEADS]), ALU.mult).then_inc(s_dtm, 1)
            for q in range(PAIRS):
                g = q // PPG
                if q % PPG == 0:
                    if q:
                        pool.wait_ge(s_sn, 2 * q)
                    else:
                        pool.wait_ge(s_btc, 3)
                        pool.wait_ge(s_gs, 4 * GH)
                        pool.wait_ge(s_o, GH)
                        for i in range(2):
                            pool.wait_ge(s_sgo[i], 16 * 8)
                        pool.wait_ge(s_pst, 16 * GH)
                        pool.wait_ge(s_cvd, 5 * NCONV)
                        pool.wait_ge(s_kdc, 2 * GH)
                        pool.wait_ge(s_gsa, 8 * GH)
                        pool.wait_ge(s_csa, 4)
                    pool.tensor_tensor(bm[0:NSAMP], bT[0:NSAMP, 2:3, g * P:g * P + P].to_broadcast([NSAMP, NS, P]),
                                       seqm.unsqueeze(2).to_broadcast([NSAMP, NS, P]), ALU.mult).then_inc(s_bm, 1)
                x_ = xdt[:, q % 2]
                o_ = xdd[:, q % 2]
                hs = slice(2 * q, 2 * q + 2)

                def byhead(a):
                    return a.rearrange("p a (h c) -> p a h c", h=2)

                pool.wait_ge(s_xdt, 2 * q + 2)
                if q >= 2:
                    pool.wait_ge(s_sn, 2 * (q - 1))
                pool.tensor_tensor(byhead(o_[:, 0:2]), byhead(x_[:, 0:2]),
                                   wdec[:, 0:2, hs].unsqueeze(3).to_broadcast([P, 2, 2, HD]), ALU.mult).then_inc(s_xdd, 1)
                pool.tensor_tensor(byhead(o_[:, 2:3]), byhead(x_[:, 0:1]),
                                   wdec[:, 2:3, hs].unsqueeze(3).to_broadcast([P, 1, 2, HD]), ALU.mult).then_inc(s_xdd, 1)
                pool.tensor_tensor(byhead(o_[0:NSAMP, 3:4]), byhead(x_[0:NSAMP, 2:3]),
                                   wdec[0:NSAMP, 3:4, hs].unsqueeze(3).to_broadcast([NSAMP, 1, 2, HD]),
                                   ALU.mult).then_inc(s_xdd, 1)
                pool.wait_ge(s_sin[q % 2], 16 * (q // 2 + 1))
                if q >= 2:
                    pool.wait_ge(s_sout[q % 2], 16 * (q // 2))
                pool.tensor_tensor(byhead(so[:, q % 2]), byhead(sn[:, q % 2]),
                                   EB[:, :, hs].unsqueeze(3).to_broadcast([P, NS, 2, HD]), ALU.mult).then_inc(s_sm, 1)
            pool.wait_ge(s_dsp, DISPATCH_STEPS)
            pool.wait_ge(s_htc, 6)
            for t, (c0, c1, rows) in enumerate(TT):
                for j in range(TOP):
                    pool.indirect_dma_start(out=d["xd"][:, :],
                                            out_offset=bass.IndirectOffsetOnAxis(ap=idx[0:rows, j, t:t + 1], axis=0),
                                            in_=hT[0:rows, t, :], in_offset=None).then_inc(s_xd, 16)

            with pool.If(few(pool)):
                for v in range(2):
                    pool.wait_ge(s_yd[v], 16 * (E // 2))
                pool.wait_ge(s_xd, 16 * 6)
                for t, (c0, c1, rows) in enumerate(TT):
                    for j, dst in enumerate((hT, y2)):
                        pool.indirect_dma_start(out=dst[0:rows, t, :], out_offset=None,
                                                in_=d["yd"].rearrange("e r c -> (e r) c"),
                                                in_offset=bass.IndirectOffsetOnAxis(ap=idx[0:rows, j, 3 + t:4 + t], axis=0)
                                                ).then_inc(s_y12[t], 16)
            with pool.Else():
                pool.wait_ge(s_cbx, E)
                for e in range(E):
                    for f in range(4):
                        pool.wait_ge(s_au, 4 * e + f + 1)
                        pool.tensor_tensor(actF[:, e % 2, f, :], actF[:, e % 2, f, :], combB[:, e, :],
                                           ALU.mult).then_inc(s_ac, 1)

        def masked_cb(dve, g):
            dve.wait_ge(s_cb, g + 1)
            o_ = cbm[:, g % 2, :]
            if g == 0:
                for i in range(2):
                    dve.memset(cbm[64:P, i, NP_:T], 0.0)
            dve.tensor_tensor(o_[:, 0:NP_], b[3][:, 0:NP_], cmask[:, 0:NP_], ALU.mult).then_inc(s_cbc, 1)
            dve.tensor_tensor(o_[0:NSAMP, NP_:T], b[3][0:NSAMP, NP_:T], cmask[0:NSAMP, NP_:T], ALU.mult).then_inc(s_cbc, 1)
            dve.tensor_copy(o_[:, T:T + P], b[3][:, T:T + P]).then_inc(s_cbc, 1)

        @block.vector
        def _(dve):
            nv = Chain(dve, s_nv)
            st = Chain(dve, s_set)
            st(dve.memset(dtx, 0.0))
            for i in range(2):
                st(dve.memset(ext[:, i, 0:3], 0.0))

            def norm(n, src=None):
                if src is not None:
                    dve.tensor_tensor(hF[:, :, :], src, src, ALU.mult).then_inc(s_nsq, 1)
                dve.wait_ge(s_nsd, n)
                nv(dve.reciprocal(rst[:, :], rst[:, :]))
                nv.wait()

            def scales(base, w):
                nv(dve.scalar_tensor_tensor(modA[:, :, :], mod[:, base:base + 8, :], 1.0,
                                            vec[:, w:w + 8].unsqueeze(2).to_broadcast([P, KT, NSEQ]), ALU.add, ALU.mult))
                nv.wait()

            def modulate(src, shift):
                for k in range(KT):
                    dve.scalar_tensor_tensor(hF[:, k, 0:NP_], src[:, k, 0:NP_], modA[:, k, 0:1], rst[:, 0:NP_],
                                             ALU.mult, ALU.mult).then_inc(s_hk, 1)
                hs = hF[:, :, NP_:T].rearrange("p k (s t) -> p k s t", t=ST)
                nv(dve.tensor_tensor(hF[:, :, NP_:T], src[:, :, NP_:T],
                                     rst[:, NP_:T].unsqueeze(1).to_broadcast([P, KT, NSAMP]), ALU.mult))
                nv.wait()
                nv(dve.tensor_tensor(hs, hs, modA[:, :, 1:].unsqueeze(3).to_broadcast([P, KT, NS, ST]), ALU.mult))
                nv.wait()
                dve.tensor_tensor(hs, hs, mod[:, shift:shift + 8, 1:].unsqueeze(3).to_broadcast([P, KT, NS, ST]),
                                  ALU.add).then_inc(s_h, 1)

            dve.wait_ge(s_ld0, 16 * 3)
            norm(1, oF[:, :, :])
            dve.wait_ge(s_adt, 8)
            dve.tensor_tensor(mod[:, 0:16, :], b[5][:, 0:16 * NSEQ].rearrange("p (a b) -> p a b", b=NSEQ),
                              vec[:, 0:16].unsqueeze(2).to_broadcast([P, 16, NSEQ]), ALU.add).then_inc(s_mod, 1)
            dve.wait_ge(s_mod, 1)
            scales(8, V_N1)
            modulate(oF, 0)

            for hd in range(GH):
                dve.wait_ge(s_gate, hd + 1)
                dve.tensor_scalar(gx[:, hd, :], b[2 + hd % 2][:, 0:T], vec[:, V_GB + hd:V_GB + hd + 1], None,
                                  ALU.add).then_inc(s_gxv, 1)
            dve.wait_ge(s_gxv, 4)
            dve.wait_ge(s_gxa, 3)
            dve.scalar_tensor_tensor(gx, gx, 0.0, gax, ALU.min, ALU.subtract).then_inc(s_gxv, 1)
            dve.wait_ge(s_gxv, 5)
            for hd in range(GH):
                dve.tensor_tensor_scan(gF[:, hd, :], reset, gx[:, hd, :], 0.0, ALU.mult, ALU.add).then_inc(s_gxv, 1)
            for v in range(8):
                dve.wait_ge(s_vtr, v + 1)
                dve.tensor_copy(vT[:, 0:2, v * P:v * P + P],
                                b[4][:, 0:2 * P].rearrange("p (a b) -> p a b", a=2)).then_inc(s_vcp, 1)
                dve.tensor_copy(vT[0:NSAMP, 2, v * P:v * P + P], b[4][0:NSAMP, 2 * P:3 * P]).then_inc(s_vcp, 1)
            dve.wait_ge(s_gxv, 9)

            def exponents(j):
                hd, lv, size, n = level_of(j)
                if not lv:
                    return
                if j >= 2 and 8 * hd + lv > 2:
                    dve.wait_ge(s_gqk, len([i for i in range(j - 1) if i % NL]))
                lo, up, v = halves(gF[:, hd, :], n, size)
                el, eu, _ = halves(ebuf[:, j % 2, :], n, size)
                mid = v[:, :, size // 2 - 1:size // 2].to_broadcast([P, n // size, size // 2])
                dve.tensor_tensor(eu, up, mid, ALU.subtract)
                dve.tensor_tensor(el, mid, lo, ALU.subtract).then_inc(s_ge, 1)

            def merge(j):
                hd, lv, size, n = level_of(j)
                a = att[:, hd % 2, :]
                bank = b[j % 2]
                dve.wait_ge(s_gp, j + 1)
                if lv == 0:
                    if hd >= 2:
                        dve.wait_ge(s_o, hd - 1)
                    dve.tensor_tensor(a[:, 0:NP_], bank[:, 0:NP_], dmask[:, 0:NP_], ALU.mult)
                    dve.tensor_tensor(a[0:NSAMP, NP_:T], bank[0:NSAMP, NP_:T], dmask[0:NSAMP, NP_:T],
                                      ALU.mult).then_inc(s_gcp, 1)
                    return
                dve.wait_ge(s_gcp, j)
                if size == 256:
                    dve.tensor_copy(a[:, T:T + P], bank[:, 0:P]).then_inc(s_gcp, 1)
                    return
                m = lvm[:, MASKED.index(size), :]
                ins = dve.copy_predicated(a[:, 0:NP_], m[:, 0:NP_], bank[:, 0:NP_])
                if size <= ST:
                    ins = dve.copy_predicated(a[0:NSAMP, NP_:T], m[0:NSAMP, NP_:T], bank[0:NSAMP, NP_:T])
                ins.then_inc(s_gcp, 1)

            def new_states(hd, bp):
                dve.wait_ge(s_gs, 4 * hd + bp + 1)
                dve.wait_ge(s_sgi, 16 * (hd + 1))
                dve.wait_ge(s_kdx, 2 * hd + 2)
                n = 2 * hd + bp // 2
                if n:
                    dve.wait_ge(s_sgo[bp % 2], 16 * n)
                for j in range(2):
                    s = 2 * bp + j
                    dve.scalar_tensor_tensor(sgo[:, bp % 2, j, :], sgi[:, s, :], eg[:, ST * s + ST - 1:ST * s + ST],
                                             b[4][:, j * GDV:(j + 1) * GDV], ALU.mult, ALU.add).then_inc(s_gsa, 1)

            def conv(ct):
                c = chan(ct)
                row = ext[:, ct % 2, :]
                dst = bcF[:, ct, :] if ct < 8 else xsF[:, ct - 8, :]
                w = [vec[:, V_CW + i * NCONV + c:V_CW + i * NCONV + c + 1] for i in range(CONVK)]
                n = EXTW - 3
                dve.wait_ge(s_ev, 25 + ct)
                dve.wait_ge(s_pre_x, ct + 1)
                cv = Chain(dve, s_cvd, 5 * ct)
                if ct == 0:
                    st.wait()
                else:
                    cv.wait()
                cv(dve.tensor_scalar(cvo[:, 0:n], row[:, 0:n], w[0], vec[:, V_CB + c:V_CB + c + 1],
                                     ALU.mult, ALU.add))
                for i in (1, 2):
                    cv.wait()
                    cv(dve.scalar_tensor_tensor(cvo[:, 0:n], row[:, i:i + n], w[i], cvo[:, 0:n], ALU.mult, ALU.add))
                cv.wait()
                cv(dve.scalar_tensor_tensor(dst[:, 0:NP_], row[:, 3:S0], w[3], cvo[:, 0:NP_], ALU.mult, ALU.add))
                cv(dve.scalar_tensor_tensor(
                    seqs(dst), row[:, S0:EXTW].rearrange("p (s t) -> p s t", t=SW)[:, :, 3:SW], w[3],
                    cvo[:, S0:S0 + NS * SW].rearrange("p (s t) -> p s t", t=SW)[:, :, 0:ST], ALU.mult, ALU.add))

            on = Chain(dve, s_onv)
            for s in range(N2 + 1):
                for j in (2 * s - 2, 2 * s - 1):
                    if 0 <= j < NL * GH:
                        merge(j)
                for hd in range(GH):
                    if s == F_SLOT[hd] + 3:
                        new_states(hd, 1)
                        new_states(hd, 2)
                    if s == F_SLOT[hd] + 4:
                        new_states(hd, 3)
                for j in (2 * s, 2 * s + 1):
                    if j < NL * GH:
                        exponents(j)
                if s in F_SLOT:
                    hd = F_SLOT.index(s)
                    g_ = gF[:, hd, :]
                    if hd:
                        dve.wait_ge(s_kdm, 2 * hd)
                    dve.tensor_scalar(ekd[:, 0:NP_], g_[:, 0:NP_], g_[:, NP_ - 1:NP_], -1.0, ALU.subtract, ALU.mult)
                    dve.tensor_tensor(seqs(ekd), seqs(g_)[:, :, ST - 1:ST].to_broadcast([P, NS, ST]), seqs(g_),
                                      ALU.subtract).then_inc(s_kde, 1)
                for hd in range(GH):
                    if s == F_SLOT[hd] + 1:
                        dve.wait_ge(s_kdt, hd + 1)
                        if hd:
                            dve.wait_ge(s_gs, 4 * hd)
                            dve.wait_ge(s_gpf, hd)
                        dve.tensor_copy(kdT, b[4][:, 0:2 * P].rearrange("p (a b) -> p a b", a=2)).then_inc(s_kdc, 1)
                        dve.tensor_tensor(kdm[0:NSAMP], b[4][0:NSAMP, 2 * P:3 * P].unsqueeze(1).to_broadcast([NSAMP, NS, P]),
                                          seqm.unsqueeze(2).to_broadcast([NSAMP, NS, P]), ALU.mult).then_inc(s_kdc, 1)
                    if s == F_SLOT[hd] + 2:
                        new_states(hd, 0)
                if 0 <= s - 9 < NCONV:
                    conv(s - 9)
                if s == 21:
                    dve.wait_ge(s_dtp, 1)
                    dve.tensor_tensor(dtx[:, 0:2, :], b[0][:, 0:64].rearrange("p (a b) -> p a b", a=2),
                                      dtb[:, :].unsqueeze(1).to_broadcast([P, 2, HEADS]), ALU.add).then_inc(s_dtv, 1)
                    dve.tensor_tensor(dtx[0:NSAMP, 2, :], b[0][0:NSAMP, 64:96], dtb[0:NSAMP, :], ALU.add).then_inc(s_dtv, 1)
                if s == 22:
                    dve.wait_ge(s_dtv, 2)
                    dve.wait_ge(s_dta, 4)
                    dve.scalar_tensor_tensor(dtx, dtx, 0.0, dta, ALU.max, ALU.add).then_inc(s_dtv, 1)
                    dve.wait_ge(s_dtv, 3)
                    dve.scalar_tensor_tensor(dta, dtx, -1.0, aex[:, :].unsqueeze(1).to_broadcast([P, 3, HEADS]),
                                             ALU.mult, ALU.mult).then_inc(s_dtv, 1)
                if s == 23:
                    dve.wait_ge(s_cs, 1)
                    dve.tensor_copy(csT[:, 0:2, :], b[1][:, 0:64].rearrange("p (a b) -> p a b", a=2)).then_inc(s_dtv, 1)
                    dve.tensor_copy(csT[0:NSAMP, 2, :], b[1][0:NSAMP, 64:96]).then_inc(s_dtv, 1)
                if s == 24:
                    dve.wait_ge(s_oc, 2 * GH)
                    dve.wait_ge(s_kdm, 2 * GH)
                    dve.tensor_tensor(osq, oF[:, :, :], oF[:, :, :], ALU.mult).then_inc(s_osq, 1)
                    dve.wait_ge(s_gpf, GH)
                    dve.wait_ge(s_gs, 4 * GH)
                    for i in range(2):
                        st(dve.memset(L[64:P, i, NP_:T], 0.0)) if i == 0 else dve.memset(L[64:P, i, NP_:T], 0.0)
                if s in (26, 27):
                    for j in range(2):
                        hd = 2 * (s - 26) + j
                        dve.wait_ge(s_oss, hd + 1)
                        if hd == 0:
                            dve.wait_ge(s_kdx, 2 * GH)
                        on(dve.tensor_scalar(rsg[:, hd, :], b[1 + j][:, 0:T], 1.0 / GDV, EPS, ALU.mult, ALU.add))
                if s == 28:
                    masked_cb(dve, 0)
                if s == 29:
                    dve.wait_ge(s_osd, 1)
                    on(dve.reciprocal(rsg, rsg))
                if s in (30, 31):
                    on.wait()
                    for hd in (2 * s - 60, 2 * s - 59):
                        for v in range(2):
                            o_ = oF[:, 2 * hd + v, :]
                            on(dve.scalar_tensor_tensor(o_, o_, vec[:, V_GN + v:V_GN + v + 1], rsg[:, hd, :],
                                                        ALU.mult, ALU.mult))
                if s == 32:
                    on.wait()
                    dve.wait_ge(s_sil, 1)
                    on(dve.tensor_tensor(oF[:, :, :], oF[:, :, :], rF[:, :, :], ALU.mult))
                if s and s % 2 == 0:
                    c = 7 + s // 2
                    dve.wait_ge(s_adt, c + 1)
                    dve.tensor_tensor(mod[:, 2 * c:2 * c + 2, :], b[5][:, 256:256 + 2 * NSEQ].rearrange("p (a b) -> p a b", b=NSEQ),
                                      vec[:, 2 * c:2 * c + 2].unsqueeze(2).to_broadcast([P, 2, NSEQ]),
                                      ALU.add).then_inc(s_mod, 1)
            for q in range(PAIRS):
                g = q // PPG
                x_ = xdt[:, q % 2]
                hs = slice(2 * q, 2 * q + 2)
                dve.wait_ge(s_xt, q + 1)
                if q >= 2:
                    dve.wait_ge(s_y, q - 1)
                    dve.wait_ge(s_xdd, 3 * (q - 1))
                elif q == 0:
                    dve.wait_ge(s_ncv, 2 * NCONV)
                    dve.wait_ge(s_pst, 16 * GH)
                dve.tensor_tensor(x_[:, 0:2].rearrange("p a (h c) -> p a h c", h=2),
                                  b[0][:, 0:2 * P].rearrange("p (a h c) -> p a h c", a=2, h=2),
                                  dtx[:, 0:2, hs].unsqueeze(3).to_broadcast([P, 2, 2, HD]), ALU.mult).then_inc(s_xdt, 1)
                dve.tensor_tensor(x_[0:NSAMP, 2].rearrange("p (h c) -> p h c", h=2),
                                  b[0][0:NSAMP, 2 * P:3 * P].rearrange("p (h c) -> p h c", h=2),
                                  dtx[0:NSAMP, 2, hs].unsqueeze(2).to_broadcast([NSAMP, 2, HD]), ALU.mult).then_inc(s_xdt, 1)
                for j in range(2):
                    h = 2 * q + j
                    dve.wait_ge(s_csb, h + 1)
                    if q:
                        dve.wait_ge(s_Lx, h - 1)
                    for t, (c0, c1, rows) in enumerate(TT):
                        dve.tensor_scalar(L[0:rows, j, c0:c1], b[1 + j][0:rows, c0:c1], csT[0:rows, t, h:h + 1], 0.0,
                                          ALU.subtract, ALU.min).then_inc(s_L, 1)
                for j in range(2):
                    h = 2 * q + j
                    dve.wait_ge(s_Lx, h + 1)
                    dve.wait_ge(s_cbc, 3 * g + 3)
                    dve.tensor_tensor(M[:, j, :], M[:, j, :], cbm[:, g % 2, 0:T], ALU.mult).then_inc(s_M, 1)
                yv = Chain(dve, s_yv, 3 * q)
                dve.wait_ge(s_y, q + 1)
                dve.wait_ge(s_ebc, 2 * q + 2)
                if q:
                    yv.wait()
                yv(dve.scalar_tensor_tensor(xsF[:, q, :], xsF[:, q, :], vec[:, V_DS + q:V_DS + q + 1], b[4][:, 0:T],
                                            ALU.mult, ALU.add))
                yv(dve.tensor_tensor(t2, b[4][:, T:512], eb, ALU.mult))
                yv.wait()
                yv(dve.tensor_tensor(xsF[:, q, P:T], xsF[:, q, P:T], t2, ALU.add))
                dve.wait_ge(s_sm, q + 1)
                for half in range(2):
                    dve.wait_ge(s_sn, 2 * q + half + 1)
                    bank = b[5] if half == 0 else b[3]
                    o_ = so[:, q % 2, 4 * half:4 * half + 4]
                    dve.tensor_tensor(o_, o_, bank[:, :].rearrange("p (a b) -> p a b", a=4), ALU.add).then_inc(s_sa, 1)
                if q % PPG == PPG - 1 and g + 1 < GROUPS:
                    masked_cb(dve, g + 1)

            dve.wait_ge(s_yv, 3 * PAIRS)
            for g in range(GROUPS):
                dve.wait_ge(s_sil, 2 + g)
                y_ = xsF[:, 4 * g:4 * g + 4, :]
                dve.tensor_tensor(y_, y_, zF[:, 4 * g:4 * g + 4, :], ALU.mult).then_inc(s_ysm, 1)
            dve.wait_ge(s_ysm, GROUPS)
            yn = Chain(dve, s_ynv)
            for i in range(2):
                dve.wait_ge(s_sout[i], 16 * (PAIRS // 2))
            dve.wait_ge(s_ev, 80)
            mv = Chain(dve, s_mxv)
            for t in range(8):
                dve.wait_ge(s_used if t % 2 else s_first, C_GLA + t // 2 + 1)
                mv(dve.tensor_tensor(gbF[:, t, :], gbF[:, t, :], pj[t % 2][:, 0:T], ALU.mult))
                if t == 2:
                    for g in range(GROUPS):
                        dve.wait_ge(s_yss, g + 1)
                        yn(dve.tensor_scalar(rs4[:, g, :], b[g][:, 0:T], 1.0 / 512, EPS, ALU.mult, ALU.add))
                if t in (3, 4):
                    if t == 3:
                        dve.wait_ge(s_ysd, 1)
                    yn(dve.reciprocal(rs4[:, 2 * t - 6:2 * t - 4], rs4[:, 2 * t - 6:2 * t - 4]))
                if t in (5, 6, 7):
                    if t == 5:
                        yn.wait()
                    for u in ((0, 1, 2, 3, 4, 5), (6, 7, 8, 9, 10), (11, 12, 13, 14, 15))[t - 5]:
                        y_ = xsF[:, u, :]
                        yn(dve.scalar_tensor_tensor(y_, y_, vec[:, V_SSDN + u:V_SSDN + u + 1], rs4[:, u // 4, :],
                                                    ALU.mult, ALU.mult))
            for t in range(8):
                dve.wait_ge(s_used if t % 2 else s_first, C_SSD + 2 * (t // 2) + 2)
                dve.wait_ge(s_sil, 6 + t)
                mv(dve.tensor_tensor(rF[:, t, :], rF[:, t, :], pj[t % 2][:, 0:T], ALU.mult))
                mv.wait()
                mv(dve.tensor_tensor(gbF[:, t, :], gbF[:, t, :], rF[:, t, :], ALU.add))
            dve.wait_ge(s_x, 16)
            dve.wait_ge(s_mod, 17)
            scales(32, V_N2)
            dve.tensor_copy(gsx.rearrange("p k (s t) -> p k s t", t=ST),
                            mod[:, 40:48, 1:].unsqueeze(3).to_broadcast([P, KT, NS, ST])).then_inc(s_gsx, 1)

            def residual(src, base, t, chain, tmp):
                x_ = x2[:, t, :]
                chain(dve.scalar_tensor_tensor(x_[:, 0:NP_], src[:, 0:NP_], mod[:, base + t, 0:1], x_[:, 0:NP_],
                                               ALU.mult, ALU.add))
                chain(dve.tensor_tensor(seqs(tmp), seqs(src), mod[:, base + t, 1:].unsqueeze(2).to_broadcast([P, NS, ST]),
                                        ALU.mult))
                chain.wait()
                chain(dve.tensor_tensor(seqs(x_), seqs(x_), seqs(tmp), ALU.add))

            for t in range(8):
                dve.wait_ge(s_used if t % 2 else s_first, C_OUT + t // 2 + 1)
                residual(pj[t % 2], 16, t, mv, rs4[:, t % 2, :])
            mv.wait()
            st(dve.memset(scr, 0.5))
            norm(2)
            modulate(x2, 24)

            rt = Chain(dve, s_rtv)

            def step(ins):
                rt(ins)
                rt.wait()

            def first_largest(out, val, w, prio, tmp):
                step(dve.tensor_reduce(mx, val, AX.X, ALU.max))
                step(dve.tensor_tensor(tmp, val, mx.to_broadcast([P, 3, w]), ALU.is_equal))
                step(dve.tensor_tensor(tmp, tmp, prio.unsqueeze(1).to_broadcast([P, 3, w]), ALU.mult))
                step(dve.tensor_reduce(mx2, tmp, AX.X, ALU.max))
                step(dve.tensor_tensor(out, tmp, mx2.to_broadcast([P, 3, w]), ALU.is_equal))

            def flat(a):
                return a.rearrange("p a b -> p (a b)")

            bie = flat(bi).rearrange("p (a b) -> p a b", a=3)
            dve.wait_ge(s_rta, 2)
            st.wait()
            step(dve.tensor_tensor(bie, scr, rb[:, :].unsqueeze(1).to_broadcast([P, 3, E]), ALU.add))
            step(dve.tensor_tensor(pair[:, :, 0:3], bi[:, :, 0:3], bi[:, :, 1:4], ALU.add))
            step(dve.tensor_tensor(pair[:, :, 3:5], bi[:, :, 0:2], bi[:, :, 2:4], ALU.add))
            step(dve.tensor_tensor(pair[:, :, 5:6], bi[:, :, 0:1], bi[:, :, 3:4], ALU.add))
            step(dve.tensor_reduce(flat(gsc).unsqueeze(2), pair, AX.X, ALU.max))
            first_largest(gone, gsc, EG, prio4, geq)
            mb4 = flat(mb).rearrange("p (a b) -> p a b", a=12)
            step(dve.tensor_tensor(mb4, bi, flat(gone).unsqueeze(2).to_broadcast([P, 12, EPG]), ALU.mult))
            step(dve.tensor_scalar(gone, gone, 1.0, -NEG, ALU.subtract, ALU.mult))
            step(dve.tensor_tensor(mb4, mb4, flat(gone).unsqueeze(2).to_broadcast([P, 12, EPG]), ALU.add))
            first_largest(o1, mb, E, prio16, eq)
            step(dve.scalar_tensor_tensor(mb, o1, NEG, mb, ALU.mult, ALU.add))
            first_largest(o2, mb, E, prio16, eq)
            step(dve.tensor_tensor(os_, o1, o2, ALU.add))
            assert rt.n == ROUTER_OS, rt.n
            step(dve.tensor_tensor(mb, os_, scr, ALU.mult))
            step(dve.tensor_reduce(mx, mb, AX.X, ALU.add))
            step(dve.reciprocal(mx, mx))
            step(dve.tensor_tensor(comb.rearrange("p (a b) -> p a b", a=3), mb, mx.to_broadcast([P, 3, E]), ALU.mult))

            ds_ = Chain(dve, s_dsp)

            def dstep(ins):
                ds_(ins)
                ds_.wait()

            dve.wait_ge(s_rank, 1)
            ranks = b[1][:, 64:64 + 3 * E].rearrange("p (a b) -> p a b", a=3)
            dstep(dve.tensor_copy(cnt, b[1][:, 64 + 3 * E:64 + 4 * E]))
            dstep(dve.tensor_tensor_scan(cin, ones[:, 0:E], cnt, 0.0, ALU.mult, ALU.add))
            dstep(dve.tensor_tensor(mf[:, 0:E], cin, cnt, ALU.subtract))
            dstep(dve.tensor_reduce(mf[:, E:E + 1], cnt, AX.X, ALU.max))
            dstep(dve.tensor_copy(meta[:, :], mf))
            assert ds_.n == DISPATCH_META, ds_.n
            for n, first_row in ((0, mf[:, 0:E]), (1, yrow)):
                dstep(dve.tensor_tensor(pos[:, n].rearrange("p (a b) -> p a b", a=3), ranks,
                                        first_row.unsqueeze(1).to_broadcast([P, 3, E]), ALU.add))
            for j, o_ in enumerate((o1, o2)):
                dstep(dve.tensor_tensor(picks, pos, flat(o_).unsqueeze(1).to_broadcast([P, 3, 3 * E]), ALU.mult))
                dstep(dve.tensor_reduce(sel[:, j, :].unsqueeze(2),
                                        picks.rearrange("p a (b c) -> p (a b) c", b=3), AX.X, ALU.add))
            dstep(dve.tensor_scalar(sel[:, :, 0:6], sel[:, :, 0:6], -1.0, None, ALU.add))
            dstep(dve.tensor_copy(idx[:, :, :], sel[:, :, 0:6]))
            assert ds_.n == DISPATCH_STEPS, ds_.n

            cm = Chain(dve, s_cmb)

            def add_to_stream(t, rows):
                if cm.n:
                    cm.wait()
                y_ = hT[0:rows, t, :]
                cm(dve.tensor_tensor(y_, y_, gT[0:rows, t // 2, :], ALU.mult))
                cm.wait()
                dve.tensor_tensor(y_, y_, xT[0:rows, t, :], ALU.add).then_inc(s_x3, 1)

            with dve.If(few(dve)):
                def second_half(e, v):
                    dve.wait_ge(s_xt2, e + 1)
                    dve.tensor_copy(heF[:, v, 4:8, :], b[1][:, 0:4 * CAP].rearrange("p (k c) -> p k c", k=4)
                                    ).then_inc(s_hev, 1)

                second_half(0, 0)

                def two(i, first, last):
                    for v in range(2):
                        e = 2 * i + v
                        dve.wait_ge(s_used, 6 * e + (C_MOE + 4))
                        dve.wait_ge(s_esg, e + 1)
                        dve.tensor_tensor(actE[:, v, :], sgE[:, v, :], b[4 + v][:, 0:4 * CAP], ALU.mult).then_inc(s_eac, 1)
                        if not (last and v):
                            second_half(e + 1, 1 - v)
                        dve.wait_ge(s_used, 6 * e + (C_MOE + 6))
                        if not first:
                            dve.wait_ge(s_yd[v], 16 * i)
                        dve.tensor_copy(yE[0:CAP, v, 512:1024], pj[1][0:CAP, :]).then_inc(s_eyv, 1)

                expert_pairs(dve, two)
                for t, (c0, c1, rows) in enumerate(TT):
                    dve.wait_ge(s_w1, t + 1)
                    cm(dve.scalar_tensor_tensor(hT[0:rows, t, :], y2[0:rows, t, :], sel[0:rows, 1, 6 + t:7 + t],
                                                hT[0:rows, t, :], ALU.mult, ALU.add))
                    add_to_stream(t, rows)
            with dve.Else():
                def two(i, first, last):
                    for v in range(2):
                        e = 2 * i + v
                        for f in range(4):
                            if not first:
                                dve.wait_ge(s_used, 6 * e + (C_MOE - 6))
                            dve.wait_ge(s_sg, 4 * e + (f + 1))
                            if f % 2:
                                dve.wait_ge(s_used, 6 * e + (C_MOE + 3 + f // 2))
                            else:
                                dve.wait_ge(s_first, 4 * e + (C_MOE + 3 + f // 2))
                            dve.tensor_tensor(actF[:, v, f, :], sgt[:, f, :], b[2 + f % 2][:, 0:T],
                                              ALU.mult).then_inc(s_au, 1)
                        for t in range(8):
                            down_done(dve, e, t // 4, t % 4)
                            if first and v == 0:
                                dve.tensor_copy(yacc[:, t, :], pj[t % 2][:, 0:T]).then_inc(s_ya, 1)
                            else:
                                if t == 0:
                                    dve.wait_ge(s_ya, 8 * e)
                                dve.tensor_tensor(yacc[:, t, :], yacc[:, t, :], pj[t % 2][:, 0:T], ALU.add).then_inc(s_ya, 1)

                expert_pairs(dve, two)
                cm.n = 0
                for t, (c0, c1, rows) in enumerate(TT):
                    dve.wait_ge(s_ytc, 2 * t + 2)
                    add_to_stream(t, rows)
            for t, (c0, c1, rows) in enumerate(TT):
                dve.wait_ge(s_fsd, t + 1)
                dve.reciprocal(ssq[0:rows, t:t + 1], ssq[0:rows, t:t + 1]).then_inc(s_frc, 1)
                dve.wait_ge(s_frc, t + 1)
                y_ = hT[0:rows, t, :]
                dve.scalar_tensor_tensor(y_, y_, ssq[0:rows, t:t + 1], wT[0:rows, :], ALU.mult, ALU.mult).then_inc(s_f, 1)


def constants():
    c = np.zeros((P, NC), np.float32)
    i = np.arange(P)
    c[:, C_ID:C_ID + P] = np.eye(P)
    c[:, C_U:C_U + P] = i[:, None] <= i[None, :]
    c[:, C_R:C_R + P] = i[:, None] > i[None, :]
    c[:, C_ONE:C_ONE + P] = 1
    s = np.arange(NSAMP)
    same = (s[:, None] // ST) == (s[None, :] // ST)
    us = same & (s[:, None] <= s[None, :])
    c[:, C_CM:C_CM + P] = c[:, C_CM + P:C_CM + 2 * P] = c[:, C_U:C_U + P]
    c[:NSAMP, C_CM + 2 * P:C_CM + T] = us
    c[:, C_DM:C_DM + P] = c[:, C_DM + P:C_DM + 2 * P] = np.eye(P)
    c[:NSAMP, C_DM + 2 * P:C_DM + T] = np.eye(NSAMP)
    r = np.ones(T, np.float32)
    r[0] = 0
    r[NP_::ST] = 0
    c[:, C_RS:C_RS + T] = r
    c[:NSAMP, C_US:C_US + NSAMP] = us
    c[:NSAMP, C_RSS:C_RSS + NSAMP] = same & (s[:, None] > s[None, :])
    c[:NSAMP, C_SEQ:C_SEQ + NS] = (s[:, None] // ST) == np.arange(NS)[None, :]
    c[:, C_PR:C_PR + 16] = 16 - np.arange(16)
    c[:, C_PR + 16:C_PR + 20] = 4 - np.arange(4)
    c[:, C_YR:C_YR + E] = CAP * np.arange(E)
    c[:, C_EPS] = EPS
    m = np.zeros((P, len(MASKED), T), np.uint8)
    for n, size in enumerate(MASKED):
        blk = (i[:, None] // size == i[None, :] // size) & (i[:, None] % size < size // 2) & (i[None, :] % size >= size // 2)
        m[:, n, 0:P] = m[:, n, P:2 * P] = blk
        if size <= ST:
            m[:NSAMP, n, NP_:T] = blk[:NSAMP, :NSAMP]
    return c, m.reshape(P, -1).view(np.int32)


def kernel(**inputs):
    import concourse.bacc as _bacc
    from concourse.bass_utils import run_bass_kernel_spmd as _run

    a = {k: np.asarray(v) for k, v in inputs.items()}

    def cols(w):
        k, c = w.shape
        return w.reshape(k // P, P, c // 256, 256).transpose(2, 1, 0, 3).reshape(c // 256, P, -1)

    w_in, ada = a["w_in"][0], cols(a["w_ada"][0])
    gla, out = cols(a["w_gla_br"][0]), cols(a["w_out"][0])
    ssd = [cols(a["w_ssd_br"][0][h * D:(h + 1) * D]) for h in range(2)]
    w = np.empty((N_CHUNK, P, CH), np.float32)
    for n, c in enumerate(ORDER):
        if c[0] == "in":
            w[n] = cols(w_in[:, c[1]:c[1] + 256])[0]
        elif c[0] == "ada":
            w[n] = ada[c[1]]
        elif c[0] == "gla":
            w[n] = gla[c[1]]
        elif c[0] == "ssd":
            w[n] = ssd[c[2]][c[1]]
        elif c[0] == "out":
            w[n] = out[c[1]]
        elif c[0] == "gate":
            w[n] = cols(a["w_exp_gate"][0, c[1]][:, 256 * c[2]:256 * c[2] + 256])[0]
        elif c[0] == "up":
            w[n] = cols(a["w_exp_up"][0, c[1]][:, 256 * c[2]:256 * c[2] + 256])[0]
        else:
            w[n] = a["w_exp_down"][0, c[1]][:, 512 * c[2]:512 * c[2] + 512].reshape(4, P, 512).transpose(1, 0, 2).reshape(P, CH)

    def fmajor(v):
        return v.reshape(v.shape[0], -1, P).transpose(2, 1, 0)

    x = np.concatenate([a["x_prompt"][0], a["x_sample"].reshape(NSAMP, D)])
    c = np.concatenate([a["c_prompt"], a["c_sample"]])
    ds = np.repeat(a["d_skip"][0].reshape(PAIRS, 2), HD, axis=1)
    vec = np.concatenate([
        np.concatenate([a[n].reshape(-1) for n in ("b_ada", "norm1_w", "norm2_w", "final_norm_w", "conv_b", "ssd_norm_w",
                                                    "merge_b", "conv_w", "gla_gate_b", "gla_norm_w")]).reshape(-1, P),
        ds]).T
    cst, lvm = constants()
    arrays = {
        "w": w, "x": fmajor(x), "c": fmajor(c), "vec": vec, "cst": cst, "lvm": lvm,
        "cvs": fmajor(a["state_conv"][0].reshape(NS * 3, -1)),
        "wdt": w_in[:, W_DT:W_DT + HEADS].reshape(KT, P, HEADS).transpose(1, 0, 2),
        "wgl": w_in[:, W_GLR:W_GLR + RANK].reshape(KT, P, RANK).transpose(1, 0, 2),
        "gup": a["gla_gate_up"][0],
        "dt_bias": a["dt_bias"][0], "a_log": a["a_log"][0], "router_bias": a["router_bias"],
        "wr": a["w_router"].reshape(KT, P, E).transpose(1, 0, 2),
        "sg": a["state_gla"][0].transpose(1, 2, 0, 3),
        "ss": a["state_ssm"][0].reshape(NS, PAIRS, P, NSTATE).transpose(1, 3, 0, 2),
    }
    outs = {
        "y": (T, D), "conv_new": (P, NCONV, NSEQ * 3), "ssm_p": (PAIRS, NSTATE, P), "gla_p": (GH, GDK, GDV),
        "ss_new": (PAIRS, NSTATE, NS, P), "sg_new": (GH, GDK, NS, GDV),
    }
    nc = _bacc.Bacc("TRN2", target_bir_lowering=False, num_devices=1)
    arrays = {f"in_{k}": np.ascontiguousarray(v) for k, v in arrays.items()}
    d = {k[3:]: nc.dram_tensor(k, v.shape, mybir.dt.from_np(v.dtype), kind="ExternalInput").ap() for k, v in arrays.items()}
    for k, shape in outs.items():
        d[k] = nc.dram_tensor(f"out_{k}", shape, F32, kind="ExternalOutput").ap()
    d["xd"] = nc.dram_tensor("xd", (XROWS + CAP, D), F32, kind="Internal").ap()
    d["yd"] = nc.dram_tensor("yd", (E, CAP, D), F32, kind="Internal").ap()
    build(nc, d)
    r = _run(nc, [arrays], core_ids=[0]).results[0]
    o = {k: np.asarray(r[f"out_{k}"]) for k in outs}

    y = o["y"]
    cv = o["conv_new"].transpose(2, 1, 0).reshape(NSEQ, 3, NCONV * P)
    sp = o["ssm_p"].transpose(0, 2, 1).reshape(1, 1, HEADS, HD, NSTATE)
    ss = o["ss_new"].transpose(2, 0, 3, 1).reshape(1, NS, HEADS, HD, NSTATE)
    sg = o["sg_new"].transpose(2, 0, 1, 3)[None]
    outs_ = (y[None, :NP_], y[NP_:].reshape(NS, ST, D), cv[None, :1], sp, o["gla_p"][None, None], cv[None, 1:], ss, sg)
    return tuple(np.ascontiguousarray(v) for v in outs_)
```

```python
from contextlib import ExitStack

import numpy as np

import concourse.bass as bass
from concourse import mybir

ALU = mybir.AluOpType
ACT = mybir.ActivationFunctionType
AX = mybir.AxisListType
F32 = mybir.dt.float32
U8 = mybir.dt.uint8

P = 128
D = 1024
KT = D // P
NP_, NS, ST = 256, 8, 8
NSAMP = NS * ST
T = NP_ + NSAMP
NSEQ = 1 + NS
QUAD = 32
HEADS, HD, NSTATE, GROUPS = 32, 64, 128, 4
PAIRS = HEADS // 2
PPG = PAIRS // GROUPS
GH, GDK, GDV = 4, 128, 256
RANK = 16
CONVK = 4
NX, NBC = 16, 8
NCONV = NX + NBC
E, EG, EPG = 16, 4, 4
EPS = 1e-6
TOP = 2
CAP = 96
XROWS = TOP * T
TAU = 16.0
R = 6
CH = 2048
NEG = -3.0e38
LEVELS = [1, 256, 128, 64, 32, 16, 8, 4, 2]
NL = len(LEVELS)
MASKED = LEVELS[2:]
EXTW = CONVK - 1 + NP_ + NS * (CONVK - 1 + ST)
S0 = CONVK - 1 + NP_
SW = CONVK - 1 + ST

V_ADA, V_N1, V_N2, V_FIN, V_CB, V_SSDN, V_MRG = 0, 48, 56, 64, 72, 96, 112
V_CW, V_GB, V_GN, V_DS = 128, 224, 228, 230
NV = V_DS + PAIRS

C_ONE = 0
C_EPS = C_ONE + P
C_QS = C_EPS + 1
C_ID = C_QS + NSEQ
C_U = C_ID + P
C_R = C_U + P
C_CM = C_R + P
C_DM = C_CM + T
C_RS = C_DM + T
C_US = C_RS + T
C_RSS = C_US + NSAMP
C_SEQ = C_RSS + NSAMP
C_PR = C_SEQ + NS
C_YR = C_PR + 16 + 4
C_QE = C_YR + E
NC = C_QE + E

W_Z, W_X, W_B, W_C, W_DT, W_Q, W_K, W_V, W_R, W_GLR, W_GA, W_GB = (
    0, 2048, 4096, 4608, 5120, 5152, 5664, 6176, 7200, 8224, 8240, 9264)


def weight_order():
    def w_in(col, tiles):
        return [("in", col + 256 * i) for i in range(tiles // 2)]
    out = [("ada", c) for c in range(8)]
    out += w_in(W_Q, 4) + w_in(W_K, 4) + w_in(W_V, 8)
    p2 = w_in(W_R, 8) + w_in(W_B, 4) + w_in(W_C, 4) + w_in(W_X, 16)
    for i, c in enumerate(p2):
        out += [c, ("ada", 8 + i)]
    out += w_in(W_Z, 16) + w_in(W_GA, 8) + w_in(W_GB, 8)
    out += [("gla", c) for c in range(4)]
    out += [("ssd", c, h) for c in range(4) for h in range(2)]
    out += [("out", c) for c in range(4)]
    for e in range(E):
        out += [("gate", e, 0), ("gate", e, 1), ("up", e, 0), ("up", e, 1), ("down", e, 0), ("down", e, 1)]
    return out


ORDER = weight_order()
C_P1 = 8
C_P2 = C_P1 + 8
C_P3 = C_P2 + 32
C_GB = C_P3 + 12
C_GLA = C_GB + 4
C_SSD = C_GLA + 4
C_OUT = C_SSD + 8
C_MOE = C_OUT + 4
N_CHUNK = len(ORDER)
F_SLOT = [5, 9, 14, 18]
N2 = 32
ROUTER_OS = 25
DISPATCH_META = 5
DISPATCH_STEPS = 13
assert N_CHUNK - C_MOE == 6 * E and R == 6 and XROWS % P == 0
AHEAD = 3
LEAD = R - 2


def build(nc, d):
    ctx = ExitStack()
    with ctx:
        def sb(name, shape, dt=F32):
            return ctx.enter_context(nc.sbuf_tensor(name, shape, dt))

        def sem(name):
            return ctx.enter_context(nc.semaphore(name))

        ring = sb("ring", [P, R, CH])
        cst = sb("cst", [P, NC])
        lvw = sb("lvw", [P, len(MASKED) * T // 4], mybir.dt.int32)
        lvm = lvw[:, :].bitcast(U8).rearrange("p (l t) -> p l t", t=T)
        vec = sb("vec", [P, NV])
        hF = sb("hF", [P, KT, T])
        regA = sb("regA", [P, 5632])
        qF = regA[:, 0:1280].rearrange("p (h t) -> p h t", t=T)
        kF = regA[:, 1280:2560].rearrange("p (h t) -> p h t", t=T)
        vT = regA[:, 2560:5632].rearrange("p (a c) -> p a c", a=3)
        zF = regA[:, 0:5120].rearrange("p (k t) -> p k t", t=T)
        oF = sb("oF", [P, KT, T])
        rF = sb("rF", [P, KT, T])
        bcF = sb("bcF", [P, NBC, T])
        xsF = sb("xsF", [P, NX, T])
        bp = sb("bp", [P, 3 * 512 + 1248])
        bT = bp[:, 0:3 * 512].rearrange("p (a b) -> p a b", a=3)
        mod = sb("mod", [P, 48, NSEQ])
        modA = sb("modA", [P, KT, NSEQ])
        cF = sb("cF", [P, KT, NSEQ])
        scF = sb("scF", [P, KT, QUAD])
        rst = sb("rst", [P, T])
        cvs = sb("cvs", [P, NCONV, NS * 3])
        ncv = sb("ncv", [P, NCONV, NSEQ * 3])
        wdt = sb("wdt", [P, KT, HEADS])
        wgl = sb("wgl", [P, KT, RANK])
        gup = sb("gup", [RANK, 512])
        glr = sb("glr", [RANK, T])
        dtb = sb("dtb", [P, HEADS])
        aex = sb("aex", [P, HEADS])
        G_SIZE = 9900
        G = sb("G", [P, G_SIZE])
        adaS = sb("adaS", [P, 2, 256])
        ada0 = G[:, 0:1024].rearrange("p (b c) -> p b c", b=4)

        class Carve:
            def __init__(self, region, width):
                self.region, self.width, self.at = region, width, 0

            def take(self, *dims, part=P):
                n = int(np.prod(dims))
                a = self.region[0:part, self.at:self.at + n]
                self.at += n
                assert self.at <= self.width, (self.at, self.width)
                if len(dims) == 2:
                    a = a.rearrange("p (a b) -> p a b", a=dims[0])
                if len(dims) == 3:
                    a = a.rearrange("p (a b c) -> p a b c", a=dims[0], b=dims[1])
                return a

        gla = Carve(G, G_SIZE)
        gF = gla.take(GH, T)
        ebuf = gla.take(2, T)
        qk = gla.take(2, T)
        att = gla.take(2, T + P)
        kd = gla.take(T)
        ekd = gla.take(T)
        eg = gla.take(NSAMP)
        qg = gla.take(NSAMP)
        kdT = gla.take(2, P)
        kdm = gla.take(NS, P)
        sgi = gla.take(NS, GDV)
        sgo = gla.take(2, 2, GDV)
        gfin = gla.take(GDV)
        ext = gla.take(2, 348)
        cvo = gla.take(348)
        tmpx = Carve(xsF[:, :, :].rearrange("p k t -> p (k t)"), NX * T)
        gx = tmpx.take(GH, T)
        gax = tmpx.take(GH, T)
        vst = tmpx.take(2, T)

        ssd = Carve(G, G_SIZE)
        sn = ssd.take(2, NS, P)
        so = ssd.take(2, NS, P)
        L = ssd.take(4, T).rearrange("p (b a) t -> p b a t", b=2)
        cbm = ssd.take(2, T + P)
        bm = ssd.take(NS, P)
        eb = ssd.take(2, T - P)
        t2 = ssd.take(T - P)
        xdt = ssd.take(2, 3, P)
        xdd = ssd.take(2, 4, P)
        prc = Carve(bp[:, 3 * 512:], 1248)
        dtx = prc.take(3, HEADS)
        dta = prc.take(3, HEADS)
        csT = prc.take(3, HEADS)
        wdec = prc.take(4, HEADS)
        EB = prc.take(NS, HEADS)
        dtm = prc.take(NS, HEADS)
        csF = prc.take(T)

        fin2 = sb("fin2", [P, 2, P])
        moe = Carve(G, G_SIZE)
        gbF = moe.take(KT, T)
        rs4 = moe.take(GROUPS, T)
        late = Carve(G, 6656)
        xT = late.take(3, D)
        gT = late.take(2, D)
        wT = late.take(D)
        gsx = late.take(KT, NSAMP)
        moe.at = late.width
        ssq = moe.take(3)
        spare = moe.take(1)
        combF = moe.take(T)
        scr = moe.take(3, E)
        bi = moe.take(3 * EG, EPG)
        pair = moe.take(3 * EG, 6)
        gsc = moe.take(3, EG)
        geq = moe.take(3, EG)
        gone = moe.take(3, EG)
        mx = moe.take(3, 1)
        mx2 = moe.take(3, 1)
        mb = moe.take(3, E)
        eq = moe.take(3, E)
        o1 = moe.take(3, E)
        o2 = moe.take(3, E)
        os_ = moe.take(4, E)
        pos = moe.take(3, 3 * E)
        comb = pos[:, 2]
        picks = moe.take(3, 3 * E)
        sel = moe.take(TOP, 9)
        cnt = moe.take(E)
        cin = moe.take(E)
        mf = moe.take(E + 1)
        meta = sb("meta", [P, E + 1], mybir.dt.int32)
        idx = sb("idx", [P, TOP, 6], mybir.dt.uint32)

        wr = sb("wr", [P, KT, QUAD])
        rb = sb("rb", [P, E])
        combB = xsF
        hT = regA[:, 2560:5632].rearrange("p (a c) -> p a c", a=3)
        xsf = xsF[:, :, :].rearrange("p k t -> p (k t)")
        xe = xsf[:, 0:2048].rearrange("p (b c) -> p b c", b=2)
        yE = xsf[:, 2048:4096].rearrange("p (b c) -> p b c", b=2)
        y2 = xsf[:, 0:3072].rearrange("p (a c) -> p a c", a=3)
        oF_ = oF[:, :, :].rearrange("p k t -> p (k t)")
        heF = oF_[:, 0:2 * KT * CAP].rearrange("p (b k c) -> p b k c", b=2, k=KT)
        bcf = bcF[:, :, :].rearrange("p k t -> p (k t)")
        sgt = regA[:, 2560:2560 + 4 * T].rearrange("p (k t) -> p k t", t=T)
        actF = oF_[:, 0:8 * T].rearrange("p (b k t) -> p b k t", b=2, t=T)
        sgE = xsf[:, 4096:4096 + 8 * CAP].rearrange("p (b c) -> p b c", b=2)
        actE = oF_[:, 16 * CAP:24 * CAP].rearrange("p (b c) -> p b c", b=2)
        extra = [bcf[:, 0:CH], bp[:, 0:CH], rF[:, :, :].rearrange("p k t -> p (k t)")[:, 0:CH]]
        yacc = zF[:, 0:KT, :]
        x2 = zF[:, 0:KT, :]
        osq = regA[:, 0:KT * T].rearrange("p (k t) -> p k t", t=T)
        rsg = gF

        def ps(name):
            return ctx.enter_context(nc.psum_tensor(name, [P, 512], F32))

        pj = [ps("pjA"), ps("pjB")]
        b = [ps(f"bank{i}") for i in range(6)]

        ident = cst[:, C_ID:C_ID + P]
        upper = cst[:, C_U:C_U + P]
        after = cst[:, C_R:C_R + P]
        ones = cst[:, C_ONE:C_ONE + P]
        cmask = cst[:, C_CM:C_CM + T]
        dmask = cst[:, C_DM:C_DM + T]
        reset = cst[:, C_RS:C_RS + T]
        upper_s = cst[0:NSAMP, C_US:C_US + NSAMP]
        after_s = cst[0:NSAMP, C_RSS:C_RSS + NSAMP]
        seqm = cst[0:NSAMP, C_SEQ:C_SEQ + NS]
        prio16 = cst[:, C_PR:C_PR + 16]
        prio4 = cst[:, C_PR + 16:C_PR + 20]
        yrow = cst[:, C_YR:C_YR + E]
        eps = cst[:, C_EPS:C_EPS + 1]
        quads = cst[:, C_QS:C_QS + NSEQ]
        quads_e = cst[:, C_QE:C_QE + E]

        TT = [(0, P, P), (P, 2 * P, P), (NP_, T, NSAMP)]

        s_first = sem("s_first")
        s_used = sem("s_used")
        s_ready = [sem(f"s_ready{i}") for i in range(R)]
        s_ld0 = sem("s_ld0")
        s_ld1 = sem("s_ld1")
        s_ld3 = sem("s_ld3")
        s_ld2 = sem("s_ld2")
        s_ldc = sem("s_ldc")
        s_adc = sem("s_adc")
        s_adt = sem("s_adt")
        s_silc = sem("s_silc")
        s_nsq = sem("s_nsq")
        s_nss = sem("s_nss")
        s_nsd = sem("s_nsd")
        s_nv = sem("s_nv")
        s_rst = sem("s_rst")
        s_ph = sem("s_ph")
        s_h = sem("s_h")
        s_hk = sem("s_hk")
        s_mp = sem("s_mp")
        s_sq = sem("s_sq")
        s_mod = sem("s_mod")
        s_glr = sem("s_glr")
        s_glrc = sem("s_glrc")
        s_gate = sem("s_gate")
        s_gxv = sem("s_gxv")
        s_gxa = sem("s_gxa")
        s_ev = sem("s_ev")
        s_vtr = sem("s_vtr")
        s_vcp = sem("s_vcp")
        s_ge = sem("s_ge")
        s_gexp = sem("s_gexp")
        s_gqk = sem("s_gqk")
        s_gp = sem("s_gp")
        s_gcp = sem("s_gcp")
        s_kde = sem("s_kde")
        s_kdx = sem("s_kdx")
        s_kdm = sem("s_kdm")
        s_kdt = sem("s_kdt")
        s_kdc = sem("s_kdc")
        s_o = sem("s_o")
        s_oc = sem("s_oc")
        s_gs = sem("s_gs")
        s_gsa = sem("s_gsa")
        s_gpf = sem("s_gpf")
        s_gpfc = sem("s_gpfc")
        s_sgi = sem("s_sgi")
        s_sgo = [sem("s_sgo0"), sem("s_sgo1")]
        s_pst = sem("s_pst")
        s_pre_x = sem("s_pre_x")
        s_cvd = sem("s_cvd")
        s_ncv = sem("s_ncv")
        s_slu = sem("s_slu")
        s_dtp = sem("s_dtp")
        s_dtv = sem("s_dtv")
        s_dta = sem("s_dta")
        s_dtm = sem("s_dtm")
        s_cs = sem("s_cs")
        s_csa = sem("s_csa")
        s_btr = sem("s_btr")
        s_btc = sem("s_btc")
        s_cb = sem("s_cb")
        s_cbc = sem("s_cbc")
        s_bm = sem("s_bm")
        s_xt = sem("s_xt")
        s_csd = sem("s_csd")
        s_csb = [sem("s_csb0"), sem("s_csb1")]
        s_ebc = sem("s_ebc")
        s_xdt = sem("s_xdt")
        s_xdd = sem("s_xdd")
        s_L = sem("s_L")
        s_Lx = sem("s_Lx")
        s_M = sem("s_M")
        s_y = sem("s_y")
        s_yv = sem("s_yv")
        s_sn = sem("s_sn")
        s_sm = sem("s_sm")
        s_sa = sem("s_sa")
        s_pf = sem("s_pf")
        s_pfc = sem("s_pfc")
        s_sin = [sem("s_sin0"), sem("s_sin1")]
        s_sout = [sem("s_sout0"), sem("s_sout1")]
        s_pf_out = [sem("s_pf_out0"), sem("s_pf_out1")]
        s_out = sem("s_out")
        s_set = sem("s_set")
        s_osq = sem("s_osq")
        s_oss = sem("s_oss")
        s_onv = sem("s_onv")
        s_og = sem("s_og")
        s_osd = sem("s_osd")
        s_sil = sem("s_sil")
        s_ysm = sem("s_ysm")
        s_ysq = sem("s_ysq")
        s_yss = sem("s_yss")
        s_ynv = sem("s_ynv")
        s_ysd = sem("s_ysd")
        s_x = sem("s_x")
        s_mxv = sem("s_mxv")
        s_rtq = sem("s_rtq")
        s_rqc = sem("s_rqc")
        s_rtp = sem("s_rtp")
        s_rta = sem("s_rta")
        s_rtv = sem("s_rtv")
        s_ctr = sem("s_ctr")
        s_ctc = sem("s_ctc")
        s_cbb = sem("s_cbb")
        s_cbx = sem("s_cbx")
        s_sg = sem("s_sg")
        s_au = sem("s_au")
        s_ac = sem("s_ac")
        s_dn = sem("s_dn")
        s_ya = sem("s_ya")
        s_f = sem("s_f")

        s_extra = sem("s_extra")
        s_ht = sem("s_ht")
        s_htc = sem("s_htc")
        s_rank = sem("s_rank")
        s_dsp = sem("s_dsp")
        s_pad = sem("s_pad")
        s_xd = sem("s_xd")
        s_xe = [sem("s_xe0"), sem("s_xe1")]
        s_xt2 = sem("s_xt2")
        s_hea = sem("s_hea")
        s_hev = sem("s_hev")
        s_esg = sem("s_esg")
        s_eac = sem("s_eac")
        s_eya = sem("s_eya")
        s_eyv = sem("s_eyv")
        s_yd = [sem("s_yd0"), sem("s_yd1")]
        s_y12 = [sem("s_y12a"), sem("s_y12b"), sem("s_y12c")]
        s_gsx = sem("s_gsx")
        s_tm = sem("s_tm")
        s_tmc = sem("s_tmc")
        s_w1 = sem("s_w1")
        s_cmb = sem("s_cmb")
        s_gm = sem("s_gm")
        s_x3 = sem("s_x3")
        s_yt = sem("s_yt")
        s_ytc = sem("s_ytc")
        s_fsd = sem("s_fsd")
        s_frc = sem("s_frc")
        s_fsq = sem("s_fsq")

        block = ctx.enter_context(nc.Block())
        last_peel = E // 2 - 1

        def few(eng):
            eng.wait_ge(s_dsp, DISPATCH_META)
            return eng.value_load(meta[0:1, E:E + 1], min_val=0, max_val=T) <= CAP

        def expert_pairs(eng, body):
            body(0, True, False)
            with eng.Fori(1, last_peel) as i:
                body(i, False, False)
            body(last_peel, False, True)

        def expert_chunk(eng, e, j, first):
            if first and e == 1 and j < AHEAD:
                eng.wait_ge(s_extra, 16 * AHEAD)
                return extra[j]
            n = C_MOE + j if first and e == 0 else C_MOE + j - AHEAD
            eng.wait_ge(s_ready[n % R], 16 * e + 16 * (n // R + 1))
            return ring[:, n % R, :]

        def w8(i):
            return ring[:, i % R, :].rearrange("p (k c) -> p k c", k=8)

        class Chain:
            def __init__(self, eng, s, at=0):
                self.eng, self.s, self.n = eng, s, at

            def __call__(self, ins):
                ins.then_inc(self.s, 1)
                self.n += 1

            def wait(self):
                self.eng.wait_ge(self.s, self.n)

        def conv_tile(s):
            return s - 8 if 8 <= s < N2 else None

        def chan(ct):
            return 16 + ct if ct < 8 else ct - 8

        def p3_tiles(q):
            t = q + q // 2
            return [t], [t + 1] if q % 2 else []

        def tile_chunk(g):
            if g < 16:
                return C_P1 + g // 2, g % 2
            if g < 48:
                return C_P2 + 2 * ((g - 16) // 2), g % 2
            return C_P3 + (g - 48) // 2, g % 2

        def tile_done(eng, g):
            i, half = tile_chunk(g)
            eng.wait_ge(s_used if half else s_first, i + 1)

        @block.sync
        def _(sp):
            def load(i):
                if i >= R:
                    sp.wait_ge(s_used, i - R + 1)
                sp.dma_start(ring[:, i % R, :], d["w"][i]).then_inc(s_ready[i % R], 16)

            def gla_in(hd):
                if hd:
                    sp.wait_ge(s_o, hd)
                    sp.wait_ge(s_gsa, 8 * hd)
                sp.dma_start(sgi, d["sg"][hd]).then_inc(s_sgi, 16)

            def gla_out(hd, bp):
                sp.wait_ge(s_gsa, 8 * hd + 2 * bp + 2)
                sp.dma_start(d["sg_new"][hd, :, 2 * bp:2 * bp + 2], sgo[:, bp % 2]).then_inc(s_sgo[bp % 2], 16)

            def gla_fin(hd):
                sp.wait_ge(s_gpfc, hd + 1)
                sp.dma_start(d["gla_p"][hd], gfin).then_inc(s_pst, 16)

            def ssd_in(q):
                if q >= 2:
                    sp.wait_ge(s_y, q - 1)
                    sp.wait_ge(s_sm, q - 1)
                else:
                    sp.wait_ge(s_onv, 13)
                    sp.wait_ge(s_gp, NL * GH)
                sp.dma_start(sn[:, q % 2], d["ss"][q]).then_inc(s_sin[q % 2], 16)

            def sums_in(q):
                if q >= 2:
                    sp.wait_ge(s_y, q - 1)
                else:
                    sp.wait_ge(s_csd, 16)
                    sp.wait_ge(s_gs, 4 * GH)
                    sp.wait_ge(s_gsa, 8 * GH)
                    sp.wait_ge(s_gpf, GH)
                    sp.wait_ge(s_kdm, 2 * GH)
                    sp.wait_ge(s_kdc, 2 * GH)
                sp.dma_start(L[:, q % 2].rearrange("p a t -> p (a t)"),
                             d["csd"][2 * q:2 * q + 2].rearrange("a t -> (a t)").partition_broadcast(P)
                             ).then_inc(s_csb[q % 2], 16)

            def ssd_out(q):
                sp.wait_ge(s_sa, 2 * q + 2)
                sp.dma_start(d["ss_new"][q], so[:, q % 2]).then_inc(s_sout[q % 2], 16)
                sp.wait_ge(s_pfc, q + 1)
                sp.dma_start(d["ssm_p"][q], fin2[:, q % 2]).then_inc(s_pf_out[q % 2], 16)

            for i in range(C_P2):
                load(i)
            gla_in(0)
            for s in range(N2 + LEAD):
                if s < N2:
                    load(C_P2 + s)
                elif C_P2 + s < C_P3 + LEAD:
                    load(C_P2 + s)
                x = s - LEAD
                if x == 26:
                    sums_in(0)
                    sums_in(1)
                for hd in range(GH):
                    if x == F_SLOT[hd] + 2:
                        gla_out(hd, 0)
                    if x == F_SLOT[hd] + 3:
                        gla_out(hd, 1)
                        gla_out(hd, 2)
                    if x == F_SLOT[hd] + 4:
                        gla_out(hd, 3)
                        if hd + 1 < GH:
                            gla_in(hd + 1)
                        gla_fin(hd)
            ssd_in(0)
            ssd_in(1)
            nxt = C_P3 + LEAD
            for q in range(PAIRS):
                while nxt <= C_P3 + 3 * q // 4 + R - 1 and nxt < C_MOE:
                    load(nxt)
                    nxt += 1
                if q + 2 < PAIRS:
                    sums_in(q + 2)
                ssd_out(q)
                if q + 2 < PAIRS:
                    ssd_in(q + 2)
            while nxt < C_GLA + R:
                load(nxt)
                nxt += 1
            sp.wait_ge(s_yss, GROUPS)
            sp.dma_start(x2, d["x"]).then_inc(s_x, 16)
            def load_extra(j):
                sp.dma_start(extra[j], d["w"][C_MOE + 6 + j]).then_inc(s_extra, 16)

            sp.wait_ge(s_ynv, 1)
            sp.wait_ge(s_sm, PAIRS)
            load_extra(0)
            load_extra(1)
            for i in range(nxt, C_MOE + R):
                load(i)
                if i == C_OUT + R - 1:
                    sp.wait_ge(s_mxv, 24)
                    load_extra(2)

            def reload(e, j, used):
                n = (C_MOE + j - AHEAD) % R
                sp.wait_ge(s_used, used)
                sp.dma_start(ring[:, n, :], d["w"][6 * e + (C_MOE + j)]).then_inc(s_ready[n], 16)

            def second_half(e):
                for j in (3, 4, 5):
                    reload(e + 1, j, C_MOE + j - 3 + 1 if isinstance(e, int) and e == 0 else 6 * e + (C_MOE + j + 1))

            def first_half(e):
                for j in (0, 1, 2):
                    reload(e + 2, j, C_MOE + j + 3 + 1 if isinstance(e, int) and e == 0 else 6 * e + (C_MOE + 6 + j + 1))

            def first_row(e):
                return sp.value_load(meta[0:1, bass.ds(e, 1)], min_val=0, max_val=XROWS)

            def tokens_in(at, v):
                sp.dma_start(xe[0:CAP, v], d["xd"][bass.ds(at, CAP), :]).then_inc(s_xe[v], 16)

            with sp.If(few(sp)):
                starts = [first_row(v) for v in range(2)]
                sp.wait_ge(s_pad, 16)
                sp.wait_ge(s_xd, 16 * 6)
                for v in range(2):
                    tokens_in(starts[v], v)

                def two(i, first, last):
                    for v in range(2):
                        e = 2 * i + v
                        if not last:
                            sp.wait_ge(s_xt2, e + 1)
                            tokens_in(first_row(e + 2), v)
                        if not (last and v):
                            second_half(e)
                        sp.wait_ge(s_eya, e + 1)
                        sp.wait_ge(s_eyv, e + 1)
                        sp.dma_start(d["yd"][e], yE[0:CAP, v]).then_inc(s_yd[v], 16)
                        if not last:
                            first_half(e)

                expert_pairs(sp, two)
            with sp.Else():
                second_half(0)
                first_half(0)
                with sp.Fori(1, E - 2) as e:
                    second_half(e)
                    first_half(e)
                second_half(E - 2)
                sp.wait_ge(s_pad, 16)
                sp.wait_ge(s_xd, 16 * 6)
            sp.dma_start(d["conv_new"], ncv[:, :, :]).then_inc(s_out, 16)
            for t, (c0, c1, rows) in enumerate(TT):
                sp.wait_ge(s_f, t + 1)
                sp.dma_start(d["y"][c0:c1, :], hT[0:rows, t, :]).then_inc(s_out, 16)
            sp.wait_ge(s_out, 16 * 4)
            sp.wait_ge(s_pst, 16 * GH)
            for i in range(2):
                sp.wait_ge(s_sout[i], 16 * (PAIRS // 2))
                sp.wait_ge(s_pf_out[i], 16 * (PAIRS // 2))
                sp.wait_ge(s_sgo[i], 16 * 8)

        @block.tensor
        def _(pe):
            def chunk(i):
                pe.wait_ge(s_ready[i % R], 16 * (i // R + 1))
                return w8(i)

            def proj(g, rhs=None):
                i, half = tile_chunk(g)
                w = chunk(i) if half == 0 else w8(i)
                if g >= 2:
                    pe.wait_ge(s_ev, g - 1)
                for k in range(KT):
                    mm = pe.matmul(pj[g % 2][:, 0:T], w[:, k, half * P:half * P + P], hF[:, k, :],
                                   start=(k == 0), stop=(k == KT - 1))
                mm.then_inc(s_used if half else s_first, 1)

            def ada(i, out):
                w = chunk(i)
                for k in range(KT):
                    q = k % 4 * QUAD
                    mm = pe.matmul(out[q:q + QUAD, 0:256], scF[:, k, :], w[:, k, :], start=(k < 4), stop=(k >= 4),
                                   tile_position=(0, q), skip_group_check=True)
                    if k == 0:
                        mm.then_inc(s_first, 1)
                mm.then_inc(s_used, 1)

            def ada_turn(c, out):
                pe.wait_ge(s_adc, c + 1)
                for half in range(2):
                    mm = pe.matmul(out[:, half * NSEQ:(half + 1) * NSEQ],
                                      (adaS[:, c % 2, :] if c >= 8 else ada0[:, c % 4, :])[:, half * P:half * P + P],
                                   quads, start=True, stop=True)
                mm.then_inc(s_adt, 1)

            def norm_sums(n, src):
                pe.wait_ge(s_nsq, n)
                for k in range(KT):
                    mm = pe.matmul(b[0][:, 0:T], ones, src[:, k, :], start=(k == 0), stop=(k == KT - 1))
                mm.then_inc(s_nss, 1)

            def h_ready(n):
                pe.wait_ge(s_h, n)
                pe.wait_ge(s_mp, KT * n)

            pe.wait_ge(s_silc, 1)
            for c in range(8 + 3):
                if c < 8:
                    if c >= 2:
                        pe.wait_ge(s_adc, c - 1)
                    ada(c, b[2 + c % 2])
                if c >= 3:
                    pe.wait_ge(s_ld0, 16 * 3)
                    ada_turn(c - 3, b[5][:, 2 * NSEQ * (c - 3):2 * NSEQ * (c - 2)])
                if c == 5:
                    norm_sums(1, hF)

            h_ready(1)
            pe.wait_ge(s_ld1, 16 * 2)
            for k in range(KT):
                mm = pe.matmul(b[1][0:RANK, 0:T], wgl[:, k, :], hF[:, k, :], start=(k == 0), stop=(k == KT - 1))
            mm.then_inc(s_glr, 1)
            proj(0)
            pe.wait_ge(s_glrc, 1)
            for hd in range(GH):
                if hd >= 2:
                    pe.wait_ge(s_gxv, hd - 1)
                pe.matmul(b[2 + hd % 2][:, 0:T], gup[:, hd * P:hd * P + P], glr[:, :],
                          start=True, stop=True).then_inc(s_gate, 1)
            for g in range(1, 17):
                if g < 16:
                    proj(g)
                v = g - 9
                if v >= 0:
                    if v == 0:
                        pe.wait_ge(s_ld3, 16)
                    pe.wait_ge(s_ev, g)
                    if v:
                        pe.wait_ge(s_vcp, 2 * v)
                    for t, (c0, c1, rows) in enumerate(TT):
                        mm = pe.transpose(b[4][0:rows, t * P:t * P + P], vst[:, v % 2, c0:c1], ident)
                    mm.then_inc(s_vtr, 1)

            def level(j):
                hd, lv = divmod(j, NL)
                size = LEVELS[lv]
                bank = b[j % 2]
                if lv:
                    pe.wait_ge(s_gqk, 8 * hd + lv)
                else:
                    pe.wait_ge(s_ev, 16)
                if j >= 2:
                    pe.wait_ge(s_gcp, j - 1)
                buf = qk[:, j % 2, :]
                left, right = (kF[:, hd, :], qF[:, hd, :]) if lv == 0 else (buf, buf)
                if size == 256:
                    pe.matmul(bank[:, 0:P], left[:, 0:P], right[:, P:2 * P], start=True, stop=True).then_inc(s_gp, 1)
                    return
                for c0, c1, rows in TT[:3 if size <= ST else 2]:
                    mm = pe.matmul(bank[0:rows, c0:c1], left[:, c0:c1], right[:, c0:c1], start=True, stop=True)
                mm.then_inc(s_gp, 1)

            def kd_turn(hd):
                pe.wait_ge(s_kdm, 2 * hd + 1)
                if hd == 0:
                    pe.wait_ge(s_vcp, 2 * 8)
                else:
                    pe.wait_ge(s_gpfc, hd)
                for t, (c0, c1, rows) in enumerate(TT):
                    mm = pe.transpose(b[4][0:rows, t * P:t * P + P], kd[:, c0:c1], ident)
                mm.then_inc(s_kdt, 1)

            def gla_o(hd):
                a = att[:, hd % 2, :]
                pe.wait_ge(s_gcp, NL * (hd + 1))
                pe.wait_ge(s_kdm, 2 * hd + 2)
                pe.wait_ge(s_sgi, 16 * (hd + 1))
                if hd:
                    pe.wait_ge(s_oc, 2 * hd)
                else:
                    pe.wait_ge(s_gxv, 4)
                for v in range(2):
                    cols = slice(hd * GDV + v * P, hd * GDV + v * P + P)
                    o = b[2 + v]
                    pe.matmul(o[:, 0:P], vT[:, 0, cols], a[:, 0:P], start=True, stop=True)
                    pe.matmul(o[:, P:2 * P], vT[:, 0, cols], a[:, 320:448], start=True, stop=False)
                    pe.matmul(o[:, P:2 * P], vT[:, 1, cols], a[:, P:2 * P], start=False, stop=True)
                    pe.matmul(o[:, NP_:T], vT[0:NSAMP, 2, cols], a[0:NSAMP, NP_:T], start=True, stop=True)
                    for s in range(NS):
                        mm = pe.matmul(o[:, NP_ + ST * s:NP_ + ST * s + ST], sgi[:, s, v * P:v * P + P],
                                       qg[:, ST * s:ST * s + ST], start=False, stop=True,
                                       skip_group_check=True)
                mm.then_inc(s_o, 1)

            def gla_state(hd, bp):
                pe.wait_ge(s_kdc, 2 * hd + 2)
                if bp:
                    pe.wait_ge(s_gsa, 8 * hd + 2 * bp)
                for j in range(2):
                    mm = pe.matmul(b[4][:, j * GDV:(j + 1) * GDV], kdm[0:NSAMP, 2 * bp + j, :],
                                   vT[0:NSAMP, 2, hd * GDV:(hd + 1) * GDV], start=True, stop=True)
                mm.then_inc(s_gs, 1)

            def gla_prompt(hd):
                pe.wait_ge(s_gsa, 8 * hd + 8)
                for t in range(2):
                    mm = pe.matmul(b[4][:, 0:GDV], kdT[:, t, :], vT[:, t, hd * GDV:(hd + 1) * GDV],
                                   start=(t == 0), stop=(t == 1))
                mm.then_inc(s_gpf, 1)

            def dt_proj():
                pe.wait_ge(s_ld2, 16 * 7)
                pe.wait_ge(s_gcp, NL * GH)
                for t, (c0, c1, rows) in enumerate(TT):
                    for k in range(KT):
                        mm = pe.matmul(b[0][0:rows, t * HEADS:(t + 1) * HEADS], hF[:, k, c0:c1], wdt[:, k, :],
                                       start=(k == 0), stop=(k == KT - 1))
                mm.then_inc(s_dtp, 1)

            def sums():
                pe.wait_ge(s_dtv, 4)
                pe.wait_ge(s_dtm, 1)
                pe.wait_ge(s_oc, 2 * GH)
                w = b[1]
                pe.matmul(w[:, 0:64], upper, dta[:, 0:2, :].rearrange("p a b -> p (a b)"), start=True, stop=True)
                pe.matmul(w[0:NSAMP, 64:96], upper_s, dta[0:NSAMP, 2, :], start=True, stop=True)
                pe.matmul(w[:, 96:160], after, dta[:, 0:2, :].rearrange("p a b -> p (a b)"), start=True, stop=True)
                pe.matmul(w[:, 160:192], after, dta[:, 0, :], start=True, stop=False)
                pe.matmul(w[:, 160:192], ones, dta[:, 1, :], start=False, stop=True)
                pe.matmul(w[0:NSAMP, 192:224], after_s, dta[0:NSAMP, 2, :], start=True, stop=True)
                pe.matmul(w[:, 224:480], ones[0:NSAMP, :], dtm[0:NSAMP].rearrange("p a b -> p (a b)"),
                          start=True, stop=True)
                pe.matmul(b[2][0:HEADS, 0:P], dta[:, 0, :], upper, start=True, stop=True)
                pe.matmul(b[2][0:HEADS, P:2 * P], dta[:, 1, :], upper, start=True, stop=True)
                pe.matmul(b[2][0:HEADS, NP_:T], dta[0:NSAMP, 2, :], upper_s, start=True, stop=True).then_inc(s_cs, 1)

            def b_turn(t):
                c0, c1, rows = TT[t]
                if t == 0:
                    pe.wait_ge(s_slu, 1)
                    pe.wait_ge(s_dtv, 2)
                else:
                    pe.wait_ge(s_btc, t)
                for g in range(GROUPS):
                    mm = pe.transpose(b[0][0:rows, g * P:g * P + P], bcF[:, g, c0:c1], ident)
                mm.then_inc(s_btr, 1)

            def cb(g):
                if g == 0:
                    pe.wait_ge(s_slu, 2)
                    pe.wait_ge(s_oc, 2 * GH)
                else:
                    pe.wait_ge(s_sa, 8 * g)
                for c0, c1, rows in TT:
                    pe.matmul(b[3][0:rows, c0:c1], bcF[:, g, c0:c1], bcF[:, 4 + g, c0:c1], start=True, stop=True)
                pe.matmul(b[3][:, T:T + P], bcF[:, g, 0:P], bcF[:, 4 + g, P:2 * P],
                          start=True, stop=True).then_inc(s_cb, 1)

            for s in range(N2):
                for hd in range(GH):
                    if s == F_SLOT[hd] + 3:
                        gla_state(hd, 2)
                proj(16 + s)
                for hd in range(GH):
                    if s == F_SLOT[hd] + 2:
                        gla_state(hd, 0)
                    if s == F_SLOT[hd] + 4:
                        gla_prompt(hd)
                if s % 2:
                    pe.wait_ge(s_mod, 1 + s // 2)
                    ada(C_P2 + s, b[5])
                elif s:
                    ada_turn(7 + s // 2, b[5][:, 256:256 + 2 * NSEQ])
                for j in (2 * s, 2 * s + 1):
                    if j < NL * GH:
                        level(j)
                for hd in range(GH):
                    if s == F_SLOT[hd]:
                        kd_turn(hd)
                    if s == F_SLOT[hd] + 1:
                        gla_o(hd)
                    if s == F_SLOT[hd] + 2:
                        gla_state(hd, 1)
                    if s == F_SLOT[hd] + 3:
                        gla_state(hd, 3)
                if s == 20:
                    dt_proj()
                if s == 22:
                    sums()
                if 24 <= s < 27:
                    b_turn(s - 24)
                if s == 27:
                    cb(0)
                if s in (25, 26):
                    pe.wait_ge(s_osq, 1)
                    if s == 25:
                        pe.wait_ge(s_csa, 4)
                        pe.wait_ge(s_dtv, 6)
                    else:
                        pe.wait_ge(s_onv, 2)
                    for j in range(2):
                        hd = 2 * (s - 25) + j
                        for v in range(2):
                            mm = pe.matmul(b[1 + j][:, 0:T], ones, osq[:, 2 * hd + v, :],
                                           start=(v == 0), stop=(v == 1))
                        mm.then_inc(s_oss, 1)

            ada_turn(23, b[5][:, 256:256 + 2 * NSEQ])

            for q in range(PAIRS):
                g = q // PPG
                pe.wait_ge(s_slu, 3 + q // 4)
                pe.wait_ge(s_btc, 3)
                if q:
                    pe.wait_ge(s_xdt, 2 * q)
                for t, (c0, c1, rows) in enumerate(TT):
                    mm = pe.transpose(b[0][0:rows, t * P:t * P + P], xsF[:, q, c0:c1], ident)
                mm.then_inc(s_xt, 1)
                pe.wait_ge(s_csa, 4)
                pe.wait_ge(s_onv, 4)
                if q:
                    pe.wait_ge(s_pfc, q)
                before, afterwards = p3_tiles(q)
                for t in before:
                    proj(48 + t)
                x_, xd = xdt[:, q % 2], xdd[:, q % 2]
                pe.wait_ge(s_xdt, 2 * q + 2)
                if q:
                    pe.wait_ge(s_yv, 3 * q - 1)
                else:
                    pe.wait_ge(s_gpfc, GH)
                pe.wait_ge(s_M, 2 * q + 2)
                for t, (c0, c1, rows) in enumerate(TT):
                    for j in range(2):
                        pe.matmul(b[4][64 * j:64 * j + 64, c0:c1], x_[0:rows, t, 64 * j:64 * j + 64],
                                  L[0:rows, q % 2, j, c0:c1], start=True, stop=True)
                pe.wait_ge(s_xdd, 3 * q + 3)
                pe.matmul(b[4][:, T:T + P], xd[:, 0, :], cbm[:, g % 2, T:T + P], start=True, stop=True)
                pe.wait_ge(s_sin[q % 2], 16 * (q // 2 + 1))
                for s in range(NS):
                    mm = pe.matmul(b[4][:, T + P + ST * s:T + P + ST * s + ST], sn[:, q % 2, s, :],
                                   bcF[:, 4 + g, NP_ + ST * s:NP_ + ST * s + ST], start=True, stop=True)
                mm.then_inc(s_y, 1)
                pe.matmul(b[2][:, T:T + P], bT[:, 0, g * P:g * P + P], xd[:, 2, :], start=True, stop=False)
                pe.matmul(b[2][:, T:T + P], bT[:, 1, g * P:g * P + P], xd[:, 1, :],
                          start=False, stop=True).then_inc(s_pf, 1)
                pe.wait_ge(s_bm, g + 1)
                for half in range(2):
                    bank = b[5] if half == 0 else b[3]
                    if half == 0:
                        if q:
                            pe.wait_ge(s_sa, 2 * q - 1)
                        else:
                            pe.wait_ge(s_mod, 17)
                    else:
                        pe.wait_ge(s_cbc, 3 * g + 3)
                        if q:
                            pe.wait_ge(s_sa, 2 * q)
                    for s in range(4):
                        mm = pe.matmul(bank[:, s * P:s * P + P], bm[0:NSAMP, 4 * half + s, :], xd[0:NSAMP, 3, :],
                                       start=True, stop=True)
                    mm.then_inc(s_sn, 1)
                for t in afterwards:
                    proj(48 + t)
                if q % PPG == PPG - 1 and g + 1 < GROUPS:
                    cb(g + 1)

            for t in range(8):
                proj(72 + t)
            def y_sums():
                pe.wait_ge(s_sa, 2 * PAIRS)
                pe.wait_ge(s_pfc, PAIRS)
                for g in range(GROUPS):
                    pe.wait_ge(s_ysq, g + 1)
                    for t in range(4):
                        mm = pe.matmul(b[g][:, 0:T], ones, zF[:, 4 * g + t, :], start=(t == 0), stop=(t == 3))
                    mm.then_inc(s_yss, 1)

            def tile(w, half, src, k0, first, last):
                for k in range(KT):
                    mm = pe.matmul(pj[half][:, 0:T], w[:, k, half * P:half * P + P], src[:, k0 + k, :],
                                   start=(first and k == 0), stop=(last and k == KT - 1), skip_group_check=True)
                mm.then_inc(s_used if half else s_first, 1)

            pe.wait_ge(s_ev, 80)
            pe.wait_ge(s_og, 1)
            for c in range(4):
                w = chunk(C_GLA + c)
                for half in range(2):
                    if c:
                        pe.wait_ge(s_mxv, 2 * c + half - 1)
                    tile(w, half, oF, 0, True, True)
                if c == 0:
                    y_sums()
            pe.wait_ge(s_ynv, 22)
            for c in range(4):
                for h in range(2):
                    w = chunk(C_SSD + 2 * c + h)
                    for half in range(2):
                        if h == 0:
                            pe.wait_ge(s_mxv, 8 + 2 * (2 * c + half - 2) + 1 if c else 7 + half)
                        tile(w, half, xsF, h * KT, h == 0, h == 1)
            def square_sum(t):
                pe.wait_ge(s_sq, t + 1)
                mm = pe.matmul(b[0][:, 0:T], ones, hF[:, t, :], start=(t == 0), stop=(t == KT - 1),
                               skip_group_check=True)
                if t == KT - 1:
                    mm.then_inc(s_nss, 1)

            pe.wait_ge(s_mxv, 24)
            for c in range(4):
                w = chunk(C_OUT + c)
                for half in range(2):
                    if c:
                        pe.wait_ge(s_mxv, 24 + 3 * (2 * c + half - 2) + 2)
                    tile(w, half, gbF, 0, True, True)
                    if 2 * c + half >= 3:
                        square_sum(2 * c + half - 3)

            for t in range(5, 8):
                square_sum(t)
            h_ready(2)
            for k in range(KT):
                q = k % 4 * QUAD
                mm = pe.matmul(b[1][q:q + QUAD, 0:T], wr[:, k, :], hF[:, k, :], start=(k < 4), stop=(k >= 4),
                               tile_position=(0, q), skip_group_check=True)
            mm.then_inc(s_rtq, 1)
            for t, (c0, c1, rows) in enumerate(TT):
                for half in range(2):
                    n = 2 * t + half
                    if n >= 4:
                        pe.wait_ge(s_htc, n - 3)
                    for k in range(4):
                        mm = pe.transpose(b[2 + n % 4][0:rows, k * P:k * P + P], hF[:, 4 * half + k, c0:c1], ident)
                    mm.then_inc(s_ht, 1)
                    if n == 0:
                        pe.wait_ge(s_rqc, 1)
                        for u, (a0, a1, r) in enumerate(TT):
                            mm = pe.matmul(b[0][0:r, u * E:(u + 1) * E], combF[:, a0:a1], quads_e, start=True, stop=True)
                        mm.then_inc(s_rtp, 1)
            pe.wait_ge(s_rtv, ROUTER_OS)
            ranks = b[1][:, 64:64 + 4 * E]
            flat_os = os_.rearrange("p a b -> p (a b)")
            pe.matmul(ranks, upper, flat_os, start=True, stop=True)
            for t in range(1, 4):
                mm = pe.matmul(ranks[:, t * E:], ones, flat_os[:, 0:(4 - t) * E], start=False, stop=True,
                               skip_group_check=True)
            mm.then_inc(s_rank, 1)

            pe.wait_ge(s_htc, 6)
            pe.wait_ge(s_gsx, 1)
            for n in range(12):
                if n >= 4:
                    pe.wait_ge(s_tmc, n - 3)
                bank = (b[4], b[5], pj[0], pj[1])[n % 4]
                for k in range(4):
                    f = 4 * (n % 2) + k
                    if n < 6:
                        c0, c1, rows = TT[n // 2]
                        mm = pe.transpose(bank[0:rows, k * P:k * P + P], x2[:, f, c0:c1], ident)
                    elif n < 10:
                        col = vec[:, V_FIN + f:V_FIN + f + 1] if n < 8 else mod[:, 40 + f, 0:1]
                        mm = pe.matmul(bank[:, k * P:k * P + P], col.to_broadcast([P, P]), ident, start=True, stop=True)
                    else:
                        mm = pe.transpose(bank[0:NSAMP, k * P:k * P + P], gsx[:, f, :], ident)
                mm.then_inc(s_tm, 1)

            def turn_tokens(i, v):
                pe.wait_ge(s_xe[v], 16 * i + 16)
                for k in range(KT):
                    mm = pe.transpose(b[k // 4][:, (k % 4) * CAP:(k % 4 + 1) * CAP], xe[0:CAP, v, k * P:k * P + P],
                                      ident[0:CAP, 0:CAP])
                mm.then_inc(s_xt2, 1)

            with pe.If(few(pe)):
                pe.wait_ge(s_tmc, 12)
                turn_tokens(0, 0)

                def two(i, first, last):
                    for v in range(2):
                        e = 2 * i + v
                        pe.wait_ge(s_hea, e + 1)
                        pe.wait_ge(s_hev, e + 1)
                        for part, used in ((0, s_esg), (1, s_eac)):
                            if not first:
                                pe.wait_ge(used, e - 1)
                            for f in range(4):
                                if f % 2 == 0:
                                    w = expert_chunk(pe, e, 2 * part + f // 2, first).rearrange("p (k c) -> p k c", k=8)
                                for k in range(KT):
                                    mm = pe.matmul(b[2 + 2 * part + v][:, f * CAP:(f + 1) * CAP],
                                                   w[:, k, (f % 2) * P:(f % 2) * P + P], heF[:, v, k, :],
                                                   start=(k == 0), stop=(k == KT - 1))
                                if f % 2:
                                    mm.then_inc(s_used, 1)
                        if not (last and v):
                            turn_tokens(i + v, 1 - v)
                        pe.wait_ge(s_eac, e + 1)
                        for c in range(2):
                            w = expert_chunk(pe, e, 4 + c, first).rearrange("p (k c) -> p k c", k=4)
                            if not (first and v == 0):
                                pe.wait_ge(s_eyv if c else s_eya, e)
                            for k in range(4):
                                mm = pe.matmul(pj[c][0:CAP, :], actE[:, v, k * CAP:(k + 1) * CAP], w[:, k, :],
                                               start=(k == 0), stop=(k == 3))
                            mm.then_inc(s_used, 1)

                expert_pairs(pe, two)
            with pe.Else():
                pe.wait_ge(s_dsp, DISPATCH_META + 2)
                pe.wait_ge(s_tmc, 12)
                for t, (c0, c1, rows) in enumerate(TT):
                    mm = pe.transpose(b[2][0:E, c0:c1], comb[0:rows, t * E:(t + 1) * E], ident[0:rows, 0:rows])
                mm.then_inc(s_ctr, 1)
                pe.wait_ge(s_ctc, 1)
                for e in range(E):
                    if e >= 2:
                        pe.wait_ge(s_cbx, e - 1)
                    pe.matmul(b[4 + e % 2][:, 0:T], ident[0:E, e:e + 1].to_broadcast([E, P]), combF[0:E, :],
                              start=True, stop=True).then_inc(s_cbb, 1)

                def two(i, first, last):
                    for v in range(2):
                        e = 2 * i + v
                        for part, used in ((0, s_sg), (1, s_au)):
                            for f in range(4):
                                if f % 2 == 0:
                                    w = expert_chunk(pe, e, 2 * part + f // 2, first).rearrange("p (k c) -> p k c", k=8)
                                if not (first and v == 0 and f < 2):
                                    pe.wait_ge(used, 4 * e + f - 1)
                                for k in range(KT):
                                    mm = pe.matmul(b[2 * part + f % 2][:, 0:T], w[:, k, (f % 2) * P:(f % 2) * P + P],
                                                   hF[:, k, :], start=(k == 0), stop=(k == KT - 1))
                                mm.then_inc(s_used if f % 2 else s_first, 1)
                        for c in range(2):
                            w = expert_chunk(pe, e, 4 + c, first).rearrange("p (k c) -> p k c", k=4)
                            for t in range(4):
                                if not (first and v == 0 and c == 0 and t < 2):
                                    pe.wait_ge(s_ya, 8 * e + (4 * c + t - 1))
                                for k in range(4):
                                    if c == 0 and t == 0:
                                        pe.wait_ge(s_ac, 4 * e + (k + 1))
                                    mm = pe.matmul(pj[t % 2][:, 0:T], w[:, k, t * P:t * P + P], actF[:, v, k, :],
                                                   start=(k == 0), stop=(k == 3))
                                mm.then_inc(s_dn, 1) if t < 3 else mm.then_inc(s_used, 1)

                expert_pairs(pe, two)
                pe.wait_ge(s_ya, 8 * E)
                for t, (c0, c1, rows) in enumerate(TT):
                    for half in range(2):
                        n = 2 * t + half
                        if n >= 2:
                            pe.wait_ge(s_ytc, n - 1)
                        for k in range(4):
                            mm = pe.transpose(b[n % 2][0:rows, k * P:k * P + P], yacc[:, 4 * half + k, c0:c1], ident)
                        mm.then_inc(s_yt, 1)

        def down_done(eng, e, c, t):
            if t < 3:
                eng.wait_ge(s_dn, 6 * e + (3 * c + t + 1))
            else:
                eng.wait_ge(s_used, 6 * e + (C_MOE + 5 + c))

        def halves(a, n, size):
            v = a[:, 0:n].rearrange("p (b s) -> p b s", s=size)
            return v[:, :, 0:size // 2], v[:, :, size // 2:size], v

        def level_of(j):
            hd, lv = divmod(j, NL)
            size = LEVELS[lv]
            return hd, lv, size, NP_ if size > ST else T

        def seqs(a):
            return a[:, NP_:T].rearrange("p (s t) -> p s t", t=ST)

        @block.scalar
        def _(act):
            act.dma_start(cF[:, :, :], d["c"]).then_inc(s_ldc, 16)
            for dst, src in ((oF[:, :, :], "x"), (vec[:, :], "vec")):
                act.dma_start(dst, d[src]).then_inc(s_ld0, 16)
            act.dma_start(cst[:, 0:C_ID], d["cst"][:, 0:C_ID]).then_inc(s_ld0, 16)
            for dst, src in ((wgl[:, :, :], d["wgl"]), (gup[:, :], d["gup"])):
                act.dma_start(dst, src).then_inc(s_ld1, 16)
            act.wait_ge(s_ldc, 16)
            act.wait_ge(s_set, 2)
            act.activation(scF[:, :, 0:NSEQ], cF[:, :, :], ACT.Silu).then_inc(s_silc, 1)

            def root(n):
                act.wait_ge(s_nss, n)
                act.activation(rst[:, :], b[0][:, 0:T], ACT.Sqrt, bias=eps, scale=1.0 / D).then_inc(s_nsd, 1)

            def shift(n, base):
                for k in range(KT):
                    act.wait_ge(s_hk, KT * (n - 1) + k + 1)
                    act.activation(hF[:, k, 0:NP_], hF[:, k, 0:NP_], ACT.Identity,
                                   bias=mod[:, base + k, 0:1]).then_inc(s_mp, 1)

            def ada_copy(c, src):
                act.wait_ge(s_used, c + 1 if c < 8 else C_P2 + 2 * (c - 8) + 2)
                depth, dst = (2, adaS) if c >= 8 else (4, ada0)
                if c >= depth:
                    act.wait_ge(s_adt, c - depth + 1)
                act.activation(dst[:, c % depth, :], src[:, 0:256], ACT.Copy).then_inc(s_adc, 1)

            for c in range(8):
                ada_copy(c, b[2 + c % 2])
                if c == 6:
                    root(1)
            shift(1, 0)
            act.dma_start(cst[:, C_ID:], d["cst"][:, C_ID:]).then_inc(s_ld3, 16)
            for dst, src in ((lvw[:, :], d["lvm"]), (cvs[:, :, :], d["cvs"]), (wdt[:, :, :], d["wdt"]),
                             (dtb[:, :], d["dt_bias"].partition_broadcast(P)),
                             (aex[:, :], d["a_log"].partition_broadcast(P)), (wr[:, :, 0:E], d["wr"]),
                             (rb[:, :], d["router_bias"].partition_broadcast(P))):
                act.dma_start(dst, src).then_inc(s_ld2, 16)
            act.wait_ge(s_glr, 1)
            act.activation(glr[:, :], b[1][0:RANK, 0:T], ACT.Copy).then_inc(s_glrc, 1)
            def evac(g):
                tile_done(act, g)
                src = pj[g % 2][:, 0:T]
                if g < 4:
                    act.activation(qF[:, g, :], src, ACT.Copy, scale=float(GDK) ** -0.5).then_inc(s_ev, 1)
                elif g < 8:
                    act.activation(kF[:, g - 4, :], src, ACT.Copy).then_inc(s_ev, 1)
                elif g < 16:
                    if g >= 10:
                        act.wait_ge(s_vtr, g - 9)
                    act.activation(vst[:, g % 2, :], src, ACT.Copy).then_inc(s_ev, 1)
                elif g < 24:
                    act.activation(rF[:, g - 16, :], src, ACT.Copy).then_inc(s_ev, 1)
                elif g < 48:
                    ct = g - 24
                    if ct >= 2:
                        act.wait_ge(s_cvd, 5 * (ct - 1))
                        act.wait_ge(s_ncv, 2 * (ct - 1))
                    row = ext[:, ct % 2, :]
                    act.activation(row[:, 3:S0], src[:, 0:NP_], ACT.Copy)
                    act.activation(row[:, S0:EXTW].rearrange("p (s t) -> p s t", t=SW)[:, :, 3:SW], seqs(src),
                                   ACT.Copy).then_inc(s_ev, 1)
                elif g < 64:
                    if g == 48:
                        act.wait_ge(s_kdm, 8)
                        act.wait_ge(s_o, GH)
                        act.wait_ge(s_gpf, GH)
                        act.wait_ge(s_oss, GH)
                    act.activation(zF[:, g - 48, :], src, ACT.Copy).then_inc(s_ev, 1)
                elif g < 72:
                    if g == 64:
                        act.wait_ge(s_og, 1)
                    act.activation(rF[:, g - 64, :], src, ACT.Copy).then_inc(s_ev, 1)
                else:
                    t = g - 72
                    act.activation(gbF[:, t, :], src, ACT.Sigmoid,
                                   bias=vec[:, V_MRG + 8 + t:V_MRG + 9 + t]).then_inc(s_ev, 1)

            evac(0)
            act.wait_ge(s_gxv, 4)
            act.activation(gax, gx, ACT.Abs).then_inc(s_gxa, 1)
            act.wait_ge(s_gxa, 1)
            act.activation(gax, gax, ACT.Exp, scale=-1.0).then_inc(s_gxa, 1)
            act.wait_ge(s_gxa, 2)
            act.activation(gax, gax, ACT.Ln, bias=1.0).then_inc(s_gxa, 1)
            act.wait_ge(s_ld2, 16 * 7)
            act.activation(aex[:, :], aex[:, :], ACT.Exp).then_inc(s_dta, 1)
            for g in range(1, 16):
                evac(g)

            for s in range(N2):
                for j in (2 * s, 2 * s + 1):
                    if j < NL * GH and j % NL:
                        hd, lv, size, n = level_of(j)
                        act.wait_ge(s_ge, 8 * hd + lv)
                        act.activation(ebuf[:, j % 2, 0:n], ebuf[:, j % 2, 0:n], ACT.Exp,
                                       scale=1.0 / TAU).then_inc(s_gexp, 1)
                if s in F_SLOT:
                    hd = F_SLOT.index(s)
                    act.wait_ge(s_kde, hd + 1)
                    act.activation(ekd, ekd, ACT.Exp, scale=1.0 / TAU).then_inc(s_kdx, 1)
                    if hd:
                        act.wait_ge(s_kdm, 2 * hd)
                        act.wait_ge(s_gsa, 8 * hd)
                    act.activation(eg, gF[:, hd, NP_:T], ACT.Exp, scale=1.0 / TAU).then_inc(s_kdx, 1)
                evac(16 + s)
                if s % 2:
                    ada_copy(8 + s // 2, b[5])
                for hd in range(GH):
                    if s == F_SLOT[hd] + 2:
                        act.wait_ge(s_o, hd + 1)
                        for v in range(2):
                            act.activation(oF[:, 2 * hd + v, :], b[2 + v][:, 0:T], ACT.Copy).then_inc(s_oc, 1)
                    if s == F_SLOT[hd] + 4:
                        act.wait_ge(s_gpf, hd + 1)
                        if hd:
                            act.wait_ge(s_pst, 16 * hd)
                        act.activation(gfin, b[4][:, 0:GDV], ACT.Copy).then_inc(s_gpfc, 1)
                if s >= 12 and s % 4 == 0:
                    m = (s - 12) // 4
                    act.wait_ge(s_cvd, 5 * (4 * m + 4))
                    x_ = (bcF[:, 4 * m:4 * m + 4, :] if m < 2 else xsF[:, 4 * m - 8:4 * m - 4, :])
                    act.activation(x_, x_, ACT.Silu).then_inc(s_slu, 1)
                if s == 21:
                    act.wait_ge(s_dtv, 2)
                    act.activation(dta, dtx, ACT.Abs).then_inc(s_dta, 1)
                    act.wait_ge(s_dta, 2)
                    act.activation(dta, dta, ACT.Exp, scale=-1.0).then_inc(s_dta, 1)
                    act.wait_ge(s_dta, 3)
                    act.activation(dta, dta, ACT.Ln, bias=1.0).then_inc(s_dta, 1)
                if s == 23:
                    act.activation(rF[:, :, :], rF[:, :, :], ACT.Silu).then_inc(s_sil, 1)
                    act.wait_ge(s_cs, 1)
                    act.wait_ge(s_dtv, 6)
                    act.activation(wdec[:, 0:3, :], b[1][:, 96:192].rearrange("p (a b) -> p a b", a=3),
                                   ACT.Exp).then_inc(s_csa, 1)
                    act.activation(wdec[0:NSAMP, 3, :], b[1][0:NSAMP, 192:224], ACT.Exp).then_inc(s_csa, 1)
                    act.activation(EB, b[1][:, 224:480].rearrange("p (a b) -> p a b", a=NS),
                                   ACT.Exp).then_inc(s_csa, 1)
                    act.activation(csF[0:HEADS, :], b[2][0:HEADS, 0:T], ACT.Copy).then_inc(s_csa, 1)
                    act.wait_ge(s_csa, 4)
                    act.dma_start(d["csd"], csF[0:HEADS, :]).then_inc(s_csd, 16)
                if s == 24:
                    act.wait_ge(s_oc, 2 * GH)
                    act.wait_ge(s_kdm, 2 * GH)
                    act.wait_ge(s_gp, NL * GH)
                    act.activation(osq, oF[:, :, :], ACT.Square).then_inc(s_osq, 1)
                if 25 <= s < 28:
                    t = s - 25
                    rows = TT[t][2]
                    act.wait_ge(s_btr, t + 1)
                    act.activation(bT[0:rows, t, :], b[0][0:rows, :], ACT.Copy).then_inc(s_btc, 1)
                if s == 28:
                    act.wait_ge(s_onv, 4)
                    act.activation(rsg, rsg, ACT.Sqrt).then_inc(s_osd, 1)
            def sum_exp(q):
                act.wait_ge(s_csb[q % 2], 16 * (q // 2 + 1))
                if q >= 2:
                    act.wait_ge(s_yv, 3 * q - 4)
                for j in range(2):
                    act.activation(eb[64 * j:64 * j + 64, q % 2, :], L[64 * j:64 * j + 64, q % 2, j, P:T],
                                   ACT.Exp).then_inc(s_ebc, 1)

            act.wait_ge(s_ncv, 2 * NCONV)
            sum_exp(0)
            for q in range(PAIRS):
                for j in range(2):
                    act.wait_ge(s_L, 3 * (2 * q + j + 1))
                    act.activation(L[:, q % 2, j, :], L[:, q % 2, j, :], ACT.Exp).then_inc(s_Lx, 1)
                if q + 1 < PAIRS:
                    sum_exp(q + 1)
                before, afterwards = p3_tiles(q)
                for t in before:
                    evac(48 + t)
                act.wait_ge(s_pf, q + 1)
                if q >= 2:
                    act.wait_ge(s_pf_out[q % 2], 16 * (q // 2))
                act.activation(fin2[:, q % 2, :], b[2][:, T:T + P], ACT.Copy).then_inc(s_pfc, 1)
                for t in afterwards:
                    evac(48 + t)
                if q == 8:
                    act.wait_ge(s_cvd, 5 * NCONV)
                    act.activation(xsF[:, 12:16, :], xsF[:, 12:16, :], ACT.Silu).then_inc(s_slu, 1)

            for g in range(GROUPS):
                act.activation(zF[:, 4 * g:4 * g + 4, :], zF[:, 4 * g:4 * g + 4, :], ACT.Silu).then_inc(s_sil, 1)
            act.wait_ge(s_y, PAIRS)
            act.wait_ge(s_sm, PAIRS)
            for i in range(2):
                act.wait_ge(s_sout[i], 16 * (PAIRS // 2))
            for t in range(8):
                evac(72 + t)
                if t < GROUPS:
                    act.wait_ge(s_ysm, t + 1)
                    act.activation(zF[:, 4 * t:4 * t + 4, :], xsF[:, 4 * t:4 * t + 4, :], ACT.Square).then_inc(s_ysq, 1)
            act.wait_ge(s_ynv, 4)
            act.activation(rs4, rs4, ACT.Sqrt).then_inc(s_ysd, 1)
            for t in range(8):
                act.activation(rF[:, t, :], rF[:, t, :], ACT.Sigmoid,
                               bias=vec[:, V_MRG + t:V_MRG + 1 + t]).then_inc(s_sil, 1)
            for t in range(KT):
                act.wait_ge(s_mxv, 24 + 3 * t + 3)
                act.activation(hF[:, t, :], x2[:, t, :], ACT.Square).then_inc(s_sq, 1)
            root(2)
            shift(2, 24)

            act.wait_ge(s_set, 6)
            act.activation(spare, eps, ACT.Sigmoid)
            act.wait_ge(s_rtq, 1)
            act.activation(combF, b[1][:, 0:T], ACT.Copy).then_inc(s_rqc, 1)
            act.wait_ge(s_rtp, 1)
            act.wait_ge(s_set, 6)
            act.activation(scr[:, 0:2, :], b[0][:, 0:2 * E].rearrange("p (a b) -> p a b", a=2),
                           ACT.Sigmoid).then_inc(s_rta, 1)
            act.activation(scr[0:NSAMP, 2, :], b[0][0:NSAMP, 2 * E:3 * E], ACT.Sigmoid).then_inc(s_rta, 1)
            for n in range(6):
                t, half = divmod(n, 2)
                rows = TT[t][2]
                act.wait_ge(s_ht, n + 1)
                act.activation(hT[0:rows, t, half * 512:half * 512 + 512], b[2 + n % 4][0:rows, :],
                               ACT.Copy).then_inc(s_htc, 1)

            for n in range(12):
                t, half = divmod(n, 2)
                act.wait_ge(s_tm, n + 1)
                rows = TT[t][2] if n < 6 else NSAMP if n >= 10 else P
                dst = xT[:, t] if n < 6 else wT if n < 8 else gT[:, t - 4]
                act.activation(dst[0:rows, half * 512:half * 512 + 512], (b[4], b[5], pj[0], pj[1])[n % 4][0:rows, :],
                               ACT.Copy).then_inc(s_tmc, 1)

            with act.If(few(act)):
                def first_half(e, v):
                    act.wait_ge(s_xt2, e + 1)
                    act.activation(heF[:, v, 0:4, :], b[0][:, 0:4 * CAP].rearrange("p (k c) -> p k c", k=4),
                                   ACT.Copy).then_inc(s_hea, 1)

                first_half(0, 0)

                def two(i, first, last):
                    for v in range(2):
                        e = 2 * i + v
                        act.wait_ge(s_used, 6 * e + (C_MOE + 2))
                        if not first:
                            act.wait_ge(s_eac, e - 1)
                        act.activation(sgE[:, v, :], b[2 + v][:, 0:4 * CAP], ACT.Silu).then_inc(s_esg, 1)
                        if not (last and v):
                            first_half(e + 1, 1 - v)
                        act.wait_ge(s_used, 6 * e + (C_MOE + 5))
                        if not first:
                            act.wait_ge(s_yd[v], 16 * i)
                        act.activation(yE[0:CAP, v, 0:512], pj[0][0:CAP, :], ACT.Copy).then_inc(s_eya, 1)

                expert_pairs(act, two)
                for t, (c0, c1, rows) in enumerate(TT):
                    act.wait_ge(s_y12[t], 32)
                    act.activation(hT[0:rows, t, :], hT[0:rows, t, :], ACT.Copy,
                                   scale=sel[0:rows, 0, 6 + t:7 + t]).then_inc(s_w1, 1)
            with act.Else():
                act.wait_ge(s_xd, 16 * 6)
                act.wait_ge(s_ctr, 1)
                act.activation(combF[0:E, :], b[2][0:E, 0:T], ACT.Copy).then_inc(s_ctc, 1)
                for e in range(E):
                    act.wait_ge(s_cbb, e + 1)
                    act.activation(combB[:, e, :], b[4 + e % 2][:, 0:T], ACT.Copy).then_inc(s_cbx, 1)

                def two(i, first, last):
                    for v in range(2):
                        e = 2 * i + v
                        for f in range(4):
                            if f % 2:
                                act.wait_ge(s_used, 6 * e + (C_MOE + f // 2 + 1))
                            else:
                                act.wait_ge(s_first, 4 * e + (C_MOE + f // 2 + 1))
                            if not (first and v == 0):
                                act.wait_ge(s_au, 4 * e + (f - 3))
                            act.activation(sgt[:, f, :], b[f % 2][:, 0:T], ACT.Silu).then_inc(s_sg, 1)

                expert_pairs(act, two)
                for n in range(6):
                    t, half = divmod(n, 2)
                    rows = TT[t][2]
                    act.wait_ge(s_yt, n + 1)
                    act.activation(hT[0:rows, t, half * 512:half * 512 + 512], b[n % 2][0:rows, :],
                                   ACT.Copy).then_inc(s_ytc, 1)
            for t, (c0, c1, rows) in enumerate(TT):
                act.wait_ge(s_x3, t + 1)
                act.activation(y2[0:rows, t, :], hT[0:rows, t, :], ACT.Square,
                               accum_out=ssq[0:rows, t:t + 1]).then_inc(s_fsq, 1)
                act.wait_ge(s_fsq, t + 1)
                act.activation(ssq[0:rows, t:t + 1], ssq[0:rows, t:t + 1], ACT.Sqrt, bias=eps[0:rows, :],
                               scale=1.0 / D).then_inc(s_fsd, 1)

        @block.gpsimd
        def _(pool):
            pool.dma_start(d["xd"][XROWS:XROWS + CAP, :], d["w"][0][0:CAP // 2].rearrange("p (a c) -> (p a) c", a=2)
                           ).then_inc(s_pad, 16)

            def modulate(n, src, shift):
                h_ = hF[:, :, NP_:T]
                hs = h_.rearrange("p k (s t) -> p k s t", t=ST)
                ph = Chain(pool, s_ph, 2 * (n - 1))
                pool.wait_ge(s_rst, n)
                pool.wait_ge(s_nv, n)
                ph(pool.tensor_tensor(h_, src[:, :, NP_:T], rst[:, NP_:T].unsqueeze(1).to_broadcast([P, KT, NSAMP]),
                                      ALU.mult))
                ph.wait()
                ph(pool.tensor_tensor(hs, hs, modA[:, :, 1:].unsqueeze(3).to_broadcast([P, KT, NS, ST]), ALU.mult))
                ph.wait()
                pool.tensor_tensor(hs, hs, mod[:, shift:shift + 8, 1:].unsqueeze(3).to_broadcast([P, KT, NS, ST]),
                                   ALU.add).then_inc(s_h, 1)

            pool.wait_ge(s_ld0, 16 * 3)
            modulate(1, oF, 0)
            pool.wait_ge(s_ld3, 16)
            pool.wait_ge(s_ld2, 16 * 7)
            for s in range(N2 + 1):
                for j in (2 * s, 2 * s + 1):
                    if j < NL * GH and j % NL:
                        hd, lv, size, n = level_of(j)
                        el, eu, _ = halves(ebuf[:, j % 2, :], n, size)
                        ol, ou, _ = halves(qk[:, j % 2, :], n, size)
                        kl, _, _ = halves(kF[:, hd, :], n, size)
                        _, qu, _ = halves(qF[:, hd, :], n, size)
                        pool.wait_ge(s_gexp, 8 * hd + lv)
                        pool.wait_ge(s_ev, 16)
                        if j >= 2:
                            pool.wait_ge(s_gp, j - 1)
                        pool.tensor_tensor(ol, kl, el, ALU.mult)
                        pool.tensor_tensor(ou, qu, eu, ALU.mult).then_inc(s_gqk, 1)
                if s in F_SLOT:
                    hd = F_SLOT.index(s)
                    if hd:
                        pool.wait_ge(s_kdt, hd)
                        pool.wait_ge(s_o, hd)
                    pool.wait_ge(s_kdx, 2 * hd + 1)
                    pool.tensor_tensor(kd, kF[:, hd, :], ekd, ALU.mult).then_inc(s_kdm, 1)
                    pool.wait_ge(s_kdx, 2 * hd + 2)
                    pool.tensor_tensor(qg, qF[:, hd, NP_:T], eg, ALU.mult).then_inc(s_kdm, 1)
                ct = s - 8
                if 0 <= ct < NCONV:
                    c = chan(ct)
                    if ct >= 2:
                        pool.wait_ge(s_cvd, 5 * (ct - 1))
                    row = ext[:, ct % 2, S0:EXTW].rearrange("p (s t) -> p s t", t=SW)
                    pool.tensor_copy(row[:, :, 0:3], cvs[:, c, :].rearrange("p (s t) -> p s t", t=3)).then_inc(s_pre_x, 1)
                ct = s - 9
                if 0 <= ct < NCONV:
                    c = chan(ct)
                    pool.wait_ge(s_ev, 16 + s)
                    row = ext[:, ct % 2, :]
                    pool.tensor_copy(ncv[:, c, 0:3], row[:, S0 - 3:S0]).then_inc(s_ncv, 1)
                    pool.tensor_copy(ncv[:, c, 3:27].rearrange("p (s t) -> p s t", t=3),
                                     row[:, S0:EXTW].rearrange("p (s t) -> p s t", t=SW)[:, :, SW - 3:SW]).then_inc(s_ncv, 1)
                if s == 22:
                    pool.wait_ge(s_dtv, 4)
                    pool.tensor_tensor(dtm[0:NSAMP], dta[0:NSAMP, 2:3, :].to_broadcast([NSAMP, NS, HEADS]),
                                       seqm.unsqueeze(2).to_broadcast([NSAMP, NS, HEADS]), ALU.mult).then_inc(s_dtm, 1)
            for q in range(PAIRS):
                g = q // PPG
                if q % PPG == 0:
                    if q:
                        pool.wait_ge(s_sn, 2 * q)
                    else:
                        pool.wait_ge(s_btc, 3)
                        pool.wait_ge(s_gs, 4 * GH)
                        pool.wait_ge(s_o, GH)
                        for i in range(2):
                            pool.wait_ge(s_sgo[i], 16 * 8)
                        pool.wait_ge(s_pst, 16 * GH)
                        pool.wait_ge(s_cvd, 5 * NCONV)
                        pool.wait_ge(s_kdc, 2 * GH)
                        pool.wait_ge(s_gsa, 8 * GH)
                        pool.wait_ge(s_csa, 4)
                    pool.tensor_tensor(bm[0:NSAMP], bT[0:NSAMP, 2:3, g * P:g * P + P].to_broadcast([NSAMP, NS, P]),
                                       seqm.unsqueeze(2).to_broadcast([NSAMP, NS, P]), ALU.mult).then_inc(s_bm, 1)
                x_ = xdt[:, q % 2]
                o_ = xdd[:, q % 2]
                hs = slice(2 * q, 2 * q + 2)

                def byhead(a):
                    return a.rearrange("p a (h c) -> p a h c", h=2)

                pool.wait_ge(s_xdt, 2 * q + 2)
                if q >= 2:
                    pool.wait_ge(s_sn, 2 * (q - 1))
                pool.tensor_tensor(byhead(o_[:, 0:2]), byhead(x_[:, 0:2]),
                                   wdec[:, 0:2, hs].unsqueeze(3).to_broadcast([P, 2, 2, HD]), ALU.mult).then_inc(s_xdd, 1)
                pool.tensor_tensor(byhead(o_[:, 2:3]), byhead(x_[:, 0:1]),
                                   wdec[:, 2:3, hs].unsqueeze(3).to_broadcast([P, 1, 2, HD]), ALU.mult).then_inc(s_xdd, 1)
                pool.tensor_tensor(byhead(o_[0:NSAMP, 3:4]), byhead(x_[0:NSAMP, 2:3]),
                                   wdec[0:NSAMP, 3:4, hs].unsqueeze(3).to_broadcast([NSAMP, 1, 2, HD]),
                                   ALU.mult).then_inc(s_xdd, 1)
                pool.wait_ge(s_sin[q % 2], 16 * (q // 2 + 1))
                if q >= 2:
                    pool.wait_ge(s_sout[q % 2], 16 * (q // 2))
                pool.tensor_tensor(byhead(so[:, q % 2]), byhead(sn[:, q % 2]),
                                   EB[:, :, hs].unsqueeze(3).to_broadcast([P, NS, 2, HD]), ALU.mult).then_inc(s_sm, 1)
                if q == 1:
                    pool.wait_ge(s_onv, 13)
                    pool.wait_ge(s_sil, 1)
                    pool.tensor_tensor(oF[:, :, :], oF[:, :, :], rF[:, :, :], ALU.mult).then_inc(s_og, 1)
            pool.wait_ge(s_mxv, 48)
            modulate(2, x2, 24)
            pool.wait_ge(s_dsp, DISPATCH_STEPS)
            pool.wait_ge(s_htc, 6)
            for t, (c0, c1, rows) in enumerate(TT):
                for j in range(TOP):
                    pool.indirect_dma_start(out=d["xd"][:, :],
                                            out_offset=bass.IndirectOffsetOnAxis(ap=idx[0:rows, j, t:t + 1], axis=0),
                                            in_=hT[0:rows, t, :], in_offset=None).then_inc(s_xd, 16)

            with pool.If(few(pool)):
                for v in range(2):
                    pool.wait_ge(s_yd[v], 16 * (E // 2))
                pool.wait_ge(s_xd, 16 * 6)
                for t, (c0, c1, rows) in enumerate(TT):
                    for j, dst in enumerate((hT, y2)):
                        pool.indirect_dma_start(out=dst[0:rows, t, :], out_offset=None,
                                                in_=d["yd"].rearrange("e r c -> (e r) c"),
                                                in_offset=bass.IndirectOffsetOnAxis(ap=idx[0:rows, j, 3 + t:4 + t], axis=0)
                                                ).then_inc(s_y12[t], 16)
            with pool.Else():
                pool.wait_ge(s_cbx, E)
                for e in range(E):
                    for f in range(4):
                        pool.wait_ge(s_au, 4 * e + f + 1)
                        pool.tensor_tensor(actF[:, e % 2, f, :], actF[:, e % 2, f, :], combB[:, e, :],
                                           ALU.mult).then_inc(s_ac, 1)

            for t, (c0, c1, rows) in enumerate(TT):
                pool.wait_ge(s_gm, t + 1)
                pool.tensor_tensor(hT[0:rows, t, :], hT[0:rows, t, :], xT[0:rows, t, :], ALU.add).then_inc(s_x3, 1)

        def masked_cb(dve, g):
            dve.wait_ge(s_cb, g + 1)
            o_ = cbm[:, g % 2, :]
            if g == 0:
                for i in range(2):
                    dve.memset(cbm[64:P, i, NP_:T], 0.0)
            dve.tensor_tensor(o_[:, 0:NP_], b[3][:, 0:NP_], cmask[:, 0:NP_], ALU.mult).then_inc(s_cbc, 1)
            dve.tensor_tensor(o_[0:NSAMP, NP_:T], b[3][0:NSAMP, NP_:T], cmask[0:NSAMP, NP_:T], ALU.mult).then_inc(s_cbc, 1)
            dve.tensor_copy(o_[:, T:T + P], b[3][:, T:T + P]).then_inc(s_cbc, 1)

        @block.vector
        def _(dve):
            nv = Chain(dve, s_nv)
            st = Chain(dve, s_set)
            st(dve.memset(scF[:, :, :], 0.0))
            st(dve.memset(wr[:, :, :], 0.0))
            st(dve.memset(dtx, 0.0))
            for i in range(2):
                st(dve.memset(ext[:, i, 0:3], 0.0))

            def norm(n, src=None):
                if src is not None:
                    dve.tensor_tensor(hF[:, :, :], src, src, ALU.mult).then_inc(s_nsq, 1)
                dve.wait_ge(s_nsd, n)
                dve.reciprocal(rst[:, :], rst[:, :]).then_inc(s_rst, 1)
                dve.wait_ge(s_rst, n)

            def scales(base, w):
                nv(dve.scalar_tensor_tensor(modA[:, :, :], mod[:, base:base + 8, :], 1.0,
                                            vec[:, w:w + 8].unsqueeze(2).to_broadcast([P, KT, NSEQ]), ALU.add, ALU.mult))
                nv.wait()

            def modulate(src):
                for k in range(KT):
                    dve.scalar_tensor_tensor(hF[:, k, 0:NP_], src[:, k, 0:NP_], modA[:, k, 0:1], rst[:, 0:NP_],
                                             ALU.mult, ALU.mult).then_inc(s_hk, 1)

            dve.wait_ge(s_ld0, 16 * 3)
            norm(1, oF[:, :, :])
            dve.wait_ge(s_adt, 8)
            dve.tensor_tensor(mod[:, 0:16, :], b[5][:, 0:16 * NSEQ].rearrange("p (a b) -> p a b", b=NSEQ),
                              vec[:, 0:16].unsqueeze(2).to_broadcast([P, 16, NSEQ]), ALU.add).then_inc(s_mod, 1)
            dve.wait_ge(s_mod, 1)
            scales(8, V_N1)
            modulate(oF)

            for hd in range(GH):
                dve.wait_ge(s_gate, hd + 1)
                dve.tensor_scalar(gx[:, hd, :], b[2 + hd % 2][:, 0:T], vec[:, V_GB + hd:V_GB + hd + 1], None,
                                  ALU.add).then_inc(s_gxv, 1)
            dve.wait_ge(s_gxv, 4)
            dve.wait_ge(s_gxa, 3)
            dve.scalar_tensor_tensor(gx, gx, 0.0, gax, ALU.min, ALU.subtract).then_inc(s_gxv, 1)
            dve.wait_ge(s_gxv, 5)
            dve.wait_ge(s_ld3, 16)
            for hd in range(GH):
                dve.tensor_tensor_scan(gF[:, hd, :], reset, gx[:, hd, :], 0.0, ALU.mult, ALU.add).then_inc(s_gxv, 1)
            for v in range(8):
                dve.wait_ge(s_vtr, v + 1)
                dve.tensor_copy(vT[:, 0:2, v * P:v * P + P],
                                b[4][:, 0:2 * P].rearrange("p (a b) -> p a b", a=2)).then_inc(s_vcp, 1)
                dve.tensor_copy(vT[0:NSAMP, 2, v * P:v * P + P], b[4][0:NSAMP, 2 * P:3 * P]).then_inc(s_vcp, 1)
            dve.wait_ge(s_gxv, 9)
            dve.wait_ge(s_ld2, 16 * 7)

            def exponents(j):
                hd, lv, size, n = level_of(j)
                if not lv:
                    return
                if j >= 2 and 8 * hd + lv > 2:
                    dve.wait_ge(s_gqk, len([i for i in range(j - 1) if i % NL]))
                lo, up, v = halves(gF[:, hd, :], n, size)
                el, eu, _ = halves(ebuf[:, j % 2, :], n, size)
                mid = v[:, :, size // 2 - 1:size // 2].to_broadcast([P, n // size, size // 2])
                dve.tensor_tensor(eu, up, mid, ALU.subtract)
                dve.tensor_tensor(el, mid, lo, ALU.subtract).then_inc(s_ge, 1)

            def merge(j):
                hd, lv, size, n = level_of(j)
                a = att[:, hd % 2, :]
                bank = b[j % 2]
                dve.wait_ge(s_gp, j + 1)
                if lv == 0:
                    if hd >= 2:
                        dve.wait_ge(s_o, hd - 1)
                    dve.tensor_tensor(a[:, 0:NP_], bank[:, 0:NP_], dmask[:, 0:NP_], ALU.mult)
                    dve.tensor_tensor(a[0:NSAMP, NP_:T], bank[0:NSAMP, NP_:T], dmask[0:NSAMP, NP_:T],
                                      ALU.mult).then_inc(s_gcp, 1)
                    return
                dve.wait_ge(s_gcp, j)
                if size == 256:
                    dve.tensor_copy(a[:, T:T + P], bank[:, 0:P]).then_inc(s_gcp, 1)
                    return
                m = lvm[:, MASKED.index(size), :]
                ins = dve.copy_predicated(a[:, 0:NP_], m[:, 0:NP_], bank[:, 0:NP_])
                if size <= ST:
                    ins = dve.copy_predicated(a[0:NSAMP, NP_:T], m[0:NSAMP, NP_:T], bank[0:NSAMP, NP_:T])
                ins.then_inc(s_gcp, 1)

            def new_states(hd, bp):
                dve.wait_ge(s_gs, 4 * hd + bp + 1)
                dve.wait_ge(s_sgi, 16 * (hd + 1))
                dve.wait_ge(s_kdx, 2 * hd + 2)
                n = 2 * hd + bp // 2
                if n:
                    dve.wait_ge(s_sgo[bp % 2], 16 * n)
                for j in range(2):
                    s = 2 * bp + j
                    dve.scalar_tensor_tensor(sgo[:, bp % 2, j, :], sgi[:, s, :], eg[:, ST * s + ST - 1:ST * s + ST],
                                             b[4][:, j * GDV:(j + 1) * GDV], ALU.mult, ALU.add).then_inc(s_gsa, 1)

            def conv(ct):
                c = chan(ct)
                row = ext[:, ct % 2, :]
                dst = bcF[:, ct, :] if ct < 8 else xsF[:, ct - 8, :]
                w = [vec[:, V_CW + i * NCONV + c:V_CW + i * NCONV + c + 1] for i in range(CONVK)]
                n = EXTW - 3
                dve.wait_ge(s_ev, 25 + ct)
                dve.wait_ge(s_pre_x, ct + 1)
                cv = Chain(dve, s_cvd, 5 * ct)
                if ct == 0:
                    st.wait()
                else:
                    cv.wait()
                cv(dve.tensor_scalar(cvo[:, 0:n], row[:, 0:n], w[0], vec[:, V_CB + c:V_CB + c + 1],
                                     ALU.mult, ALU.add))
                for i in (1, 2):
                    cv.wait()
                    cv(dve.scalar_tensor_tensor(cvo[:, 0:n], row[:, i:i + n], w[i], cvo[:, 0:n], ALU.mult, ALU.add))
                cv.wait()
                cv(dve.scalar_tensor_tensor(dst[:, 0:NP_], row[:, 3:S0], w[3], cvo[:, 0:NP_], ALU.mult, ALU.add))
                cv(dve.scalar_tensor_tensor(
                    seqs(dst), row[:, S0:EXTW].rearrange("p (s t) -> p s t", t=SW)[:, :, 3:SW], w[3],
                    cvo[:, S0:S0 + NS * SW].rearrange("p (s t) -> p s t", t=SW)[:, :, 0:ST], ALU.mult, ALU.add))

            on = Chain(dve, s_onv)
            for s in range(N2 + 1):
                for j in (2 * s - 2, 2 * s - 1):
                    if 0 <= j < NL * GH:
                        merge(j)
                for hd in range(GH):
                    if s == F_SLOT[hd] + 3:
                        new_states(hd, 1)
                        new_states(hd, 2)
                    if s == F_SLOT[hd] + 4:
                        new_states(hd, 3)
                for j in (2 * s, 2 * s + 1):
                    if j < NL * GH:
                        exponents(j)
                if s in F_SLOT:
                    hd = F_SLOT.index(s)
                    g_ = gF[:, hd, :]
                    if hd:
                        dve.wait_ge(s_kdm, 2 * hd)
                    dve.tensor_scalar(ekd[:, 0:NP_], g_[:, 0:NP_], g_[:, NP_ - 1:NP_], -1.0, ALU.subtract, ALU.mult)
                    dve.tensor_tensor(seqs(ekd), seqs(g_)[:, :, ST - 1:ST].to_broadcast([P, NS, ST]), seqs(g_),
                                      ALU.subtract).then_inc(s_kde, 1)
                for hd in range(GH):
                    if s == F_SLOT[hd] + 1:
                        dve.wait_ge(s_kdt, hd + 1)
                        if hd:
                            dve.wait_ge(s_gs, 4 * hd)
                            dve.wait_ge(s_gpf, hd)
                        dve.tensor_copy(kdT, b[4][:, 0:2 * P].rearrange("p (a b) -> p a b", a=2)).then_inc(s_kdc, 1)
                        dve.tensor_tensor(kdm[0:NSAMP], b[4][0:NSAMP, 2 * P:3 * P].unsqueeze(1).to_broadcast([NSAMP, NS, P]),
                                          seqm.unsqueeze(2).to_broadcast([NSAMP, NS, P]), ALU.mult).then_inc(s_kdc, 1)
                    if s == F_SLOT[hd] + 2:
                        new_states(hd, 0)
                if 0 <= s - 9 < NCONV:
                    conv(s - 9)
                if s == 21:
                    dve.wait_ge(s_dtp, 1)
                    dve.tensor_tensor(dtx[:, 0:2, :], b[0][:, 0:64].rearrange("p (a b) -> p a b", a=2),
                                      dtb[:, :].unsqueeze(1).to_broadcast([P, 2, HEADS]), ALU.add).then_inc(s_dtv, 1)
                    dve.tensor_tensor(dtx[0:NSAMP, 2, :], b[0][0:NSAMP, 64:96], dtb[0:NSAMP, :], ALU.add).then_inc(s_dtv, 1)
                if s == 22:
                    dve.wait_ge(s_dtv, 2)
                    dve.wait_ge(s_dta, 4)
                    dve.scalar_tensor_tensor(dtx, dtx, 0.0, dta, ALU.max, ALU.add).then_inc(s_dtv, 1)
                    dve.wait_ge(s_dtv, 3)
                    dve.scalar_tensor_tensor(dta, dtx, -1.0, aex[:, :].unsqueeze(1).to_broadcast([P, 3, HEADS]),
                                             ALU.mult, ALU.mult).then_inc(s_dtv, 1)
                if s == 23:
                    dve.wait_ge(s_cs, 1)
                    dve.tensor_copy(csT[:, 0:2, :], b[1][:, 0:64].rearrange("p (a b) -> p a b", a=2)).then_inc(s_dtv, 1)
                    dve.tensor_copy(csT[0:NSAMP, 2, :], b[1][0:NSAMP, 64:96]).then_inc(s_dtv, 1)
                if s == 24:
                    dve.wait_ge(s_gpf, GH)
                    dve.wait_ge(s_gs, 4 * GH)
                if s in (26, 27):
                    for j in range(2):
                        hd = 2 * (s - 26) + j
                        dve.wait_ge(s_oss, hd + 1)
                        if hd == 0:
                            dve.wait_ge(s_kdx, 2 * GH)
                        on(dve.tensor_scalar(rsg[:, hd, :], b[1 + j][:, 0:T], 1.0 / GDV, EPS, ALU.mult, ALU.add))
                if s == 28:
                    masked_cb(dve, 0)
                if s == 29:
                    dve.wait_ge(s_osd, 1)
                    on(dve.reciprocal(rsg, rsg))
                if s in (30, 31):
                    on.wait()
                    for hd in (2 * s - 60, 2 * s - 59):
                        for v in range(2):
                            o_ = oF[:, 2 * hd + v, :]
                            on(dve.scalar_tensor_tensor(o_, o_, vec[:, V_GN + v:V_GN + v + 1], rsg[:, hd, :],
                                                        ALU.mult, ALU.mult))
                if s and s % 2 == 0:
                    c = 7 + s // 2
                    dve.wait_ge(s_adt, c + 1)
                    dve.tensor_tensor(mod[:, 2 * c:2 * c + 2, :], b[5][:, 256:256 + 2 * NSEQ].rearrange("p (a b) -> p a b", b=NSEQ),
                                      vec[:, 2 * c:2 * c + 2].unsqueeze(2).to_broadcast([P, 2, NSEQ]),
                                      ALU.add).then_inc(s_mod, 1)
            for q in range(PAIRS):
                g = q // PPG
                x_ = xdt[:, q % 2]
                hs = slice(2 * q, 2 * q + 2)
                dve.wait_ge(s_xt, q + 1)
                if q >= 2:
                    dve.wait_ge(s_y, q - 1)
                    dve.wait_ge(s_xdd, 3 * (q - 1))
                elif q == 0:
                    dve.wait_ge(s_ncv, 2 * NCONV)
                    dve.wait_ge(s_pst, 16 * GH)
                dve.tensor_tensor(x_[:, 0:2].rearrange("p a (h c) -> p a h c", h=2),
                                  b[0][:, 0:2 * P].rearrange("p (a h c) -> p a h c", a=2, h=2),
                                  dtx[:, 0:2, hs].unsqueeze(3).to_broadcast([P, 2, 2, HD]), ALU.mult).then_inc(s_xdt, 1)
                dve.tensor_tensor(x_[0:NSAMP, 2].rearrange("p (h c) -> p h c", h=2),
                                  b[0][0:NSAMP, 2 * P:3 * P].rearrange("p (h c) -> p h c", h=2),
                                  dtx[0:NSAMP, 2, hs].unsqueeze(2).to_broadcast([NSAMP, 2, HD]), ALU.mult).then_inc(s_xdt, 1)
                for j in range(2):
                    h = 2 * q + j
                    dve.wait_ge(s_csb[q % 2], 16 * (q // 2 + 1))
                    dve.wait_ge(s_ebc, 2 * q + 2)
                    for t, (c0, c1, rows) in enumerate(TT):
                        dve.tensor_scalar(L[0:rows, q % 2, j, c0:c1], L[0:rows, q % 2, j, c0:c1], csT[0:rows, t, h:h + 1], 0.0,
                                          ALU.subtract, ALU.min).then_inc(s_L, 1)
                for j in range(2):
                    h = 2 * q + j
                    dve.wait_ge(s_Lx, h + 1)
                    dve.wait_ge(s_cbc, 3 * g + 3)
                    dve.tensor_tensor(L[:, q % 2, j, :], L[:, q % 2, j, :], cbm[:, g % 2, 0:T], ALU.mult).then_inc(s_M, 1)
                yv = Chain(dve, s_yv, 3 * q)
                dve.wait_ge(s_y, q + 1)
                dve.wait_ge(s_ebc, 2 * q + 2)
                if q:
                    yv.wait()
                yv(dve.scalar_tensor_tensor(xsF[:, q, :], xsF[:, q, :], vec[:, V_DS + q:V_DS + q + 1], b[4][:, 0:T],
                                            ALU.mult, ALU.add))
                yv(dve.tensor_tensor(t2, b[4][:, T:512], eb[:, q % 2, :], ALU.mult))
                yv.wait()
                yv(dve.tensor_tensor(xsF[:, q, P:T], xsF[:, q, P:T], t2, ALU.add))
                dve.wait_ge(s_sm, q + 1)
                for half in range(2):
                    dve.wait_ge(s_sn, 2 * q + half + 1)
                    bank = b[5] if half == 0 else b[3]
                    o_ = so[:, q % 2, 4 * half:4 * half + 4]
                    dve.tensor_tensor(o_, o_, bank[:, :].rearrange("p (a b) -> p a b", a=4), ALU.add).then_inc(s_sa, 1)
                if q % PPG == PPG - 1 and g + 1 < GROUPS:
                    masked_cb(dve, g + 1)

            dve.wait_ge(s_yv, 3 * PAIRS)
            for g in range(GROUPS):
                dve.wait_ge(s_sil, 2 + g)
                y_ = xsF[:, 4 * g:4 * g + 4, :]
                dve.tensor_tensor(y_, y_, zF[:, 4 * g:4 * g + 4, :], ALU.mult).then_inc(s_ysm, 1)
            dve.wait_ge(s_ysm, GROUPS)
            yn = Chain(dve, s_ynv)
            for i in range(2):
                dve.wait_ge(s_sout[i], 16 * (PAIRS // 2))
            dve.wait_ge(s_ev, 80)
            mv = Chain(dve, s_mxv)
            for t in range(8):
                dve.wait_ge(s_used if t % 2 else s_first, C_GLA + t // 2 + 1)
                mv(dve.tensor_tensor(gbF[:, t, :], gbF[:, t, :], pj[t % 2][:, 0:T], ALU.mult))
                if t == 2:
                    for g in range(GROUPS):
                        dve.wait_ge(s_yss, g + 1)
                        yn(dve.tensor_scalar(rs4[:, g, :], b[g][:, 0:T], 1.0 / 512, EPS, ALU.mult, ALU.add))
                if t in (3, 4):
                    if t == 3:
                        dve.wait_ge(s_ysd, 1)
                    yn(dve.reciprocal(rs4[:, 2 * t - 6:2 * t - 4], rs4[:, 2 * t - 6:2 * t - 4]))
                if t in (5, 6, 7):
                    if t == 5:
                        yn.wait()
                    for u in ((0, 1, 2, 3, 4, 5), (6, 7, 8, 9, 10), (11, 12, 13, 14, 15))[t - 5]:
                        y_ = xsF[:, u, :]
                        yn(dve.scalar_tensor_tensor(y_, y_, vec[:, V_SSDN + u:V_SSDN + u + 1], rs4[:, u // 4, :],
                                                    ALU.mult, ALU.mult))
            for t in range(8):
                dve.wait_ge(s_used if t % 2 else s_first, C_SSD + 2 * (t // 2) + 2)
                dve.wait_ge(s_sil, 6 + t)
                mv(dve.tensor_tensor(rF[:, t, :], rF[:, t, :], pj[t % 2][:, 0:T], ALU.mult))
                mv.wait()
                mv(dve.tensor_tensor(gbF[:, t, :], gbF[:, t, :], rF[:, t, :], ALU.add))
            dve.wait_ge(s_x, 16)
            dve.wait_ge(s_mod, 17)
            scales(32, V_N2)
            dve.tensor_copy(gsx.rearrange("p k (s t) -> p k s t", t=ST),
                            mod[:, 40:48, 1:].unsqueeze(3).to_broadcast([P, KT, NS, ST])).then_inc(s_gsx, 1)

            def residual(src, base, t, chain, tmp):
                x_ = x2[:, t, :]
                chain(dve.scalar_tensor_tensor(x_[:, 0:NP_], src[:, 0:NP_], mod[:, base + t, 0:1], x_[:, 0:NP_],
                                               ALU.mult, ALU.add))
                chain(dve.tensor_tensor(seqs(tmp), seqs(src), mod[:, base + t, 1:].unsqueeze(2).to_broadcast([P, NS, ST]),
                                        ALU.mult))
                chain.wait()
                chain(dve.tensor_tensor(seqs(x_), seqs(x_), seqs(tmp), ALU.add))

            for t in range(8):
                dve.wait_ge(s_used if t % 2 else s_first, C_OUT + t // 2 + 1)
                residual(pj[t % 2], 16, t, mv, rs4[:, t % 2, :])
            mv.wait()
            dve.memset(os_, 0.0)
            st(dve.memset(scr, 0.5))
            norm(2)
            modulate(x2)

            rt = Chain(dve, s_rtv)

            def step(ins):
                rt(ins)
                rt.wait()

            def first_largest(out, val, w, prio, tmp):
                step(dve.tensor_reduce(mx, val, AX.X, ALU.max))
                step(dve.tensor_tensor(tmp, val, mx.to_broadcast([P, 3, w]), ALU.is_equal))
                step(dve.tensor_tensor(tmp, tmp, prio.unsqueeze(1).to_broadcast([P, 3, w]), ALU.mult))
                step(dve.tensor_reduce(mx2, tmp, AX.X, ALU.max))
                step(dve.tensor_tensor(out, tmp, mx2.to_broadcast([P, 3, w]), ALU.is_equal))

            def flat(a):
                return a.rearrange("p a b -> p (a b)")

            bie = flat(bi).rearrange("p (a b) -> p a b", a=3)
            dve.wait_ge(s_rta, 2)
            st.wait()
            step(dve.tensor_tensor(bie, scr, rb[:, :].unsqueeze(1).to_broadcast([P, 3, E]), ALU.add))
            step(dve.tensor_tensor(pair[:, :, 0:3], bi[:, :, 0:3], bi[:, :, 1:4], ALU.add))
            step(dve.tensor_tensor(pair[:, :, 3:5], bi[:, :, 0:2], bi[:, :, 2:4], ALU.add))
            step(dve.tensor_tensor(pair[:, :, 5:6], bi[:, :, 0:1], bi[:, :, 3:4], ALU.add))
            step(dve.tensor_reduce(flat(gsc).unsqueeze(2), pair, AX.X, ALU.max))
            first_largest(gone, gsc, EG, prio4, geq)
            mb4 = flat(mb).rearrange("p (a b) -> p a b", a=12)
            step(dve.tensor_tensor(mb4, bi, flat(gone).unsqueeze(2).to_broadcast([P, 12, EPG]), ALU.mult))
            step(dve.tensor_scalar(gone, gone, 1.0, -NEG, ALU.subtract, ALU.mult))
            step(dve.tensor_tensor(mb4, mb4, flat(gone).unsqueeze(2).to_broadcast([P, 12, EPG]), ALU.add))
            first_largest(o1, mb, E, prio16, eq)
            step(dve.scalar_tensor_tensor(mb, o1, NEG, mb, ALU.mult, ALU.add))
            first_largest(o2, mb, E, prio16, eq)
            dve.tensor_tensor(os_[:, 0:2], o1[:, 0:2], o2[:, 0:2], ALU.add)
            step(dve.tensor_tensor(os_[0:NSAMP, 2], o1[0:NSAMP, 2], o2[0:NSAMP, 2], ALU.add))
            assert rt.n == ROUTER_OS, rt.n
            step(dve.tensor_tensor(mb, o1, o2, ALU.add))
            step(dve.tensor_tensor(mb, mb, scr, ALU.mult))
            step(dve.tensor_reduce(mx, mb, AX.X, ALU.add))
            step(dve.reciprocal(mx, mx))
            step(dve.tensor_tensor(comb.rearrange("p (a b) -> p a b", a=3), mb, mx.to_broadcast([P, 3, E]), ALU.mult))

            ds_ = Chain(dve, s_dsp)

            def dstep(ins):
                ds_(ins)
                ds_.wait()

            dve.wait_ge(s_rank, 1)
            ranks = b[1][:, 64:64 + 3 * E].rearrange("p (a b) -> p a b", a=3)
            dstep(dve.tensor_copy(cnt, b[1][:, 64 + 3 * E:64 + 4 * E]))
            dstep(dve.tensor_tensor_scan(cin, ones[:, 0:E], cnt, 0.0, ALU.mult, ALU.add))
            dstep(dve.tensor_tensor(mf[:, 0:E], cin, cnt, ALU.subtract))
            dstep(dve.tensor_reduce(mf[:, E:E + 1], cnt, AX.X, ALU.max))
            dstep(dve.tensor_copy(meta[:, :], mf))
            assert ds_.n == DISPATCH_META, ds_.n
            for n, first_row in ((0, mf[:, 0:E]), (1, yrow)):
                dstep(dve.tensor_tensor(pos[:, n].rearrange("p (a b) -> p a b", a=3), ranks,
                                        first_row.unsqueeze(1).to_broadcast([P, 3, E]), ALU.add))
            for j, o_ in enumerate((o1, o2)):
                dstep(dve.tensor_tensor(picks, pos, flat(o_).unsqueeze(1).to_broadcast([P, 3, 3 * E]), ALU.mult))
                dstep(dve.tensor_reduce(sel[:, j, :].unsqueeze(2),
                                        picks.rearrange("p a (b c) -> p (a b) c", b=3), AX.X, ALU.add))
            dstep(dve.tensor_scalar(sel[:, :, 0:6], sel[:, :, 0:6], -1.0, None, ALU.add))
            dstep(dve.tensor_copy(idx[:, :, :], sel[:, :, 0:6]))
            assert ds_.n == DISPATCH_STEPS, ds_.n

            cm = Chain(dve, s_cmb)

            def gated(t, rows):
                if cm.n:
                    cm.wait()
                y_ = hT[0:rows, t, :]
                dve.tensor_tensor(y_, y_, gT[0:rows, t // 2, :], ALU.mult).then_inc(s_gm, 1)

            with dve.If(few(dve)):
                def second_half(e, v):
                    dve.wait_ge(s_xt2, e + 1)
                    dve.tensor_copy(heF[:, v, 4:8, :], b[1][:, 0:4 * CAP].rearrange("p (k c) -> p k c", k=4)
                                    ).then_inc(s_hev, 1)

                second_half(0, 0)

                def two(i, first, last):
                    for v in range(2):
                        e = 2 * i + v
                        dve.wait_ge(s_used, 6 * e + (C_MOE + 4))
                        dve.wait_ge(s_esg, e + 1)
                        dve.tensor_tensor(actE[:, v, :], sgE[:, v, :], b[4 + v][:, 0:4 * CAP], ALU.mult).then_inc(s_eac, 1)
                        if not (last and v):
                            second_half(e + 1, 1 - v)
                        dve.wait_ge(s_used, 6 * e + (C_MOE + 6))
                        if not first:
                            dve.wait_ge(s_yd[v], 16 * i)
                        dve.tensor_copy(yE[0:CAP, v, 512:1024], pj[1][0:CAP, :]).then_inc(s_eyv, 1)

                expert_pairs(dve, two)
                for t, (c0, c1, rows) in enumerate(TT):
                    dve.wait_ge(s_w1, t + 1)
                    cm(dve.scalar_tensor_tensor(hT[0:rows, t, :], y2[0:rows, t, :], sel[0:rows, 1, 6 + t:7 + t],
                                                hT[0:rows, t, :], ALU.mult, ALU.add))
                    gated(t, rows)
            with dve.Else():
                dve.wait_ge(s_tm, 12)
                def two(i, first, last):
                    for v in range(2):
                        e = 2 * i + v
                        for f in range(4):
                            if not first:
                                dve.wait_ge(s_used, 6 * e + (C_MOE - 6))
                            dve.wait_ge(s_sg, 4 * e + (f + 1))
                            if f % 2:
                                dve.wait_ge(s_used, 6 * e + (C_MOE + 3 + f // 2))
                            else:
                                dve.wait_ge(s_first, 4 * e + (C_MOE + 3 + f // 2))
                            dve.tensor_tensor(actF[:, v, f, :], sgt[:, f, :], b[2 + f % 2][:, 0:T],
                                              ALU.mult).then_inc(s_au, 1)
                        for t in range(8):
                            down_done(dve, e, t // 4, t % 4)
                            if first and v == 0:
                                dve.tensor_copy(yacc[:, t, :], pj[t % 2][:, 0:T]).then_inc(s_ya, 1)
                            else:
                                if t == 0:
                                    dve.wait_ge(s_ya, 8 * e)
                                dve.tensor_tensor(yacc[:, t, :], yacc[:, t, :], pj[t % 2][:, 0:T], ALU.add).then_inc(s_ya, 1)

                expert_pairs(dve, two)
                cm.n = 0
                for t, (c0, c1, rows) in enumerate(TT):
                    dve.wait_ge(s_ytc, 2 * t + 2)
                    gated(t, rows)
            for t, (c0, c1, rows) in enumerate(TT):
                dve.wait_ge(s_fsd, t + 1)
                dve.reciprocal(ssq[0:rows, t:t + 1], ssq[0:rows, t:t + 1]).then_inc(s_frc, 1)
                dve.wait_ge(s_frc, t + 1)
                y_ = hT[0:rows, t, :]
                dve.scalar_tensor_tensor(y_, y_, ssq[0:rows, t:t + 1], wT[0:rows, :], ALU.mult, ALU.mult).then_inc(s_f, 1)


def constants():
    c = np.zeros((P, NC), np.float32)
    i = np.arange(P)
    c[:, C_ID:C_ID + P] = np.eye(P)
    c[:, C_U:C_U + P] = i[:, None] <= i[None, :]
    c[:, C_R:C_R + P] = i[:, None] > i[None, :]
    c[:, C_ONE:C_ONE + P] = 1
    s = np.arange(NSAMP)
    same = (s[:, None] // ST) == (s[None, :] // ST)
    us = same & (s[:, None] <= s[None, :])
    c[:, C_CM:C_CM + P] = c[:, C_CM + P:C_CM + 2 * P] = c[:, C_U:C_U + P]
    c[:NSAMP, C_CM + 2 * P:C_CM + T] = us
    c[:, C_DM:C_DM + P] = c[:, C_DM + P:C_DM + 2 * P] = np.eye(P)
    c[:NSAMP, C_DM + 2 * P:C_DM + T] = np.eye(NSAMP)
    r = np.ones(T, np.float32)
    r[0] = 0
    r[NP_::ST] = 0
    c[:, C_RS:C_RS + T] = r
    c[:NSAMP, C_US:C_US + NSAMP] = us
    c[:NSAMP, C_RSS:C_RSS + NSAMP] = same & (s[:, None] > s[None, :])
    c[:NSAMP, C_SEQ:C_SEQ + NS] = (s[:, None] // ST) == np.arange(NS)[None, :]
    c[:, C_PR:C_PR + 16] = 16 - np.arange(16)
    c[:, C_PR + 16:C_PR + 20] = 4 - np.arange(4)
    c[:, C_YR:C_YR + E] = CAP * np.arange(E)
    c[:, C_EPS] = EPS
    c[:, C_QE:C_QE + E] = i[:, None] % QUAD == np.arange(E)
    c[:, C_QS:C_QS + NSEQ] = i[:, None] % QUAD == np.arange(NSEQ)
    m = np.zeros((P, len(MASKED), T), np.uint8)
    for n, size in enumerate(MASKED):
        blk = (i[:, None] // size == i[None, :] // size) & (i[:, None] % size < size // 2) & (i[None, :] % size >= size // 2)
        m[:, n, 0:P] = m[:, n, P:2 * P] = blk
        if size <= ST:
            m[:NSAMP, n, NP_:T] = blk[:NSAMP, :NSAMP]
    return c, m.reshape(P, -1).view(np.int32)


def kernel(**inputs):
    import concourse.bacc as _bacc
    from concourse.bass_utils import run_bass_kernel_spmd as _run

    a = {k: np.asarray(v) for k, v in inputs.items()}

    def cols(w):
        k, c = w.shape
        return w.reshape(k // P, P, c // 256, 256).transpose(2, 1, 0, 3).reshape(c // 256, P, -1)

    w_in, ada = a["w_in"][0], cols(a["w_ada"][0])
    gla, out = cols(a["w_gla_br"][0]), cols(a["w_out"][0])
    ssd = [cols(a["w_ssd_br"][0][h * D:(h + 1) * D]) for h in range(2)]
    w = np.empty((N_CHUNK, P, CH), np.float32)
    for n, c in enumerate(ORDER):
        if c[0] == "in":
            w[n] = cols(w_in[:, c[1]:c[1] + 256])[0]
        elif c[0] == "ada":
            w[n] = ada[c[1]]
        elif c[0] == "gla":
            w[n] = gla[c[1]]
        elif c[0] == "ssd":
            w[n] = ssd[c[2]][c[1]]
        elif c[0] == "out":
            w[n] = out[c[1]]
        elif c[0] == "gate":
            w[n] = cols(a["w_exp_gate"][0, c[1]][:, 256 * c[2]:256 * c[2] + 256])[0]
        elif c[0] == "up":
            w[n] = cols(a["w_exp_up"][0, c[1]][:, 256 * c[2]:256 * c[2] + 256])[0]
        else:
            w[n] = a["w_exp_down"][0, c[1]][:, 512 * c[2]:512 * c[2] + 512].reshape(4, P, 512).transpose(1, 0, 2).reshape(P, CH)

    def fmajor(v):
        return v.reshape(v.shape[0], -1, P).transpose(2, 1, 0)

    x = np.concatenate([a["x_prompt"][0], a["x_sample"].reshape(NSAMP, D)])
    c = np.concatenate([a["c_prompt"], a["c_sample"]])
    ds = np.repeat(a["d_skip"][0].reshape(PAIRS, 2), HD, axis=1)
    vec = np.concatenate([
        np.concatenate([a[n].reshape(-1) for n in ("b_ada", "norm1_w", "norm2_w", "final_norm_w", "conv_b", "ssd_norm_w",
                                                    "merge_b", "conv_w", "gla_gate_b", "gla_norm_w")]).reshape(-1, P),
        ds]).T
    cst, lvm = constants()
    arrays = {
        "w": w, "x": fmajor(x), "c": fmajor(c), "vec": vec, "cst": cst, "lvm": lvm,
        "cvs": fmajor(a["state_conv"][0].reshape(NS * 3, -1)),
        "wdt": w_in[:, W_DT:W_DT + HEADS].reshape(KT, P, HEADS).transpose(1, 0, 2),
        "wgl": w_in[:, W_GLR:W_GLR + RANK].reshape(KT, P, RANK).transpose(1, 0, 2),
        "gup": a["gla_gate_up"][0],
        "dt_bias": a["dt_bias"][0], "a_log": a["a_log"][0], "router_bias": a["router_bias"],
        "wr": a["w_router"].reshape(KT, P, E).transpose(1, 0, 2),
        "sg": a["state_gla"][0].transpose(1, 2, 0, 3),
        "ss": a["state_ssm"][0].reshape(NS, PAIRS, P, NSTATE).transpose(1, 3, 0, 2),
    }
    outs = {
        "y": (T, D), "conv_new": (P, NCONV, NSEQ * 3), "ssm_p": (PAIRS, NSTATE, P), "gla_p": (GH, GDK, GDV),
        "ss_new": (PAIRS, NSTATE, NS, P), "sg_new": (GH, GDK, NS, GDV),
    }
    nc = _bacc.Bacc("TRN2", target_bir_lowering=False, num_devices=1)
    arrays = {f"in_{k}": np.ascontiguousarray(v) for k, v in arrays.items()}
    d = {k[3:]: nc.dram_tensor(k, v.shape, mybir.dt.from_np(v.dtype), kind="ExternalInput").ap() for k, v in arrays.items()}
    for k, shape in outs.items():
        d[k] = nc.dram_tensor(f"out_{k}", shape, F32, kind="ExternalOutput").ap()
    d["xd"] = nc.dram_tensor("xd", (XROWS + CAP, D), F32, kind="Internal").ap()
    d["yd"] = nc.dram_tensor("yd", (E, CAP, D), F32, kind="Internal").ap()
    d["csd"] = nc.dram_tensor("csd", (HEADS, T), F32, kind="Internal").ap()
    build(nc, d)
    r = _run(nc, [arrays], core_ids=[0]).results[0]
    o = {k: np.asarray(r[f"out_{k}"]) for k in outs}

    y = o["y"]
    cv = o["conv_new"].transpose(2, 1, 0).reshape(NSEQ, 3, NCONV * P)
    sp = o["ssm_p"].transpose(0, 2, 1).reshape(1, 1, HEADS, HD, NSTATE)
    ss = o["ss_new"].transpose(2, 0, 3, 1).reshape(1, NS, HEADS, HD, NSTATE)
    sg = o["sg_new"].transpose(2, 0, 1, 3)[None]
    outs_ = (y[None, :NP_], y[NP_:].reshape(NS, ST, D), cv[None, :1], sp, o["gla_p"][None, None], cv[None, 1:], ss, sg)
    return tuple(np.ascontiguousarray(v) for v in outs_)
```
